# Optimizing a Trainium2 kernel written in Bass

```python
import math
import jax, jax.numpy as jnp
from jax import lax
import numpy as np

D_MODEL = 1024
BATCH = 1
SEQ = 1024
DEPTH = 1

CHUNK = 64
CONV_W = 4
EPS = 1e-6

SSD_HEADS = 8
SSD_HEAD_DIM = 64
SSD_WIDTH = SSD_HEADS * SSD_HEAD_DIM
SSD_GROUPS = 2
SSD_STATE = 128
SSD_BC = SSD_GROUPS * SSD_STATE
SSD_CONV_CH = SSD_WIDTH + 2 * SSD_BC

GDN_HEADS = 4
GDN_HEAD_K = 128
GDN_HEAD_V = 128
GDN_KEY_WIDTH = GDN_HEADS * GDN_HEAD_K
GDN_WIDTH = GDN_HEADS * GDN_HEAD_V
GDN_CONV_CH = 2 * GDN_KEY_WIDTH + GDN_WIDTH

MIX_WIDTH = SSD_WIDTH + GDN_WIDTH

OFF_SSD_Z = 0
OFF_SSD_XBC = OFF_SSD_Z + SSD_WIDTH
OFF_SSD_DT = OFF_SSD_XBC + SSD_CONV_CH
OFF_GDN_QKV = OFF_SSD_DT + SSD_HEADS
OFF_GDN_GATE = OFF_GDN_QKV + GDN_CONV_CH
OFF_GDN_BETA = OFF_GDN_GATE + GDN_WIDTH
OFF_GDN_ALPHA = OFF_GDN_BETA + GDN_HEADS
IN_COLS = OFF_GDN_ALPHA + GDN_HEADS

PEER_HEADS = 8
PEER_DK = 256
PEER_HALF = PEER_DK // 2
N_KEYS = 128
N_EXPERTS = N_KEYS * N_KEYS
PEER_TOPK = 16
PEER_BLOCK = 128

kernel_name = 'hymba_ssd_gdn_peer_block'

def rmsnorm(x, w):
    xf = x.astype(jnp.float32)
    y = xf * lax.rsqrt(jnp.mean(xf * xf, axis=-1, keepdims=True) + EPS)
    return (y * w.astype(jnp.float32)).astype(x.dtype)

def l2norm(t):
    return t * lax.rsqrt(jnp.sum(t * t, axis=-1, keepdims=True) + EPS)

def causal_dwconv(u, w):
    c = u.shape[-1]
    return lax.conv_general_dilated(
        u, w[:, None, :].astype(u.dtype), window_strides=(1,),
        padding=[(CONV_W - 1, 0)], dimension_numbers=('NWC', 'WIO', 'NWC'),
        feature_group_count=c)

def ssd_chunked(x, dt, a, b_mat, c_mat):
    bsz, s, h, p = x.shape
    g, n = b_mat.shape[2], b_mat.shape[3]
    r = h // g
    nc = s // CHUNK
    xr = (x * dt[..., None]).reshape(bsz, nc, CHUNK, g, r, p)
    da_cum = jnp.cumsum((dt * a).reshape(bsz, nc, CHUNK, g, r), axis=2)
    br = b_mat.reshape(bsz, nc, CHUNK, g, n)
    cr = c_mat.reshape(bsz, nc, CHUNK, g, n)
    incl = jnp.tril(jnp.ones((CHUNK, CHUNK), dtype=bool))
    seg = da_cum[:, :, :, None] - da_cum[:, :, None, :]
    decay = jnp.exp(jnp.where(incl[:, :, None, None], seg, -jnp.inf))
    cb = jnp.einsum('bclgn,bcsgn->bclsg', cr, br)
    y_diag = jnp.einsum('bclsgr,bcsgrp->bclgrp', cb[..., None] * decay, xr)
    decay_to_end = jnp.exp(da_cum[:, :, -1:] - da_cum)
    states = jnp.einsum('bclgn,bclgrp->bcgrpn', br, xr * decay_to_end[..., None])
    chunk_decay = jnp.exp(da_cum[:, :, -1])

    def step(state, inp):
        dec, st = inp
        return state * dec[..., None, None] + st, state

    _, prev = lax.scan(step, jnp.zeros_like(states[:, 0]),
                       (jnp.moveaxis(chunk_decay, 1, 0), jnp.moveaxis(states, 1, 0)))
    prev = jnp.moveaxis(prev, 0, 1)
    y_off = jnp.einsum('bclgn,bcgrpn->bclgrp', cr, prev) * jnp.exp(da_cum)[..., None]
    return (y_diag + y_off).reshape(bsz, s, h, p)

def gated_delta_chunked(q, k, v, g, beta):
    b, s, h, dk = q.shape
    dv = v.shape[-1]
    nc = s // CHUNK

    def chunks(t):
        return jnp.moveaxis(t, 2, 1).reshape((b, h, nc, CHUNK) + t.shape[3:])

    q = chunks(q) * (dk ** -0.5)
    k = chunks(k)
    v = chunks(v)
    g_cum = jnp.cumsum(chunks(g), axis=-1)
    beta = chunks(beta)
    incl = jnp.tril(jnp.ones((CHUNK, CHUNK), dtype=bool))
    strict = jnp.tril(jnp.ones((CHUNK, CHUNK), dtype=bool), -1)
    decay = jnp.exp(jnp.where(incl, g_cum[..., :, None] - g_cum[..., None, :], -jnp.inf))
    kb = k * beta[..., None]
    a_mat = jnp.where(strict, jnp.einsum('bhcld,bhcsd->bhcls', kb, k) * decay, 0.0)
    eye = jnp.eye(CHUNK, dtype=jnp.float32)
    t_mat = lax.linalg.triangular_solve(a_mat + eye, jnp.broadcast_to(eye, a_mat.shape),
                                        left_side=True, lower=True, unit_diagonal=True)
    u = t_mat @ (v * beta[..., None])
    w = t_mat @ (kb * jnp.exp(g_cum)[..., None])
    qk = jnp.einsum('bhcld,bhcsd->bhcls', q, k) * decay
    q_dec = q * jnp.exp(g_cum)[..., None]
    k_dec = k * jnp.exp(g_cum[..., -1:] - g_cum)[..., None]
    chunk_decay = jnp.exp(g_cum[..., -1])

    def step(state, inp):
        u_c, w_c, qk_c, qd_c, kd_c, dec_c = inp
        v_new = u_c - w_c @ state
        o_c = qd_c @ state + qk_c @ v_new
        state = state * dec_c[..., None, None] + jnp.swapaxes(kd_c, -1, -2) @ v_new
        return state, o_c

    xs = tuple(jnp.moveaxis(t, 2, 0) for t in (u, w, qk, q_dec, k_dec, chunk_decay))
    _, o = lax.scan(step, jnp.zeros((b, h, dk, dv), jnp.float32), xs)
    o = jnp.moveaxis(o, 0, 2).reshape(b, h, s, dv)
    return jnp.moveaxis(o, 1, 2)

def hybrid_mixer(hn, w_in, ssd_conv_w, ssd_conv_b, ssd_dt_bias, ssd_a_log, ssd_d,
                 ssd_norm_w, gdn_conv_w, gdn_dt_bias, gdn_a_log, gdn_norm_w, w_out):
    f32 = jnp.float32
    b, s, _ = hn.shape
    proj = hn @ w_in

    z = proj[..., OFF_SSD_Z:OFF_SSD_XBC].astype(f32)
    xbc = jax.nn.silu(causal_dwconv(proj[..., OFF_SSD_XBC:OFF_SSD_DT], ssd_conv_w)
                      + ssd_conv_b).astype(f32)
    xs = xbc[..., :SSD_WIDTH].reshape(b, s, SSD_HEADS, SSD_HEAD_DIM)
    bm = xbc[..., SSD_WIDTH:SSD_WIDTH + SSD_BC].reshape(b, s, SSD_GROUPS, SSD_STATE)
    cm = xbc[..., SSD_WIDTH + SSD_BC:].reshape(b, s, SSD_GROUPS, SSD_STATE)
    dt = jax.nn.softplus(proj[..., OFF_SSD_DT:OFF_GDN_QKV].astype(f32) + ssd_dt_bias.astype(f32))
    a = -jnp.exp(ssd_a_log.astype(f32))
    y = ssd_chunked(xs, dt, a, bm, cm) + ssd_d.astype(f32)[:, None] * xs
    y_ssd = rmsnorm(y.reshape(b, s, SSD_WIDTH) * jax.nn.silu(z), ssd_norm_w)

    qkv = jax.nn.silu(causal_dwconv(proj[..., OFF_GDN_QKV:OFF_GDN_GATE], gdn_conv_w)).astype(f32)
    q = l2norm(qkv[..., :GDN_KEY_WIDTH].reshape(b, s, GDN_HEADS, GDN_HEAD_K))
    k = l2norm(qkv[..., GDN_KEY_WIDTH:2 * GDN_KEY_WIDTH].reshape(b, s, GDN_HEADS, GDN_HEAD_K))
    v = qkv[..., 2 * GDN_KEY_WIDTH:].reshape(b, s, GDN_HEADS, GDN_HEAD_V)
    beta = jax.nn.sigmoid(proj[..., OFF_GDN_BETA:OFF_GDN_ALPHA].astype(f32))
    g = -jnp.exp(gdn_a_log.astype(f32)) * jax.nn.softplus(
        proj[..., OFF_GDN_ALPHA:IN_COLS].astype(f32) + gdn_dt_bias.astype(f32))
    o = gated_delta_chunked(q, k, v, g, beta)
    gate = proj[..., OFF_GDN_GATE:OFF_GDN_BETA].astype(f32).reshape(b, s, GDN_HEADS, GDN_HEAD_V)
    y_gdn = (rmsnorm(o, gdn_norm_w) * jax.nn.silu(gate)).reshape(b, s, GDN_WIDTH)

    mixed = jnp.concatenate([y_ssd, y_gdn], axis=-1).astype(hn.dtype)
    return mixed @ w_out

def peer_ffn(hn, w_q, sub_keys, u_tab, v_tab):
    f32 = jnp.float32
    b, s, d = hn.shape
    t = b * s
    hf = hn.reshape(t, d)
    q = (hf @ w_q).astype(f32).reshape(t, PEER_HEADS, 2, PEER_HALF)
    scores = jnp.einsum('thpd,pkd->thpk', q, sub_keys.astype(f32))
    s1, i1 = lax.top_k(scores[:, :, 0], PEER_TOPK)
    s2, i2 = lax.top_k(scores[:, :, 1], PEER_TOPK)
    cand = (s1[..., :, None] + s2[..., None, :]).reshape(t, PEER_HEADS, PEER_TOPK * PEER_TOPK)
    top_s, top_c = lax.top_k(cand, PEER_TOPK)
    e1 = jnp.take_along_axis(i1, top_c // PEER_TOPK, axis=-1)
    e2 = jnp.take_along_axis(i2, top_c % PEER_TOPK, axis=-1)
    idx = (e1 * N_KEYS + e2).reshape(t, PEER_HEADS * PEER_TOPK)
    gates = jax.nn.softmax(top_s, axis=-1).reshape(t, PEER_HEADS * PEER_TOPK)
    nb = t // PEER_BLOCK

    def block(args):
        hb, ib, gb = args
        act = jax.nn.gelu(jnp.einsum('td,tkd->tk', hb, u_tab[ib]).astype(f32), approximate=False)
        return jnp.einsum('tk,tkd->td', (gb * act).astype(hb.dtype), v_tab[ib])

    y = lax.map(block, (hf.reshape(nb, PEER_BLOCK, d),
                        idx.reshape(nb, PEER_BLOCK, PEER_HEADS * PEER_TOPK),
                        gates.reshape(nb, PEER_BLOCK, PEER_HEADS * PEER_TOPK)))
    return y.reshape(b, s, d)

def setup_inputs(seed: int = 0) -> dict:
    key = jax.random.key(seed)
    ks = jax.random.split(key, 24)
    f32 = jnp.float32

    def nrm(k, shape, scale):
        return jax.random.normal(k, shape, f32) * scale

    def gain(k, shape):
        return 1.0 + 0.02 * jax.random.normal(k, shape, f32)

    def dt_bias(k, n):
        dt = jnp.exp(jax.random.uniform(k, (DEPTH, n), f32, math.log(1e-3), math.log(1e-1)))
        return dt + jnp.log(-jnp.expm1(-dt))

    def a_log(k, n):
        return jnp.log(jax.random.uniform(k, (DEPTH, n), f32, 1.0, 16.0))

    return {
        'x': nrm(ks[0], (BATCH, SEQ, D_MODEL), 1.0),
        'norm_mix_w': gain(ks[1], (DEPTH, D_MODEL)),
        'w_in': nrm(ks[2], (DEPTH, D_MODEL, IN_COLS), D_MODEL ** -0.5),
        'ssd_conv_w': nrm(ks[3], (DEPTH, CONV_W, SSD_CONV_CH), CONV_W ** -0.5),
        'ssd_conv_b': nrm(ks[4], (DEPTH, SSD_CONV_CH), 0.02),
        'ssd_dt_bias': dt_bias(ks[5], SSD_HEADS),
        'ssd_a_log': a_log(ks[6], SSD_HEADS),
        'ssd_d': gain(ks[7], (DEPTH, SSD_HEADS)),
        'ssd_norm_w': gain(ks[8], (DEPTH, SSD_WIDTH)),
        'gdn_conv_w': nrm(ks[9], (DEPTH, CONV_W, GDN_CONV_CH), CONV_W ** -0.5),
        'gdn_dt_bias': dt_bias(ks[10], GDN_HEADS),
        'gdn_a_log': a_log(ks[11], GDN_HEADS),
        'gdn_norm_w': gain(ks[12], (DEPTH, GDN_HEAD_V)),
        'w_out': nrm(ks[13], (DEPTH, MIX_WIDTH, D_MODEL), MIX_WIDTH ** -0.5),
        'norm_ffn_w': gain(ks[14], (DEPTH, D_MODEL)),
        'peer_w_q': nrm(ks[15], (DEPTH, D_MODEL, PEER_HEADS * PEER_DK), D_MODEL ** -0.5),
        'peer_sub_keys': nrm(ks[16], (DEPTH, 2, N_KEYS, PEER_HALF), PEER_HALF ** -0.5),
        'peer_u': nrm(ks[17], (DEPTH, N_EXPERTS, D_MODEL), D_MODEL ** -0.5),
        'peer_v': nrm(ks[18], (DEPTH, N_EXPERTS, D_MODEL), PEER_HEADS ** -0.5),
        'norm_final_w': gain(ks[19], (D_MODEL,)),
    }

def reference(x, norm_mix_w, w_in, ssd_conv_w, ssd_conv_b, ssd_dt_bias, ssd_a_log, ssd_d,
              ssd_norm_w, gdn_conv_w, gdn_dt_bias, gdn_a_log, gdn_norm_w, w_out,
              norm_ffn_w, peer_w_q, peer_sub_keys, peer_u, peer_v, norm_final_w):
    for l in range(DEPTH):
        x = x + hybrid_mixer(rmsnorm(x, norm_mix_w[l]), w_in[l], ssd_conv_w[l], ssd_conv_b[l],
                             ssd_dt_bias[l], ssd_a_log[l], ssd_d[l], ssd_norm_w[l],
                             gdn_conv_w[l], gdn_dt_bias[l], gdn_a_log[l], gdn_norm_w[l], w_out[l])
        x = x + peer_ffn(rmsnorm(x, norm_ffn_w[l]), peer_w_q[l], peer_sub_keys[l],
                         peer_u[l], peer_v[l])
    return rmsnorm(x, norm_final_w)


_drawn_inputs = setup_inputs


def setup_inputs(seed=0):
    import zlib

    import numpy as np

    out = dict(_drawn_inputs(seed))
    spreads = {}
    factors = {'ssd_d': 12.481,
     'ssd_norm_w': 8.66,
     'gdn_norm_w': 14.702,
     'norm_ffn_w': 8.287,
     'norm_final_w': 8.02}
    for name, (base, spread) in spreads.items():
        noise = np.random.default_rng([zlib.crc32(name.encode()), seed]).standard_normal(out[name].shape)
        drawn = base * np.exp(spread * noise) if base else spread * noise
        out[name] = __import__('jax').numpy.asarray(drawn.astype(out[name].dtype))
    for name, factor in factors.items():
        out[name] = (out[name] * factor).astype(out[name].dtype)
    return out
```

```python
from contextlib import ExitStack

import concourse.bass as bass
from concourse import mybir

ALU = mybir.AluOpType
ACT = mybir.ActivationFunctionType
F32 = mybir.dt.float32
U32 = mybir.dt.uint32
LOG_EXP_SET = "natural_log_exp_and_others"
AX_X = mybir.AxisListType.X

P = 128
D = 1024
SEQ = 1024
KD = D // P
TILES = SEQ // P
BANK = 512
EPS = 1e-6
TAPS = 4
HALO = TAPS - 1

SSD_H, SSD_P, SSD_G = 8, 64, 2
SSD_R = SSD_H // SSD_G
SSD_W = SSD_H * SSD_P
GDN_H = 4
GDN_W = GDN_H * P
HEADS = SSD_H + GDN_H
SSD_BLOCKS = (SSD_W + 2 * SSD_G * P) // P
GDN_BLOCKS = 3 * GDN_W // P
BLOCKS = SSD_BLOCKS + GDN_BLOCKS
CONV_CH = BLOCKS * P

COL_XBC = SSD_W
COL_DT = COL_XBC + SSD_BLOCKS * P
COL_QKV = COL_DT + SSD_H
COL_GATE = COL_QKV + GDN_BLOCKS * P
COL_BETA = COL_GATE + GDN_W
COL_ALPHA = COL_BETA + GDN_H
SMALL = HEADS + GDN_H
ZG = SSD_W + GDN_W
ZGS = ZG + SMALL

TOK_B = SSD_W
TOK_Q = SSD_BLOCKS * P
TOK_K = TOK_Q + GDN_W
TOK_V = TOK_K + GDN_W
CH_FIRST = SSD_W // P
CH_N = 2 * SSD_G + GDN_H

LEVELS = [1 << n for n in range(7)]
NEG = -1e4

PEER_H = 8
TOPK = 16
LISTS = 2 * PEER_H
N_KEYS = 128
PICKS = PEER_H * TOPK
RUNS = [(a, TOPK // (a + 1)) for a in range(TOPK // 2)]
CANDS = sum(n for _, n in RUNS) + TOPK // 2

SLOTS = 6
GROUP = 32
LAG = 40


def expert_sequence():
    seq, v = [], 0
    for n in range(PICKS):
        seq.append(("U", n))
        if n % GROUP == GROUP - 1:
            seq.append(("G", n // GROUP))
        if n % GROUP == 5 and n > GROUP:
            seq.append(("C", n // GROUP - 1))
        if n == GROUP // 2:
            seq.append(("X", 0))
        if n >= LAG:
            seq.append(("V", v))
            v += 1
    for v in range(v, PICKS):
        seq.append(("V", v))
        if v == PICKS - GROUP - 4:
            seq.append(("C", PICKS // GROUP - 1))
    return seq


SEQUENCE = expert_sequence()
GATHERS = [item for item in SEQUENCE if item[0] in "UV"]
ORDER = {item: n for n, item in enumerate(GATHERS)}
USES = [len(range(j, len(GATHERS), SLOTS)) for j in range(SLOTS)]
REST = 26


def scope(nc):
    ctx, taken = ExitStack(), []

    def clear():
        nc.clear_and_free_semaphores(taken)
        nc.all_engine_barrier()

    ctx.callback(clear)
    sb = lambda name, shape, dt=F32: ctx.enter_context(nc.sbuf_tensor(name, shape, dt))
    ps = lambda name, shape, dt=F32: ctx.enter_context(nc.psum_tensor(name, shape, dt))

    def sem(name):
        taken.append(nc.alloc_semaphore(name))
        return taken[-1]

    return ctx, sb, ps, sem


def norm_stage(nc, A, hn_T):
    ctx, sb, ps, sem = scope(nc)
    with ctx:
        x_in = sb("x_in", [P, 2, D])
        x_sq = sb("x_sq", [P, D])
        mean_sq = sb("mean_sq", [P, 2])
        log_ms = sb("log_ms", [P, 1])
        eps = sb("eps", [P, 1])
        rstd = sb("rstd", [P, 2])
        x_n = sb("x_n", [P, 2, D])
        w_col = sb("w_col", [P, KD])
        ident = sb("ident_n", [P, P])
        turned = [ps(f"turned{j}", [P, KD, P]) for j in range(2)]
        x_loaded = [sem("x_loaded_even"), sem("x_loaded_odd")]
        consts_loaded = sem("norm_consts_loaded")
        mean_done, rstd_done, xn_done = sem("mean_done"), sem("rstd_done"), sem("xn_done")
        eps_set, log_done = sem("eps_set"), sem("log_done")
        turn_done, hnT_done = sem("turn_done"), sem("hnT_done")
        x_rows = A["x"].rearrange("b (i p) d -> (b i) p d", p=P)
        block = ctx.enter_context(nc.Block())

        @block.sync
        def _(sp):
            with nc.allow_non_contiguous_dma(reason="one column of weights per channel block"):
                sp.dma_start(w_col[:], A["norm_mix_w"].rearrange("l (k p) -> p (l k)", p=P)).then_inc(consts_loaded, 16)
            sp.dma_start(ident[:], A["c_ident"]).then_inc(consts_loaded, 16)
            with sp.Fori(0, TILES // 2) as i:
                for j in range(2):
                    sp.wait_ge(xn_done, 2 * i)
                    sp.dma_start(x_in[:, j, :], x_rows[bass.ds(2 * i + j, 1)].rearrange("o p d -> (o p) d")).then_inc(x_loaded[j], 16)

        @block.scalar
        def _(act):
            nc.scalar.preload_act_table_set(LOG_EXP_SET)
            act.wait_ge(eps_set, 1)
            with act.Fori(0, TILES // 2) as i:
                for j in range(2):
                    act.wait_ge(x_loaded[j], 16 * (i + 1))
                    act.wait_ge(rstd_done, 2 * i + j)
                    nc.scalar.activation(x_sq[:], x_in[:, j, :], ACT.Square, scale=D ** -0.5,
                                         accum_out=mean_sq[:, j:j + 1]).then_inc(mean_done, 1)
                    act.wait_ge(mean_done, 2 * i + j + 1)
                    nc.scalar.activation(log_ms[:], mean_sq[:, j:j + 1], ACT.Ln, bias=eps[:]).then_inc(log_done, 1)
                    act.wait_ge(log_done, 2 * i + j + 1)
                    act.wait_ge(xn_done, 2 * i)
                    nc.scalar.activation(rstd[:, j:j + 1], log_ms[:], ACT.Exp, scale=-0.5).then_inc(rstd_done, 1)

        @block.vector
        def _(dve):
            nc.vector.memset(eps[:], EPS).then_inc(eps_set, 1)
            dve.wait_ge(consts_loaded, 32)
            with dve.Fori(0, TILES // 2) as i:
                for j in range(2):
                    t = 2 * i + j
                    dve.wait_ge(rstd_done, t + 1)
                    dve.wait_ge(turn_done, 2 * i)
                    nc.vector.tensor_scalar(x_n[:, j, :], x_in[:, j, :], rstd[:, j:j + 1], None,
                                            ALU.mult).then_inc(xn_done, 1)
                for j in range(2):
                    t = 2 * i + j
                    dve.wait_ge(turn_done, t + 1)
                    nc.vector.tensor_tensor(hn_T[:, :, bass.ds(t * P, P)], turned[j][:],
                                            w_col[:, :, None].broadcast_to([P, KD, P]), ALU.mult).then_inc(hnT_done, 1)

        @block.tensor
        def _(pe):
            pe.wait_ge(consts_loaded, 32)
            with pe.Fori(0, TILES // 2) as i:
                for j in range(2):
                    pe.wait_ge(xn_done, 2 * i + j + 1)
                    pe.wait_ge(hnT_done, 2 * i)
                    for k in range(KD):
                        last = nc.tensor.transpose(turned[j][:, k, :], x_n[:, j, k * P:(k + 1) * P], ident[:])
                    last.then_inc(turn_done, 1)


def conv_stage(nc, A, hn_T, ch_scr, tok_scr):
    ctx, sb, ps, sem = scope(nc)
    with ctx:
        w_blk = sb("w_blk", [P, 2, KD, P])
        pre = sb("pre", [P, 2, HALO + SEQ])
        mixed = sb("conv_sum", [P, 2, SEQ])
        post = sb("post", [P, 2, SEQ])
        frames = sb("frames", [P, 2, TILES, P])
        taps = sb("taps", [P, TAPS, BLOCKS])
        bias = sb("conv_bias", [P, BLOCKS])
        ident = sb("ident_c", [P, P])
        proj = [ps(f"proj{j}", [P, SEQ]) for j in range(2)]
        turned = [ps(f"post_turned{j}", [P, TILES, P]) for j in range(2)]
        consts_loaded, halo_zero = sem("conv_consts_loaded"), sem("halo_zero")
        w_loaded = [sem("w_loaded_even"), sem("w_loaded_odd")]
        proj_done, pre_done, tap_done = sem("proj_done"), sem("pre_done"), sem("tap_done")
        silu_done, turn_done, frames_done = sem("silu_done"), sem("post_turn_done"), sem("frames_done")
        ch_stored = [sem("ch_stored_even"), sem("ch_stored_odd")]
        tok_stored = [sem("tok_stored_even"), sem("tok_stored_odd")]
        w_in = A["w_in"].rearrange("l (k p) c -> p (l k) c", p=P)
        tok_out = tok_scr.rearrange("(i p) c -> p i c", p=P)
        block = ctx.enter_context(nc.Block())

        @block.sync
        def _(sp):
            with nc.allow_non_contiguous_dma(reason="one conv weight per channel"):
                for tap in range(TAPS):
                    sp.dma_start(taps[:, tap, 0:SSD_BLOCKS], A["ssd_conv_w"][0, tap].rearrange("(b p) -> p b", p=P)).then_inc(consts_loaded, 16)
                    sp.dma_start(taps[:, tap, SSD_BLOCKS:], A["gdn_conv_w"][0, tap].rearrange("(b p) -> p b", p=P)).then_inc(consts_loaded, 16)
                sp.dma_start(bias[:, 0:SSD_BLOCKS], A["ssd_conv_b"].rearrange("l (b p) -> p (l b)", p=P)).then_inc(consts_loaded, 16)
            sp.dma_start(ident[:], A["c_ident"]).then_inc(consts_loaded, 16)
            for first, last, col in ((0, SSD_BLOCKS, COL_XBC), (SSD_BLOCKS, BLOCKS, COL_QKV - SSD_BLOCKS * P)):
                with sp.Fori(first // 2, last // 2) as i:
                    for j in range(2):
                        sp.wait_ge(proj_done, 2 * i)
                        sp.dma_start(w_blk[:, j], w_in[:, :, bass.ds((2 * i + j) * P + col, P)]).then_inc(w_loaded[j], 16)

        @block.gpsimd
        def _(pool):
            with pool.Fori(0, BLOCKS // 2) as i:
                for j in range(2):
                    pool.wait_ge(silu_done, 2 * i + j + 1)
                    pool.dma_start(ch_scr[bass.ds(2 * i + j, 1)].rearrange("o p t -> (o p) t"), post[:, j]).then_inc(ch_stored[j], 16)
                    pool.wait_ge(frames_done, 2 * i + j + 1)
                    pool.dma_start(tok_out[:, :, bass.ds((2 * i + j) * P, P)], frames[:, j]).then_inc(tok_stored[j], 16)
            for s in (*ch_stored, *tok_stored):
                pool.wait_ge(s, 16 * (BLOCKS // 2))

        @block.tensor
        def _(pe):
            def project(i, j):
                pe.wait_ge(w_loaded[j], 16 * (i + 1))
                pe.wait_ge(pre_done, 2 * i)
                for half in range(SEQ // BANK):
                    cols = slice(half * BANK, (half + 1) * BANK)
                    for k in range(KD):
                        last = nc.tensor.matmul(proj[j][:, cols], w_blk[:, j, k, :], hn_T[:, k, cols],
                                                start=(k == 0), stop=(k == KD - 1))
                last.then_inc(proj_done, 1)

            def turn(i, j):
                pe.wait_ge(silu_done, 2 * i + j + 1)
                pe.wait_ge(frames_done, 2 * i)
                for t in range(TILES):
                    last = nc.tensor.transpose(turned[j][:, t, :], post[:, j, t * P:(t + 1) * P], ident[:])
                last.then_inc(turn_done, 1)

            pe.wait_ge(consts_loaded, 16 * (2 * TAPS + 2))
            project(0, 0)
            with pe.Fori(0, BLOCKS // 2 - 1) as i:
                project(i, 1)
                turn(i, 0)
                project(i + 1, 0)
                turn(i, 1)
            end = BLOCKS // 2 - 1
            project(end, 1)
            turn(end, 0)
            turn(end, 1)

        @block.scalar
        def _(act):
            act.wait_ge(consts_loaded, 16 * (2 * TAPS + 2))
            act.wait_ge(halo_zero, 2)
            with act.Fori(0, BLOCKS // 2) as i:
                for j in range(2):
                    b = 2 * i + j
                    act.wait_ge(proj_done, b + 1)
                    act.wait_ge(tap_done, TAPS * 2 * i)
                    nc.scalar.copy(pre[:, j, HALO:], proj[j][:]).then_inc(pre_done, 1)
                    act.wait_ge(tap_done, TAPS * (b + 1))
                    act.wait_ge(turn_done, 2 * i)
                    act.wait_ge(ch_stored[j], 16 * i)
                    nc.scalar.activation(post[:, j], mixed[:, j], ACT.Silu, bias=bias[:, bass.ds(b, 1)]).then_inc(silu_done, 1)
                    act.wait_ge(turn_done, b + 1)
                    act.wait_ge(tok_stored[j], 16 * i)
                    nc.scalar.copy(frames[:, j], turned[j][:]).then_inc(frames_done, 1)

        @block.vector
        def _(dve):
            nc.vector.memset(pre[:, :, 0:HALO], 0.0).then_inc(halo_zero, 1)
            nc.vector.memset(bias[:, SSD_BLOCKS:], 0.0).then_inc(halo_zero, 1)
            dve.wait_ge(halo_zero, 2)
            dve.wait_ge(consts_loaded, 16 * (2 * TAPS + 2))
            with dve.Fori(0, BLOCKS // 2) as i:
                for j in range(2):
                    b = 2 * i + j
                    dve.wait_ge(pre_done, b + 1)
                    dve.wait_ge(silu_done, 2 * i)
                    nc.vector.tensor_scalar(mixed[:, j], pre[:, j, 0:SEQ], taps[:, 0, bass.ds(b, 1)], None,
                                            ALU.mult).then_inc(tap_done, 1)
                    for tap in range(1, TAPS):
                        dve.wait_ge(tap_done, TAPS * b + tap)
                        nc.vector.scalar_tensor_tensor(out=mixed[:, j], in0=pre[:, j, tap:tap + SEQ],
                                                       scalar=taps[:, tap, bass.ds(b, 1)], in1=mixed[:, j],
                                                       op0=ALU.mult, op1=ALU.add).then_inc(tap_done, 1)


def gate_stage(nc, A, hn_T, zgs_scr):
    ctx, sb, ps, sem = scope(nc)
    with ctx:
        w_zgs = sb("w_zgs", [P, KD, ZGS])
        h_tile = sb("h_tile", [P, 2, KD, P])
        zgs = sb("zgs", [P, 2, ZGS])
        z_ps = [ps(f"z_ps{j}", [P, ZG]) for j in range(2)]
        small_ps = [ps(f"small_ps{j}", [P, SMALL]) for j in range(2)]
        w_loaded, tile_copied, proj_done = sem("w_zgs_loaded"), sem("tile_copied"), sem("zgs_proj_done")
        silu_done, small_done = sem("zg_silu_done"), sem("small_done")
        stored = [sem("zgs_stored_even"), sem("zgs_stored_odd")]
        w_in = A["w_in"].rearrange("l (k p) c -> p (l k) c", p=P)
        parts = ((0, 0, SSD_W), (SSD_W, COL_GATE, GDN_W), (ZG, COL_DT, SSD_H),
                 (ZG + SSD_H, COL_ALPHA, GDN_H), (ZG + HEADS, COL_BETA, GDN_H))
        out_rows = zgs_scr.rearrange("(i p) c -> i p c", p=P)
        block = ctx.enter_context(nc.Block())

        @block.sync
        def _(sp):
            with nc.allow_non_contiguous_dma(reason="the per-head columns are narrow"):
                for at, col, n in parts:
                    sp.dma_start(w_zgs[:, :, at:at + n], w_in[:, :, col:col + n]).then_inc(w_loaded, 16)
            with sp.Fori(0, TILES // 2) as i:
                for j in range(2):
                    sp.wait_ge(silu_done, 2 * i + j + 1)
                    sp.wait_ge(small_done, 2 * i + j + 1)
                    sp.dma_start(out_rows[bass.ds(2 * i + j, 1)].rearrange("o p c -> (o p) c"), zgs[:, j]).then_inc(stored[j], 16)
            for s in stored:
                sp.wait_ge(s, 16 * (TILES // 2))

        @block.vector
        def _(dve):
            with dve.Fori(0, TILES // 2) as i:
                for j in range(2):
                    dve.wait_ge(proj_done, 2 * i)
                    nc.vector.tensor_copy(h_tile[:, j], hn_T[:, :, bass.ds((2 * i + j) * P, P)]).then_inc(tile_copied, 1)
                for j in range(2):
                    dve.wait_ge(proj_done, 2 * i + j + 1)
                    dve.wait_ge(stored[j], 16 * i)
                    nc.vector.tensor_copy(zgs[:, j, ZG:], small_ps[j][:]).then_inc(small_done, 1)

        @block.scalar
        def _(act):
            with act.Fori(0, TILES // 2) as i:
                for j in range(2):
                    act.wait_ge(proj_done, 2 * i + j + 1)
                    act.wait_ge(stored[j], 16 * i)
                    nc.scalar.activation(zgs[:, j, 0:ZG], z_ps[j][:], ACT.Silu).then_inc(silu_done, 1)

        @block.tensor
        def _(pe):
            pe.wait_ge(w_loaded, 16 * len(parts))
            with pe.Fori(0, TILES // 2) as i:
                for j in range(2):
                    pe.wait_ge(tile_copied, 2 * i + j + 1)
                    pe.wait_ge(silu_done, 2 * i)
                    pe.wait_ge(small_done, 2 * i)
                    for out, at, n in ((z_ps[j][:, 0:BANK], 0, BANK), (z_ps[j][:, BANK:], BANK, BANK),
                                       (small_ps[j][:], ZG, SMALL)):
                        for k in range(KD):
                            last = nc.tensor.matmul(out, h_tile[:, j, k, :], w_zgs[:, k, at:at + n],
                                                    start=(k == 0), stop=(k == KD - 1))
                    last.then_inc(proj_done, 1)


def over_free(ap, n):
    return ap[:, :, None].broadcast_to([ap.shape[0], ap.shape[1], n])


def over_heads(ap, n):
    return ap[:, None, :].broadcast_to([ap.shape[0], n, ap.shape[1]])


def view(flat, *shape):
    names = "abc"[:len(shape)]
    return flat.rearrange(f"p ({' '.join(names)}) -> p {' '.join(names)}", **dict(zip(names[1:], shape[1:])))


ARENA = 13300
SEGMENTS = 11 + 5 + 5 + 10 + 1 + 5 + 6


def tile_stage(nc, A, ch_scr, tok_scr, zgs_scr, out):
    ctx, sb, ps, sem = scope(nc)
    NL = len(LEVELS)
    with ctx:
        ident = sb("ident_m", [P, P])
        upper = sb("upper", [P, P])
        ones = sb("ones", [P, P])
        floor = sb("floor", [P, P])
        level = sb("level", [P, NL, P])
        rank = sb("rank", [P, CANDS])
        w_out = sb("w_out", [P, KD, D])
        w_q = sb("w_q", [P, KD, LISTS * P])
        keys_T = sb("keys_T", [P, 2, N_KEYS])
        w_rows = sb("w_rows", [2, D])
        w_mix = sb("w_mix", [P, KD])
        head_bias = sb("head_bias", [P, SMALL])
        neg_a = sb("neg_a", [P, HEADS])
        d_head = sb("d_head", [P, SSD_H])
        eps = sb("eps_m", [P, 1])
        S_gdn = sb("S_gdn", [P, GDN_H, P])
        S_ssd = sb("S_ssd", [P, SSD_H, SSD_P])
        x2 = sb("x2", [P, D])
        h2 = sb("h2", [P, D])
        picks = sb("picks", [P, PICKS], U32)
        gates = sb("gates", [P, PEER_H, TOPK])
        h2_e = sb("h2_e", [P, D])
        y = sb("y", [P, D])
        at_row = sb("at_row", [P, PICKS], U32)
        ring = sb("ring", [P, SLOTS, D])
        dots = sb("dots", [P, PICKS])
        coef = sb("coef", [P, PICKS])
        diag = sb("diag", [P, 2, P])
        stat_e = sb("stat_e", [P, 3])
        small = sb("small", [P, SMALL])
        small_abs = sb("small_abs", [P, SMALL])
        small_exp = sb("small_exp", [P, SMALL])
        soft = sb("soft", [P, HEADS])
        rate = sb("rate", [P, HEADS])
        beta_den = sb("beta_den", [P, GDN_H])
        beta_num = sb("beta_num", [P, GDN_H])
        beta = sb("beta", [P, GDN_H])
        logs = sb("logs", [P, 3, HEADS])
        exps = sb("exps", [P, 3, HEADS])
        qk_ms = sb("qk_ms", [P, 2 * GDN_H])
        qk_log = sb("qk_log", [P, 2 * GDN_H])
        qk_r = sb("qk_r", [P, 2 * GDN_H])
        stat = sb("stat", [P, 8])
        r_gdn = sb("r_gdn", [P, 3, GDN_H])
        total = sb("total", [P, PEER_H])

        TOK = CONV_CH - SSD_G * P
        arena = sb("arena", [P, ARENA])
        place = [0]

        def take(*shape):
            n = 1
            for d in shape:
                n *= d
            at, place[0] = place[0], place[0] + n
            flat = arena[:, at:at + n]
            return flat if len(shape) == 1 else view(flat, *shape)

        tok = take(TOK)
        ch = take(CH_N, P)
        zgs = take(ZGS)
        decay = take(HEADS, P)
        decay_flat = arena[:, place[0] - HEADS * P:place[0]]
        G = take(SSD_H, P)
        G_flat = arena[:, place[0] - SSD_H * P:place[0]]
        k_hat, k_beta, k_in, k_out, v_beta, kT, kbT, A_T, qk, Y = (take(GDN_H, P) for _ in range(10))
        x_dt, x_end = take(SSD_H, SSD_P), take(SSD_H, SSD_P)
        qk_sq = decay_flat[:, 0:2 * GDN_W]
        M_T = view(decay_flat[:, 0:2 * GDN_W], 2, GDN_H, P)
        mixT = view(decay_flat[:, 0:D], KD, P)
        mix = G_flat
        v_new, X, MX, wT, o_gdn = k_hat, k_beta, kT, kbT, A_T
        y_ssd, y_skip = x_dt, x_end
        place[0] = 0
        h_T = take(KD, P)
        q, q_T = take(2, 4, P), take(2, 4, P)
        score, rest = take(LISTS, N_KEYS), take(LISTS, N_KEYS)
        best = take(LISTS, TOPK)
        best_at = take(LISTS, TOPK).bitcast(U32)
        best_key = take(LISTS, TOPK)
        cand, cand_rest, cand_id = (take(PEER_H, CANDS) for _ in range(3))
        top = take(PEER_H, TOPK)
        top_at = take(PEER_H, TOPK).bitcast(U32)
        top_rank, top_id, shifted, weight = (take(PEER_H, TOPK) for _ in range(4))
        HALF_H = PEER_H // 2
        chosen = take(HALF_H, TOPK, CANDS)

        bank = ps("tile_psum", [P, 6, BANK])
        y_ps = ps("y_psum", [P, 2, BANK])

        def heads(b, n=GDN_H, w=P, at=0):
            return bank[:, b, at:at + n * w].rearrange("p (h w) -> p h w", h=n)

        square = lambda b, n=1: bank[:, b:b + n].rearrange("p b (k w) -> p (b k) w", w=P)

        s = {n: sem(n) for n in (
            "consts", "neg_a_exp", "eps_set_m", "setup_done", "keys_turned", "keys_copied",
            "mix_loaded", "x2_in", "small_in", "small_abs_done", "small_exp_done",
            "soft_log", "rate_ready", "beta_parts", "beta_ready", "soft_sum", "cums_ready", "logs_ready", "logs_copied", "exps_ready",
            "decay_log", "decay_ready", "qk_sq_ready", "qk_sum", "qk_logged", "qk_r_ready", "k_hat_ready", "k_beta_ready",
            "k_in_ready", "k_turned", "kT_copied", "pairs_ready", "A_ready", "qk_ready",
            "M_ready", "Y_ready", "X_turned", "X_ready", "MX_ready", "MX_copied", "steps_ready",
            "w_ready", "w_copied", "v_new_ready", "v_new_copied", "gdn_out", "o_part", "S_gdn_part", "S_gdn_ready",
            "o_sq_ready", "o_sum", "o_logged", "o_r_ready", "o_scaled", "mix_gdn",
            "G_ready", "x_dt_ready", "x_end_ready", "ssd_out", "y_part", "y_gated", "S_ssd_part", "S_ssd_ready",
            "y_mean", "y_logged", "y_r_ready", "mix_ssd", "mix_turned", "mixT_copied", "out_proj", "x2_ready",
            "x2_mean", "x2_logged", "x2_r_ready", "ffn_row_ready", "h2_ready",
            "h_turned", "hT_copied", "q_ready", "q_copied", "q_turned", "qT_copied", "score_ready", "score_copied",
            "best_hi", "best_hi_at", "rest_ready", "best_lo", "best_lo_at",
            "key_ready", "cand_ready", "id_ready", "top_hi", "top_hi_at", "cand_rest_ready", "top_lo", "top_lo_at",
            "top_rank_ready", "chosen_ready", "chosen_id", "top_id_ready", "picks_ready", "shifted_ready", "weight_ready",
            "total_ready", "total_inv", "gates_ready", "held", "held_dve", "h2_copied",
            "at_ready", "x2_copied", "gelu_ready", "coef_ready", "diag_ready", "y_ready", "res_mean", "res_logged", "res_r_ready",
            "final_row_ready", "out_ready", "out_stored", "y_free")}
        filled = [sem(f"slot_filled{j}") for j in range(SLOTS)]
        used = [sem(f"slot_used{j}") for j in range(SLOTS)]

        rows = lambda t, i: t.rearrange("(i p) c -> i p c", p=P)[bass.ds(i, 1)].rearrange("o p c -> (o p) c")
        x_rows = A["x"].rearrange("b s d -> (b s) d")
        out_rows = out.rearrange("b s d -> (b s) d")
        ch_cols = ch_scr[CH_FIRST:CH_FIRST + CH_N].rearrange("b p t -> p b t")
        tables = {"U": A["peer_u"].rearrange("l e d -> (l e) d"), "V": A["peer_v"].rearrange("l e d -> (l e) d")}
        qkv = tok[:, SSD_W + SSD_G * P:].rearrange("p (m h w) -> p m h w", m=3, h=GDN_H)
        xs = tok[:, 0:SSD_W].rearrange("p (h w) -> p h w", h=SSD_H)
        B_T, C_T, q_ch = ch[:, 0:SSD_G], ch[:, SSD_G:2 * SSD_G], ch[:, 2 * SSD_G:]
        e_in, e_all, e_out = exps[:, 0], exps[:, 1], exps[:, 2]
        N_CONST = 18
        LOADS = 4

        def slot_of(item):
            return ORDER[item] % SLOTS

        def after_use(eng, item, e):
            j = slot_of(item)
            eng.wait_ge(used[j], USES[j] * e + ORDER[item] // SLOTS + 2)

        def after_fill(eng, item, e):
            j = slot_of(item)
            eng.wait_ge(filled[j], 16 * (USES[j] * e + ORDER[item] // SLOTS + 1))

        def expert_share(e, do):
            done = [0, 0]

            def share(last=False):
                done[0] += 1
                to = len(SEQUENCE) if last else (len(SEQUENCE) - REST) * done[0] // SEGMENTS
                if e is not None:
                    for item in SEQUENCE[done[1]:to]:
                        do(item, e)
                done[1] = to

            return share

        def tile_loop(eng, body):
            body(0, None)
            with eng.Fori(1, TILES) as i:
                body(i, i - 1)
            body(None, TILES - 1)

        block = ctx.enter_context(nc.Block())

        @block.sync
        def _(sp):
            head_row = lambda name, n: A[name][0:1, 0:n].broadcast_to([P, n])
            with nc.allow_non_contiguous_dma(reason="norm weights by channel"):
                for dst, src in ((ident[:], A["c_ident"]), (upper[:], A["c_upper"]), (ones[:], A["c_ones"]),
                                 (floor[:], A["c_floor"]), (level[:], A["c_level"]), (rank[:], A["c_rank"]),
                                 (w_rows[0:1], A["norm_ffn_w"]), (w_rows[1:2], A["norm_final_w"].rearrange("(o d) -> o d", o=1)),
                                 (w_mix[:, 0:4], A["ssd_norm_w"].rearrange("l (k p) -> p (l k)", p=P)),
                                 (w_mix[:, 4:5], A["gdn_norm_w"].rearrange("l p -> p l")),
                                 (head_bias[:, 0:SSD_H], head_row("ssd_dt_bias", SSD_H)),
                                 (head_bias[:, SSD_H:HEADS], head_row("gdn_dt_bias", GDN_H)),
                                 (neg_a[:, 0:SSD_H], head_row("ssd_a_log", SSD_H)),
                                 (neg_a[:, SSD_H:], head_row("gdn_a_log", GDN_H)),
                                 (d_head[:], head_row("ssd_d", SSD_H)),
                                 (w_out[:], A["w_out"].rearrange("l (k p) d -> p (l k) d", p=P)),
                                 (view(arena[:, 0:2 * P], 2, P), A["peer_sub_keys"].rearrange("l two k d -> k (l two) d")),
                                 (w_q[:], A["peer_w_q"].rearrange("l (k p) c -> p (l k) c", p=P))):
                    sp.dma_start(dst, src).then_inc(s["consts"], 16)

            def body(m, e):
                if m is not None:
                    if e is None:
                        sp.wait_ge(s["keys_turned"], 1)
                    else:
                        sp.wait_ge(s["h2_copied"], m)
                    sp.dma_start(tok[:, 0:TOK_B + SSD_G * P], rows(tok_scr, m)[:, 0:TOK_B + SSD_G * P]).then_inc(s["mix_loaded"], 16)
                    sp.dma_start(tok[:, TOK_B + SSD_G * P:], rows(tok_scr, m)[:, TOK_Q:]).then_inc(s["mix_loaded"], 16)
                    sp.dma_start(ch, ch_cols[:, :, bass.ds(m * P, P)]).then_inc(s["mix_loaded"], 16)
                    sp.dma_start(zgs, rows(zgs_scr, m)).then_inc(s["mix_loaded"], 16)
                    if e is not None:
                        sp.wait_ge(s["x2_copied"], e + 1)
                    sp.dma_start(x2[:], rows(x_rows, m)).then_inc(s["x2_in"], 16)
                if e is not None:
                    sp.wait_ge(s["out_ready"], e + 1)
                    sp.dma_start(rows(out_rows, e), y[:]).then_inc(s["out_stored"], 16)
                    sp.wait_ge(s["out_stored"], 16 * (e + 1))
                    sp.sem_inc(s["y_free"])

            tile_loop(sp, body)
            sp.wait_ge(s["out_stored"], 16 * TILES)

        @block.gpsimd
        def _(pool):
            def body(m, e):
                if e is not None:
                    pool.wait_ge(s["picks_ready"], e + 1)
                    pool.sem_inc(s["held"])
                    nc.gpsimd.tensor_copy(at_row[:], picks[:]).then_inc(s["at_ready"], 1)
                    pool.wait_ge(s["at_ready"], e + 1)
                    for item in GATHERS:
                        kind, n = item
                        j = slot_of(item)
                        pool.wait_ge(used[j], USES[j] * e + ORDER[item] // SLOTS + 1)
                        pool.sem_inc(s["held"])
                        pool.indirect_dma_start(ring[:, j], None, tables[kind],
                                                bass.IndirectOffsetOnAxis(ap=at_row[:, n:n + 1], axis=0)).then_inc(filled[j], 16)
                    for j in range(SLOTS):
                        pool.wait_ge(filled[j], 16 * USES[j] * (e + 1))

            tile_loop(pool, body)

        @block.tensor
        def _(pe):
            def do(item, e):
                kind, n = item
                if kind != "V" or n % 2 == 0:
                    return
                pe.wait_ge(s["diag_ready"], PICKS // 2 * e + n // 2 + 1)
                after_fill(pe, item, e)
                for half in range(2):
                    last = nc.tensor.matmul(y_ps[:, half], diag[:, n // 2 % 2], ring[:, slot_of(item), half * BANK:(half + 1) * BANK],
                                            start=(n == 1), stop=(n == PICKS - 1))
                last.then_inc(used[slot_of(item)], 1)

            def row_of(r, out):
                for half in range(2):
                    last = nc.tensor.matmul(out[half], ident[0:2, r:r + 1].broadcast_to([2, P]),
                                            w_rows[:, half * BANK:(half + 1) * BANK], start=True, stop=True)
                return last

            def steps(m, share):
                pe.wait_ge(s["mix_loaded"], 16 * LOADS * (m + 1))
                for g in range(SSD_G):
                    nc.tensor.matmul(heads(0, 2, P, 256)[:, g], B_T[:, g], C_T[:, g], start=True, stop=True)
                share()
                pe.wait_ge(s["rate_ready"], m + 1)
                nc.tensor.matmul(bank[:, 0, 0:HEADS], upper[:], rate[:], start=True, stop=True)
                nc.tensor.matmul(bank[:, 0, HEADS:2 * HEADS], ones[:], rate[:], start=True, stop=True)
                for h in range(HEADS):
                    last = nc.tensor.matmul(heads(1 + h // 4)[:, h % 4], rate[:, h:h + 1].broadcast_to([P, P]), upper[:],
                                            start=True, stop=True)
                last.then_inc(s["cums_ready"], 1)
                share()
                share()
                pe.wait_ge(s["k_hat_ready"], m + 1)
                pe.wait_ge(s["k_beta_ready"], m + 1)
                for h in range(GDN_H):
                    nc.tensor.transpose(heads(4)[:, h], k_hat[:, h], ident[:])
                    last = nc.tensor.transpose(heads(5)[:, h], k_beta[:, h], ident[:])
                last.then_inc(s["k_turned"], 1)
                share()
                pe.wait_ge(s["kT_copied"], 2 * (m + 1))
                pe.wait_ge(s["decay_log"], m + 1)
                for h in range(GDN_H):
                    nc.tensor.matmul(heads(1)[:, h], kT[:, h], kbT[:, h], start=True, stop=True)
                    last = nc.tensor.matmul(heads(2)[:, h], kT[:, h], q_ch[:, h], start=True, stop=True)
                last.then_inc(s["pairs_ready"], 1)
                share()
                pe.wait_ge(s["Y_ready"], NL * m + 1)
                for h in range(GDN_H):
                    last = nc.tensor.transpose(heads(3)[:, h], Y[:, h], ident[:])
                last.then_inc(s["X_turned"], 1)
                pe.wait_ge(s["G_ready"], m + 1)
                pe.wait_ge(s["x_end_ready"], m + 1)
                pe.wait_ge(s["A_ready"], m + 1)
                for h in range(SSD_H):
                    nc.tensor.matmul(heads(4, SSD_H, SSD_P)[:, h], G[:, h], x_dt[:, h], start=True, stop=True)
                for g in range(SSD_G):
                    half = slice(g * SSD_R * SSD_P, (g + 1) * SSD_R * SSD_P)
                    group = slice(g * SSD_R, (g + 1) * SSD_R)
                    nc.tensor.matmul(bank[:, 5, half], C_T[:, g], S_ssd[:, group].rearrange("p h w -> p (h w)"),
                                     start=True, stop=True)
                    last = nc.tensor.matmul(bank[:, 1, half], tok[:, TOK_B + g * P:TOK_B + (g + 1) * P],
                                            x_end[:, group].rearrange("p h w -> p (h w)"), start=True, stop=True)
                last.then_inc(s["ssd_out"], 1)
                share()
                pe.wait_ge(s["qk_ready"], m + 1)
                for n in range(1, NL):
                    pe.wait_ge(s["M_ready"], NL * m + n + 1)
                    pe.wait_ge(s["X_ready"], (NL - 1) * m + n)
                    for h in range(GDN_H):
                        last = nc.tensor.matmul(heads(0)[:, h], M_T[:, n % 2, h], X[:, h], start=True, stop=True)
                    last.then_inc(s["MX_ready"], 1)
                    pe.wait_ge(s["MX_copied"], (NL - 1) * m + n)
                    pe.wait_ge(s["Y_ready"], NL * m + n)
                    for h in range(GDN_H):
                        if n < NL - 1:
                            nc.tensor.matmul(heads(2)[:, h], Y[:, h], MX[:, h], start=True, stop=True)
                        last = nc.tensor.matmul(heads(3)[:, h], MX[:, h], Y[:, h], start=True, stop=True)
                    last.then_inc(s["steps_ready"], 1)
                    share()
                pe.wait_ge(s["Y_ready"], NL * (m + 1))
                for h in range(GDN_H):
                    last = nc.tensor.matmul(heads(0)[:, h], k_in[:, h], Y[:, h], start=True, stop=True)
                last.then_inc(s["w_ready"], 1)
                pe.wait_ge(s["w_copied"], m + 1)
                for h in range(GDN_H):
                    nc.tensor.matmul(heads(2)[:, h], Y[:, h], v_beta[:, h], start=True, stop=False)
                    last = nc.tensor.matmul(heads(2)[:, h], wT[:, h], S_gdn[:, h], start=False, stop=True)
                last.then_inc(s["v_new_ready"], 1)
                pe.wait_ge(s["y_part"], 2 * (m + 1))
                pe.wait_ge(s["v_new_copied"], m + 1)
                for h in range(GDN_H):
                    nc.tensor.matmul(heads(3)[:, h], q_ch[:, h], S_gdn[:, h], start=True, stop=True)
                    nc.tensor.matmul(heads(4)[:, h], qk[:, h], v_new[:, h], start=True, stop=True)
                    last = nc.tensor.matmul(heads(5)[:, h], k_out[:, h], v_new[:, h], start=True, stop=True)
                last.then_inc(s["gdn_out"], 1)
                share()
                share()
                share()
                pe.wait_ge(s["mix_ssd"], m + 1)
                pe.wait_ge(s["mix_gdn"], m + 1)
                pe.wait_ge(s["S_ssd_ready"], m + 1)
                for k in range(KD):
                    last = nc.tensor.transpose(heads(k // 4)[:, k % 4], mix[:, k * P:(k + 1) * P], ident[:])
                last.then_inc(s["mix_turned"], 1)
                pe.wait_ge(s["mixT_copied"], m + 1)
                for half in range(D // BANK):
                    for k in range(KD):
                        last = nc.tensor.matmul(bank[:, 2 + half], mixT[:, k], w_out[:, k, half * BANK:(half + 1) * BANK],
                                                start=(k == 0), stop=(k == KD - 1))
                last.then_inc(s["out_proj"], 1)
                row_of(0, (bank[:, 0], bank[:, 1])).then_inc(s["ffn_row_ready"], 1)
                share()
                share()
                pe.wait_ge(s["h2_ready"], m + 1)
                pe.wait_ge(s["S_gdn_ready"], m + 1)
                for k in range(KD):
                    last = nc.tensor.transpose(square(4, 2)[:, k], h2[:, k * P:(k + 1) * P], ident[:])
                last.then_inc(s["h_turned"], 1)
                pe.wait_ge(s["hT_copied"], m + 1)
                for b in range(4):
                    for k in range(KD):
                        last = nc.tensor.matmul(bank[:, b], h_T[:, k], w_q[:, k, b * BANK:(b + 1) * BANK],
                                                start=(k == 0), stop=(k == KD - 1))
                    last.then_inc(s["q_ready"], 1)
                    share()
                for b in range(4):
                    pe.wait_ge(s["q_copied"], 4 * m + b + 1)
                    if b >= 2:
                        pe.wait_ge(s["qT_copied"], 4 * m + b - 1)
                    for n in range(4):
                        last = nc.tensor.transpose(square(4 + b % 2)[:, n], q[:, b % 2, n], ident[:])
                    last.then_inc(s["q_turned"], 1)
                    pe.wait_ge(s["qT_copied"], 4 * m + b + 1)
                    for n in range(4):
                        last = nc.tensor.matmul(square(b)[:, n], q_T[:, b % 2, n], keys_T[:, n % 2], start=True, stop=True)
                last.then_inc(s["score_ready"], 1)
                share()

            pe.wait_ge(s["consts"], 16 * N_CONST)
            for half in range(2):
                last = nc.tensor.transpose(bank[:, 0, half * P:(half + 1) * P], arena[:, half * P:(half + 1) * P], ident[:])
            last.then_inc(s["keys_turned"], 1)
            pe.wait_ge(s["keys_copied"], 1)

            def body(m, e):
                share = expert_share(e, do)
                if m is not None:
                    steps(m, share)
                share(last=True)
                if e is not None:
                    pe.wait_ge(s["res_mean"], e + 1)
                    row_of(1, (y_ps[:, 0], y_ps[:, 1])).then_inc(s["final_row_ready"], 1)

            tile_loop(pe, body)

        @block.scalar
        def _(act):
            def do(item, e):
                kind, n = item
                if kind == "G":
                    after_use(act, ("U", (n + 1) * GROUP - 1), e)
                    group = slice(n * GROUP, (n + 1) * GROUP)
                    nc.scalar.activation(coef[:, group], dots[:, group], ACT.Gelu).then_inc(s["gelu_ready"], 1)
                    nc.scalar.preload_act_table_set(LOG_EXP_SET)
                if kind == "V" and n % 2:
                    act.wait_ge(s["coef_ready"], PICKS // GROUP * e + n // GROUP + 1)
                    if n >= 5:
                        after_use(act, ("V", n - 4), e)
                    nc.scalar.activation(diag[:, n // 2 % 2], ident[:], ACT.Copy, scale=coef[:, n:n + 1]).then_inc(s["diag_ready"], 1)

            def steps(m, share):
                act.wait_ge(s["small_in"], m + 1)
                nc.scalar.activation(small_abs[:], small[:], ACT.Abs).then_inc(s["small_abs_done"], 1)
                act.wait_ge(s["small_abs_done"], m + 1)
                nc.scalar.activation(small_exp[:], small_abs[:], ACT.Exp, scale=-1.0).then_inc(s["small_exp_done"], 1)
                act.wait_ge(s["small_exp_done"], m + 1)
                nc.scalar.activation(soft[:], small_exp[:, 0:HEADS], ACT.Ln, bias=1.0).then_inc(s["soft_log"], 1)
                nc.scalar.activation(qk_sq, tok[:, SSD_W + SSD_G * P:TOK - GDN_W], ACT.Square).then_inc(s["qk_sq_ready"], 1)
                share()
                act.wait_ge(s["qk_sum"], m + 1)
                nc.scalar.activation(qk_log[:], qk_ms[:], ACT.Ln, bias=eps[:]).then_inc(s["qk_logged"], 1)
                act.wait_ge(s["qk_logged"], m + 1)
                nc.scalar.activation(qk_r[:], qk_log[:], ACT.Exp, scale=-0.5).then_inc(s["qk_r_ready"], 1)
                share()
                act.wait_ge(s["logs_ready"], 2 * (m + 1))
                nc.scalar.activation(exps[:], logs[:], ACT.Exp).then_inc(s["exps_ready"], 1)
                act.wait_ge(s["decay_log"], m + 1)
                nc.scalar.activation(decay, decay, ACT.Exp).then_inc(s["decay_ready"], 1)
                share()
                act.wait_ge(s["k_turned"], m + 1)
                nc.scalar.copy(kT, heads(4)).then_inc(s["kT_copied"], 1)
                nc.scalar.copy(kbT, heads(5)).then_inc(s["kT_copied"], 1)
                share()
                share()
                act.wait_ge(s["X_turned"], m + 1)
                act.wait_ge(s["k_in_ready"], m + 1)
                nc.scalar.copy(X, heads(3)).then_inc(s["X_ready"], 1)
                share()
                for n in range(1, NL):
                    act.wait_ge(s["MX_ready"], (NL - 1) * m + n)
                    nc.scalar.copy(MX, heads(0)).then_inc(s["MX_copied"], 1)
                    share()
                act.wait_ge(s["w_ready"], m + 1)
                nc.scalar.mul(wT, heads(0), -1.0).then_inc(s["w_copied"], 1)
                act.wait_ge(s["v_new_ready"], m + 1)
                nc.scalar.copy(v_new, heads(2)).then_inc(s["v_new_copied"], 1)
                share()
                act.wait_ge(s["y_gated"], m + 1)
                nc.scalar.activation(y_skip, y_ssd, ACT.Square, scale=SSD_W ** -0.5, accum_out=stat[:, 0:1]).then_inc(s["y_mean"], 1)
                act.wait_ge(s["y_mean"], m + 1)
                nc.scalar.activation(stat[:, 1:2], stat[:, 0:1], ACT.Ln, bias=eps[:]).then_inc(s["y_logged"], 1)
                act.wait_ge(s["y_logged"], m + 1)
                nc.scalar.activation(stat[:, 2:3], stat[:, 1:2], ACT.Exp, scale=-0.5).then_inc(s["y_r_ready"], 1)
                act.wait_ge(s["o_part"], 3 * (m + 1))
                nc.scalar.activation(view(qk_sq[:, 0:GDN_W], GDN_H, P), o_gdn, ACT.Square, scale=P ** -0.5).then_inc(s["o_sq_ready"], 1)
                share()
                act.wait_ge(s["o_sum"], m + 1)
                nc.scalar.activation(r_gdn[:, 1], r_gdn[:, 0], ACT.Ln, bias=eps[:]).then_inc(s["o_logged"], 1)
                act.wait_ge(s["o_logged"], m + 1)
                nc.scalar.activation(r_gdn[:, 2], r_gdn[:, 1], ACT.Exp, scale=-0.5).then_inc(s["o_r_ready"], 1)
                share()
                act.wait_ge(s["mix_turned"], m + 1)
                nc.scalar.copy(mixT, square(0, 2)).then_inc(s["mixT_copied"], 1)
                share()
                act.wait_ge(s["x2_ready"], m + 1)
                nc.scalar.activation(mix, x2[:], ACT.Square, scale=D ** -0.5, accum_out=stat[:, 3:4]).then_inc(s["x2_mean"], 1)
                act.wait_ge(s["x2_mean"], m + 1)
                nc.scalar.activation(stat[:, 4:5], stat[:, 3:4], ACT.Ln, bias=eps[:]).then_inc(s["x2_logged"], 1)
                act.wait_ge(s["x2_logged"], m + 1)
                nc.scalar.activation(stat[:, 5:6], stat[:, 4:5], ACT.Exp, scale=-0.5).then_inc(s["x2_r_ready"], 1)
                share()
                act.wait_ge(s["h_turned"], m + 1)
                nc.scalar.copy(h_T, square(4, 2)).then_inc(s["hT_copied"], 1)
                for b in range(4):
                    act.wait_ge(s["q_ready"], 4 * m + b + 1)
                    if b < 2:
                        nc.scalar.copy(q[:, b], square(b)).then_inc(s["q_copied"], 1)
                    share()
                for b in range(4):
                    act.wait_ge(s["q_turned"], 4 * m + b + 1)
                    nc.scalar.copy(q_T[:, b % 2], square(4 + b % 2)).then_inc(s["qT_copied"], 1)
                    if b < 2:
                        nc.scalar.copy(q[:, b], square(2 + b)).then_inc(s["q_copied"], 1)
                act.wait_ge(s["score_ready"], m + 1)
                nc.scalar.copy(score, square(0, 4)).then_inc(s["score_copied"], 1)
                share()
                for _ in range(15):
                    share()
                act.wait_ge(s["shifted_ready"], m + 1)
                nc.scalar.activation(weight, shifted, ACT.Exp).then_inc(s["weight_ready"], 1)

            nc.scalar.preload_act_table_set(LOG_EXP_SET)
            act.wait_ge(s["consts"], 16 * N_CONST)
            act.wait_ge(s["eps_set_m"], 1)
            nc.scalar.activation(neg_a[:], neg_a[:], ACT.Exp).then_inc(s["neg_a_exp"], 1)
            act.wait_ge(s["keys_turned"], 1)
            nc.scalar.copy(keys_T[:], bank[:, 0, 0:2 * P].rearrange("p (n k) -> p n k", n=2)).then_inc(s["keys_copied"], 1)

            def body(m, e):
                share = expert_share(e, do)
                if m is not None:
                    steps(m, share)
                share(last=True)
                if e is not None:
                    act.wait_ge(s["y_ready"], e + 1)
                    nc.scalar.activation(y_ps[:].rearrange("p b w -> p (b w)"), y[:], ACT.Square, scale=D ** -0.5,
                                         accum_out=stat_e[:, 0:1]).then_inc(s["res_mean"], 1)
                    act.wait_ge(s["res_mean"], e + 1)
                    nc.scalar.activation(stat_e[:, 1:2], stat_e[:, 0:1], ACT.Ln, bias=eps[:]).then_inc(s["res_logged"], 1)
                    act.wait_ge(s["res_logged"], e + 1)
                    nc.scalar.activation(stat_e[:, 2:3], stat_e[:, 1:2], ACT.Exp, scale=-0.5).then_inc(s["res_r_ready"], 1)

            tile_loop(act, body)

        @block.vector
        def _(dve):
            tt, ts, stt = nc.vector.tensor_tensor, nc.vector.tensor_scalar, nc.vector.scalar_tensor_tensor

            def do(item, e):
                kind, n = item
                if kind == "U":
                    after_fill(dve, item, e)
                    j = slot_of(item)
                    nc.vector.tensor_tensor_reduce(out=ring[:, j], in0=ring[:, j], in1=h2_e[:], scale=1.0, scalar=0.0,
                                                   op0=ALU.mult, op1=ALU.add, accum_out=dots[:, n:n + 1]).then_inc(used[j], 1)
                if kind == "C":
                    group = slice(n * GROUP, (n + 1) * GROUP)
                    dve.wait_ge(s["gelu_ready"], PICKS // GROUP * e + n + 1)
                    tt(coef[:, group], coef[:, group], gates[:].rearrange("p h k -> p (h k)")[:, group], ALU.mult).then_inc(s["coef_ready"], 1)
                if kind == "X":
                    dve.wait_ge(s["y_free"], e + 1)
                    nc.vector.tensor_copy(y[:], x2[:]).then_inc(s["x2_copied"], 1)
                if kind == "V" and n % 2 == 0:
                    dve.wait_ge(s["coef_ready"], PICKS // GROUP * e + n // GROUP + 1)
                    if n == 0:
                        dve.wait_ge(s["x2_copied"], e + 1)
                    else:
                        after_use(dve, ("V", n - 2), e)
                    after_fill(dve, item, e)
                    stt(out=y[:], in0=ring[:, slot_of(item)], scalar=coef[:, n:n + 1], in1=y[:],
                        op0=ALU.mult, op1=ALU.add).then_inc(used[slot_of(item)], 1)

            def top16(m, n, src, low, value, where, hi, hi_at, low_ready, lo, lo_at, share):
                def lists(op, last_sem):
                    for t in range(n):
                        last = op(t)
                        if t % 8 == 7:
                            if t == n - 1:
                                last.then_inc(s[last_sem], 1)
                            share()

                lists(lambda t: nc.vector.max(value[:, t, 0:8], src[:, t]), hi)
                dve.wait_ge(s[hi], m + 1)
                dve.sem_inc(s["held_dve"])
                lists(lambda t: nc.vector.match_replace(low[:, t], value[:, t, 0:8], src[:, t], -3e38), low_ready)
                lists(lambda t: nc.vector.max_index(where[:, t, 0:8], value[:, t, 0:8], src[:, t]), hi_at)
                dve.wait_ge(s[low_ready], m + 1)
                dve.sem_inc(s["held_dve"])
                lists(lambda t: nc.vector.max(value[:, t, 8:16], low[:, t]), lo)
                dve.wait_ge(s[lo], m + 1)
                dve.sem_inc(s["held_dve"])
                lists(lambda t: nc.vector.max_index(where[:, t, 8:16], value[:, t, 8:16], low[:, t]), lo_at)
                dve.wait_ge(s[hi_at], m + 1)
                dve.wait_ge(s[lo_at], m + 1)

            def steps(m, share):
                dve.wait_ge(s["mix_loaded"], 16 * LOADS * (m + 1))
                tt(small[:], zgs[:, ZG:], head_bias[:], ALU.add).then_inc(s["small_in"], 1)
                share()
                dve.wait_ge(s["soft_log"], m + 1)
                stt(out=soft[:], in0=small[:, 0:HEADS], scalar=0.0, in1=soft[:], op0=ALU.max, op1=ALU.add).then_inc(s["soft_sum"], 1)
                dve.wait_ge(s["soft_sum"], m + 1)
                tt(rate[:], soft[:], neg_a[:], ALU.mult).then_inc(s["rate_ready"], 1)
                b_exp = small_exp[:, HEADS:]
                ts(beta_den[:], b_exp, 1.0, None, ALU.add).then_inc(s["beta_parts"], 1)
                stt(out=beta_num[:], in0=small[:, HEADS:], scalar=0.0, in1=b_exp, op0=ALU.is_ge, op1=ALU.max).then_inc(s["beta_parts"], 1)
                dve.wait_ge(s["beta_parts"], 3 * m + 2)
                nc.vector.reciprocal(beta_den[:], beta_den[:]).then_inc(s["beta_parts"], 1)
                dve.wait_ge(s["beta_parts"], 3 * (m + 1))
                tt(beta[:], beta_num[:], beta_den[:], ALU.mult).then_inc(s["beta_ready"], 1)
                dve.wait_ge(s["qk_sq_ready"], m + 1)
                nc.vector.tensor_reduce(qk_ms[:], view(qk_sq, 2 * GDN_H, P), AX_X, ALU.add).then_inc(s["qk_sum"], 1)
                share()
                dve.wait_ge(s["cums_ready"], m + 1)
                nc.vector.tensor_copy(logs[:, 0:2], heads(0, 2, HEADS)).then_inc(s["logs_copied"], 1)
                dve.wait_ge(s["logs_copied"], m + 1)
                tt(logs[:, 2], logs[:, 1], logs[:, 0], ALU.subtract).then_inc(s["logs_ready"], 2)
                dve.wait_ge(s["qk_sum"], m + 1)
                for h in range(HEADS):
                    last = stt(out=decay[:, h], in0=heads(1 + h // 4)[:, h % 4], scalar=logs[:, 0, h:h + 1], in1=floor[:],
                               op0=ALU.subtract, op1=ALU.min)
                last.then_inc(s["decay_log"], 1)
                share()
                dve.wait_ge(s["qk_r_ready"], m + 1)
                tt(k_hat, qkv[:, 1], over_free(qk_r[:, GDN_H:], P), ALU.mult).then_inc(s["k_hat_ready"], 1)
                dve.wait_ge(s["k_hat_ready"], m + 1)
                dve.wait_ge(s["beta_ready"], m + 1)
                tt(k_beta, k_hat, over_free(beta[:], P), ALU.mult).then_inc(s["k_beta_ready"], 1)
                tt(v_beta, qkv[:, 2], over_free(beta[:], P), ALU.mult)
                dve.wait_ge(s["exps_ready"], m + 1)
                tt(k_out, k_hat, over_free(e_out[:, SSD_H:], P), ALU.mult)
                dve.wait_ge(s["k_beta_ready"], m + 1)
                tt(k_in, k_beta, over_free(e_in[:, SSD_H:], P), ALU.mult).then_inc(s["k_in_ready"], 1)
                share()
                tt(x_dt, xs, over_free(soft[:, 0:SSD_H], SSD_P), ALU.mult).then_inc(s["x_dt_ready"], 1)
                dve.wait_ge(s["x_dt_ready"], m + 1)
                tt(x_end, x_dt, over_free(e_out[:, 0:SSD_H], SSD_P), ALU.mult).then_inc(s["x_end_ready"], 1)
                dve.wait_ge(s["decay_ready"], m + 1)
                for g in range(SSD_G):
                    group = slice(g * SSD_R, (g + 1) * SSD_R)
                    last = tt(G[:, group], over_heads(heads(0, 2, P, 256)[:, g], SSD_R), decay[:, group], ALU.mult)
                last.then_inc(s["G_ready"], 1)
                share()
                dve.wait_ge(s["pairs_ready"], m + 1)
                tt(A_T, heads(1), decay[:, SSD_H:], ALU.mult).then_inc(s["A_ready"], 1)
                tt(qk, heads(2), decay[:, SSD_H:], ALU.mult).then_inc(s["qk_ready"], 1)
                dve.wait_ge(s["A_ready"], m + 1)
                dve.wait_ge(s["G_ready"], m + 1)
                tt(M_T[:, 0], A_T, over_heads(level[:, 0], GDN_H), ALU.mult).then_inc(s["M_ready"], 1)
                dve.wait_ge(s["M_ready"], NL * m + 1)
                tt(Y, over_heads(ident[:], GDN_H), M_T[:, 0], ALU.subtract).then_inc(s["Y_ready"], 1)
                tt(M_T[:, 1], A_T, over_heads(level[:, 1], GDN_H), ALU.mult).then_inc(s["M_ready"], 1)
                share()
                for n in range(1, NL):
                    if n > 1:
                        dve.wait_ge(s["steps_ready"], (NL - 1) * m + n - 1)
                        tt(X, X, heads(2), ALU.subtract).then_inc(s["X_ready"], 1)
                        tt(Y, Y, heads(3), ALU.subtract).then_inc(s["Y_ready"], 1)
                    if n + 1 < NL:
                        dve.wait_ge(s["Y_ready"], NL * m + n)
                        tt(M_T[:, (n + 1) % 2], A_T, over_heads(level[:, n + 1], GDN_H), ALU.mult).then_inc(s["M_ready"], 1)
                    share()
                dve.wait_ge(s["steps_ready"], (NL - 1) * (m + 1))
                tt(Y, Y, heads(3), ALU.subtract).then_inc(s["Y_ready"], 1)
                dve.wait_ge(s["ssd_out"], m + 1)
                tt(y_ssd, heads(5, SSD_H, SSD_P), over_free(e_in[:, 0:SSD_H], SSD_P), ALU.mult).then_inc(s["y_part"], 1)
                tt(y_skip, xs, over_free(d_head[:], SSD_P), ALU.mult)
                dve.wait_ge(s["y_part"], 2 * m + 1)
                tt(y_ssd, y_ssd, heads(4, SSD_H, SSD_P), ALU.add).then_inc(s["y_part"], 1)
                dve.wait_ge(s["y_part"], 2 * (m + 1))
                tt(y_ssd, y_ssd, y_skip, ALU.add).then_inc(s["S_ssd_part"], 1)
                dve.wait_ge(s["S_ssd_part"], 2 * m + 1)
                tt(y_ssd, y_ssd, view(zgs[:, 0:SSD_W], SSD_H, SSD_P), ALU.mult).then_inc(s["y_gated"], 1)
                tt(S_ssd[:], S_ssd[:], over_free(e_all[:, 0:SSD_H], SSD_P), ALU.mult).then_inc(s["S_ssd_part"], 1)
                dve.wait_ge(s["S_ssd_part"], 2 * (m + 1))
                tt(S_ssd[:], S_ssd[:], heads(1, SSD_H, SSD_P), ALU.add).then_inc(s["S_ssd_ready"], 1)
                share()
                dve.wait_ge(s["gdn_out"], m + 1)
                tt(o_gdn, heads(3), over_free(e_in[:, SSD_H:], P), ALU.mult).then_inc(s["o_part"], 1)
                dve.wait_ge(s["o_part"], 3 * m + 1)
                tt(o_gdn, o_gdn, heads(4), ALU.add).then_inc(s["o_part"], 1)
                tt(S_gdn[:], S_gdn[:], over_free(e_all[:, SSD_H:], P), ALU.mult).then_inc(s["S_gdn_part"], 1)
                dve.wait_ge(s["o_part"], 3 * m + 2)
                stt(out=o_gdn, in0=o_gdn, scalar=P ** -0.5, in1=over_free(qk_r[:, 0:GDN_H], P),
                    op0=ALU.mult, op1=ALU.mult).then_inc(s["o_part"], 1)
                dve.wait_ge(s["S_gdn_part"], m + 1)
                tt(S_gdn[:], S_gdn[:], heads(5), ALU.add).then_inc(s["S_gdn_ready"], 1)
                share()
                dve.wait_ge(s["y_r_ready"], m + 1)
                ts(mix[:, 0:SSD_W], y_ssd.rearrange("p h w -> p (h w)"), stat[:, 2:3], None, ALU.mult).then_inc(s["mix_ssd"], 1)
                dve.wait_ge(s["o_sq_ready"], m + 1)
                nc.vector.tensor_reduce(r_gdn[:, 0], view(qk_sq[:, 0:GDN_W], GDN_H, P), AX_X, ALU.add).then_inc(s["o_sum"], 1)
                share()
                dve.wait_ge(s["o_r_ready"], m + 1)
                tt(o_gdn, o_gdn, over_free(r_gdn[:, 2], P), ALU.mult).then_inc(s["o_scaled"], 1)
                dve.wait_ge(s["o_scaled"], m + 1)
                tt(view(mix[:, SSD_W:], GDN_H, P), o_gdn, view(zgs[:, SSD_W:ZG], GDN_H, P), ALU.mult).then_inc(s["mix_gdn"], 1)
                share()
                dve.wait_ge(s["out_proj"], m + 1)
                dve.wait_ge(s["x2_in"], 16 * (m + 1))
                tt(x2[:], x2[:], bank[:, 2:4].rearrange("p b w -> p (b w)"), ALU.add).then_inc(s["x2_ready"], 1)
                share()
                dve.wait_ge(s["x2_r_ready"], m + 1)
                dve.wait_ge(s["ffn_row_ready"], m + 1)
                stt(out=h2[:], in0=x2[:], scalar=stat[:, 5:6], in1=bank[:, 0:2].rearrange("p b w -> p (b w)"),
                    op0=ALU.mult, op1=ALU.mult).then_inc(s["h2_ready"], 1)
                for _ in range(5):
                    share()
                dve.wait_ge(s["score_copied"], m + 1)
                dve.sem_inc(s["held_dve"])
                top16(m, LISTS, score, rest, best, best_at, "best_hi", "best_hi_at", "rest_ready", "best_lo", "best_lo_at", share)
                nc.vector.tensor_copy(best_key, best_at).then_inc(s["key_ready"], 1)
                b, k = (t.rearrange("p (h two) k -> p h two k", two=2) for t in (best, best_key))
                n8, at = TOPK // 2, 0
                dve.wait_ge(s["key_ready"], m + 1)
                for a, n in RUNS:
                    tt(cand[:, :, at:at + n], b[:, :, 0, a:a + 1].broadcast_to([P, PEER_H, n]), b[:, :, 1, 0:n], ALU.add)
                    stt(out=cand_id[:, :, at:at + n], in0=k[:, :, 0, a:a + 1].broadcast_to([P, PEER_H, n]), scalar=float(N_KEYS),
                        in1=k[:, :, 1, 0:n], op0=ALU.mult, op1=ALU.add)
                    at += n
                stt(out=cand_id[:, :, at:], in0=k[:, :, 0, n8:], scalar=float(N_KEYS),
                    in1=k[:, :, 1, 0:1].broadcast_to([P, PEER_H, n8]), op0=ALU.mult, op1=ALU.add).then_inc(s["id_ready"], 1)
                tt(cand[:, :, at:], b[:, :, 0, n8:], b[:, :, 1, 0:1].broadcast_to([P, PEER_H, n8]),
                   ALU.add).then_inc(s["cand_ready"], 1)
                share()
                dve.wait_ge(s["cand_ready"], m + 1)
                dve.sem_inc(s["held_dve"])
                top16(m, PEER_H, cand, cand_rest, top, top_at, "top_hi", "top_hi_at", "cand_rest_ready", "top_lo", "top_lo_at", share)
                nc.vector.tensor_copy(top_rank, top_at).then_inc(s["top_rank_ready"], 1)
                tt(shifted, top, top[:, :, 0:1].broadcast_to([P, PEER_H, TOPK]), ALU.subtract).then_inc(s["shifted_ready"], 1)
                dve.wait_ge(s["top_rank_ready"], m + 1)
                full = [P, HALF_H, TOPK, CANDS]
                for half in range(2):
                    hs = slice(half * HALF_H, (half + 1) * HALF_H)
                    if half:
                        dve.wait_ge(s["top_id_ready"], 2 * m + 1)
                    tt(chosen, rank[:, None, None, :].broadcast_to(full), top_rank[:, hs, :, None].broadcast_to(full),
                       ALU.is_equal).then_inc(s["chosen_ready"], 1)
                    share()
                    dve.wait_ge(s["chosen_ready"], 2 * m + half + 1)
                    tt(chosen, chosen, cand_id[:, hs, None, :].broadcast_to(full), ALU.mult).then_inc(s["chosen_id"], 1)
                    share()
                    dve.wait_ge(s["chosen_id"], 2 * m + half + 1)
                    nc.vector.tensor_reduce(top_id[:, hs], chosen, AX_X, ALU.add).then_inc(s["top_id_ready"], 1)
                    share()
                dve.wait_ge(s["weight_ready"], m + 1)
                nc.vector.tensor_reduce(total[:], weight, AX_X, ALU.add).then_inc(s["total_ready"], 1)
                dve.wait_ge(s["total_ready"], m + 1)
                nc.vector.reciprocal(total[:], total[:]).then_inc(s["total_inv"], 1)
                dve.wait_ge(s["total_inv"], m + 1)
                tt(gates[:], weight, over_free(total[:], TOPK), ALU.mult).then_inc(s["gates_ready"], 1)
                dve.wait_ge(s["top_id_ready"], 2 * (m + 1))
                nc.vector.tensor_copy(picks[:].rearrange("p (h k) -> p h k", h=PEER_H), top_id).then_inc(s["picks_ready"], 1)
                dve.wait_ge(s["h2_ready"], m + 1)
                nc.vector.tensor_copy(h2_e[:], h2[:]).then_inc(s["h2_copied"], 1)

            nc.vector.memset(eps[:], EPS).then_inc(s["eps_set_m"], 1)
            nc.vector.memset(S_gdn[:], 0.0).then_inc(s["setup_done"], 1)
            nc.vector.memset(S_ssd[:], 0.0).then_inc(s["setup_done"], 1)
            dve.wait_ge(s["consts"], 16 * N_CONST)
            nc.vector.memset(head_bias[:, HEADS:], 0.0).then_inc(s["setup_done"], 1)
            for k in range(KD):
                nc.vector.tensor_scalar(w_out[:, k], w_out[:, k], w_mix[:, min(k, 4):min(k, 4) + 1], None,
                                        ALU.mult).then_inc(s["setup_done"], 1)
            dve.wait_ge(s["neg_a_exp"], 1)
            ts(neg_a[:], neg_a[:], -1.0, None, ALU.mult).then_inc(s["setup_done"], 1)
            dve.wait_ge(s["setup_done"], 4 + KD)
            for j in range(SLOTS):
                dve.sem_inc(used[j])
            dve.sem_inc(s["y_free"])

            def body(m, e):
                share = expert_share(e, do)
                if m is not None:
                    steps(m, share)
                share(last=True)
                if e is not None:
                    after_use(dve, ("V", PICKS - 1), e)
                    after_use(dve, ("V", PICKS - 2), e)
                    tt(y[:], y[:], y_ps[:].rearrange("p b w -> p (b w)"), ALU.add).then_inc(s["y_ready"], 1)
                    dve.wait_ge(s["res_r_ready"], e + 1)
                    dve.wait_ge(s["final_row_ready"], e + 1)
                    stt(out=y[:], in0=y[:], scalar=stat_e[:, 2:3], in1=y_ps[:].rearrange("p b w -> p (b w)"),
                        op0=ALU.mult, op1=ALU.mult).then_inc(s["out_ready"], 1)

            tile_loop(dve, body)


def program(nc, A, out):
    ch_scr = nc.dram_tensor("ch_scr", [BLOCKS, P, SEQ], F32).ap()
    tok_scr = nc.dram_tensor("tok_scr", [SEQ, CONV_CH], F32).ap()
    zgs_scr = nc.dram_tensor("zgs_scr", [SEQ, ZGS], F32).ap()
    with nc.sbuf_tensor("hn_T", [P, KD, SEQ], F32) as hn_T:
        norm_stage(nc, A, hn_T)
        conv_stage(nc, A, hn_T, ch_scr, tok_scr)
        gate_stage(nc, A, hn_T, zgs_scr)
    tile_stage(nc, A, ch_scr, tok_scr, zgs_scr, out)


_OUT = ((1, SEQ, D), "float32")


def constants():
    import numpy as np

    s, l = np.arange(P)[:, None], np.arange(P)[None, :]
    level = [((s // b % 2 == 0) & (l // b == s // b + 1)).astype(np.float32) for b in LEVELS]
    return {
        "c_ident": np.eye(P, dtype=np.float32),
        "c_upper": (s <= l).astype(np.float32),
        "c_ones": np.ones((P, P), np.float32),
        "c_floor": np.where(s <= l, 0.0, NEG).astype(np.float32),
        "c_level": np.stack(level, axis=1),
        "c_rank": np.broadcast_to(np.arange(CANDS, dtype=np.float32), (P, CANDS)).copy(),
    }


def kernel(**inputs):
    import numpy as _np
    import concourse.bacc as _bacc
    from concourse import mybir as _mybir
    from concourse.bass_utils import run_bass_kernel_spmd as _run

    nc = _bacc.Bacc("TRN2", target_bir_lowering=False, num_devices=1)
    arrays, args = {}, {}
    for name, value in {**inputs, **constants()}.items():
        a = _np.ascontiguousarray(value)
        arrays[f"in_{name}_dram"] = a
        args[name] = nc.dram_tensor(f"in_{name}_dram", a.shape, _mybir.dt.from_np(a.dtype), kind="ExternalInput").ap()
    out = nc.dram_tensor("out_0_dram", _OUT[0], _mybir.dt.from_np(_np.dtype(_OUT[1])), kind="ExternalOutput").ap()
    program(nc, args, out)
    r = _run(nc, [arrays], core_ids=[0])
    return r.results[0]["out_0_dram"]
```

```python
from contextlib import ExitStack

import concourse.bass as bass
from concourse import mybir

ALU = mybir.AluOpType
ACT = mybir.ActivationFunctionType
F32 = mybir.dt.float32
U32 = mybir.dt.uint32
LOG_EXP_SET = "natural_log_exp_and_others"
AX_X = mybir.AxisListType.X

P = 128
D = 1024
SEQ = 1024
KD = D // P
TILES = SEQ // P
BANK = 512
EPS = 1e-6
TAPS = 4
HALO = TAPS - 1

SSD_H, SSD_P, SSD_G = 8, 64, 2
SSD_R = SSD_H // SSD_G
SSD_W = SSD_H * SSD_P
GDN_H = 4
GDN_W = GDN_H * P
HEADS = SSD_H + GDN_H
SSD_BLOCKS = (SSD_W + 2 * SSD_G * P) // P
GDN_BLOCKS = 3 * GDN_W // P
BLOCKS = SSD_BLOCKS + GDN_BLOCKS
CONV_CH = BLOCKS * P

COL_XBC = SSD_W
COL_DT = COL_XBC + SSD_BLOCKS * P
COL_QKV = COL_DT + SSD_H
COL_GATE = COL_QKV + GDN_BLOCKS * P
COL_BETA = COL_GATE + GDN_W
COL_ALPHA = COL_BETA + GDN_H
SMALL = HEADS + GDN_H
ZG = SSD_W + GDN_W
ZGS = ZG + SMALL

TOK_B = SSD_W
TOK_Q = SSD_BLOCKS * P
TOK_K = TOK_Q + GDN_W
TOK_V = TOK_K + GDN_W
CH_FIRST = SSD_W // P
CH_N = 2 * SSD_G + GDN_H

LEVELS = [1 << n for n in range(7)]
NEG = -1e4

PEER_H = 8
TOPK = 16
LISTS = 2 * PEER_H
N_KEYS = 128
PICKS = PEER_H * TOPK
RUNS = [(a, TOPK // (a + 1)) for a in range(TOPK // 2)]
CANDS = sum(n for _, n in RUNS) + TOPK // 2

SLOTS = 10
GROUP = 32
LAG = 40
TAIL = PICKS - LAG
assert LAG % SLOTS == 0


def expert_sequence():
    seq, v = [], 0
    for n in range(PICKS):
        seq.append(("U", n, 0))
        while v < min(LAG, (n + 1) * 7 // 6 + 1):
            seq.append(("V", TAIL + v, 1))
            v += 1
        if n >= LAG:
            seq.append(("V", n - LAG, 0))
        if n % GROUP == GROUP - 1:
            seq.append(("G", n // GROUP, 0))
        if n == 3:
            seq.append(("C", PICKS // GROUP - 1, 1))
        if n % GROUP == 5 and n > GROUP:
            seq.append(("C", n // GROUP - 1, 0))
        for at, item in ((8, ("K", 0, 0)), (36, ("F", 0, 1)), (38, ("O", 0, 1)), (LAG - 1, ("X", 0, 0))):
            if n == at:
                seq.append(item)
    return seq


SEQUENCE = expert_sequence()
FIRST, FULL, LAST = "first", "full", "last"
BACKS = {FIRST: (0,), FULL: (0, 1), LAST: (1,)}


def gathers(mode):
    return [item for item in SEQUENCE if item[0] in "UV" and item[2] in BACKS[mode]]


ORDER = {mode: {item: n for n, item in enumerate(gathers(mode))} for mode in BACKS}
PACE = ([(4, .5)] * 3
        + [(4, .5)] * 6
        + [(8, .5)] * 6
        + [(6, .5)] * 4 + [(4, .5)] * 2
        + [(5, .1)] * 5 + [(4, .1)]
        + [(5, .1)] * 13
        + [(3, .9)] * 10 + [(5, .9)] + [(3, .9)] * 5
        + [(6, .9)] * 6
        + [(15, .5)])
SEGMENTS = len(PACE) - 1


def share_ends():
    return [round(len(SEQUENCE) * sum(work for work, _ in PACE[:n + 1]) / sum(work for work, _ in PACE))
            for n in range(len(PACE))]


SHARE_ENDS = share_ends()


def split_v():
    split, owed, at = ([], []), 0.0, 0
    for end, (_, on_pe) in zip(SHARE_ENDS, PACE):
        for kind, n, _ in SEQUENCE[at:end]:
            if kind == "V":
                owed += on_pe
                split[owed < 1].append(n)
                owed -= owed >= 1
        at = end
    return [sorted(s) for s in split]


PE_PICKS, DVE_PICKS = split_v()
USES = [len(range(j, len(ORDER[FULL]), SLOTS)) for j in range(SLOTS)]
FEWER = LAG // SLOTS


def scope(nc):
    ctx, taken = ExitStack(), []

    def clear():
        nc.clear_and_free_semaphores(taken)
        nc.all_engine_barrier()

    ctx.callback(clear)
    sb = lambda name, shape, dt=F32: ctx.enter_context(nc.sbuf_tensor(name, shape, dt))
    ps = lambda name, shape, dt=F32: ctx.enter_context(nc.psum_tensor(name, shape, dt))

    def sem(name):
        taken.append(nc.alloc_semaphore(name))
        return taken[-1]

    return ctx, sb, ps, sem


def norm_stage(nc, A, hn_T):
    ctx, sb, ps, sem = scope(nc)
    with ctx:
        x_in = sb("x_in", [P, 2, D])
        x_sq = sb("x_sq", [P, D])
        mean_sq = sb("mean_sq", [P, 2])
        log_ms = sb("log_ms", [P, 1])
        eps = sb("eps", [P, 1])
        rstd = sb("rstd", [P, 2])
        x_n = sb("x_n", [P, 2, D])
        w_col = sb("w_col", [P, KD])
        ident = sb("ident_n", [P, P])
        turned = [ps(f"turned{j}", [P, KD, P]) for j in range(2)]
        x_loaded = [sem("x_loaded_even"), sem("x_loaded_odd")]
        consts_loaded = sem("norm_consts_loaded")
        mean_done, rstd_done, xn_done = sem("mean_done"), sem("rstd_done"), sem("xn_done")
        eps_set, log_done = sem("eps_set"), sem("log_done")
        turn_done, hnT_done = sem("turn_done"), sem("hnT_done")
        x_rows = A["x"].rearrange("b (i p) d -> (b i) p d", p=P)
        block = ctx.enter_context(nc.Block())

        @block.sync
        def _(sp):
            with nc.allow_non_contiguous_dma(reason="one column of weights per channel block"):
                sp.dma_start(w_col[:], A["norm_mix_w"].rearrange("l (k p) -> p (l k)", p=P)).then_inc(consts_loaded, 16)
            sp.dma_start(ident[:], A["c_ident"]).then_inc(consts_loaded, 16)
            with sp.Fori(0, TILES // 2) as i:
                for j in range(2):
                    sp.wait_ge(xn_done, 2 * i)
                    sp.dma_start(x_in[:, j, :], x_rows[bass.ds(2 * i + j, 1)].rearrange("o p d -> (o p) d")).then_inc(x_loaded[j], 16)

        @block.scalar
        def _(act):
            nc.scalar.preload_act_table_set(LOG_EXP_SET)
            act.wait_ge(eps_set, 1)
            with act.Fori(0, TILES // 2) as i:
                for j in range(2):
                    act.wait_ge(x_loaded[j], 16 * (i + 1))
                    act.wait_ge(rstd_done, 2 * i + j)
                    nc.scalar.activation(x_sq[:], x_in[:, j, :], ACT.Square, scale=D ** -0.5,
                                         accum_out=mean_sq[:, j:j + 1]).then_inc(mean_done, 1)
                    act.wait_ge(mean_done, 2 * i + j + 1)
                    nc.scalar.activation(log_ms[:], mean_sq[:, j:j + 1], ACT.Ln, bias=eps[:]).then_inc(log_done, 1)
                    act.wait_ge(log_done, 2 * i + j + 1)
                    act.wait_ge(xn_done, 2 * i)
                    nc.scalar.activation(rstd[:, j:j + 1], log_ms[:], ACT.Exp, scale=-0.5).then_inc(rstd_done, 1)

        @block.vector
        def _(dve):
            nc.vector.memset(eps[:], EPS).then_inc(eps_set, 1)
            dve.wait_ge(consts_loaded, 32)
            with dve.Fori(0, TILES // 2) as i:
                for j in range(2):
                    t = 2 * i + j
                    dve.wait_ge(rstd_done, t + 1)
                    dve.wait_ge(turn_done, 2 * i)
                    nc.vector.tensor_scalar(x_n[:, j, :], x_in[:, j, :], rstd[:, j:j + 1], None,
                                            ALU.mult).then_inc(xn_done, 1)
                for j in range(2):
                    t = 2 * i + j
                    dve.wait_ge(turn_done, t + 1)
                    nc.vector.tensor_tensor(hn_T[:, :, bass.ds(t * P, P)], turned[j][:],
                                            w_col[:, :, None].broadcast_to([P, KD, P]), ALU.mult).then_inc(hnT_done, 1)

        @block.tensor
        def _(pe):
            pe.wait_ge(consts_loaded, 32)
            with pe.Fori(0, TILES // 2) as i:
                for j in range(2):
                    pe.wait_ge(xn_done, 2 * i + j + 1)
                    pe.wait_ge(hnT_done, 2 * i)
                    for k in range(KD):
                        last = nc.tensor.transpose(turned[j][:, k, :], x_n[:, j, k * P:(k + 1) * P], ident[:])
                    last.then_inc(turn_done, 1)


def conv_stage(nc, A, hn_T, ch_scr, tok_scr):
    ctx, sb, ps, sem = scope(nc)
    with ctx:
        w_blk = sb("w_blk", [P, 2, KD, P])
        pre = sb("pre", [P, 2, HALO + SEQ])
        mixed = sb("conv_sum", [P, 2, SEQ])
        post = sb("post", [P, 2, SEQ])
        frames = sb("frames", [P, 2, TILES, P])
        taps = sb("taps", [P, TAPS, BLOCKS])
        bias = sb("conv_bias", [P, BLOCKS])
        ident = sb("ident_c", [P, P])
        proj = [ps(f"proj{j}", [P, SEQ]) for j in range(2)]
        turned = [ps(f"post_turned{j}", [P, TILES, P]) for j in range(2)]
        consts_loaded, halo_zero = sem("conv_consts_loaded"), sem("halo_zero")
        w_loaded = [sem("w_loaded_even"), sem("w_loaded_odd")]
        proj_done, pre_done, tap_done = sem("proj_done"), sem("pre_done"), sem("tap_done")
        silu_done, turn_done, frames_done = sem("silu_done"), sem("post_turn_done"), sem("frames_done")
        ch_stored = [sem("ch_stored_even"), sem("ch_stored_odd")]
        tok_stored = [sem("tok_stored_even"), sem("tok_stored_odd")]
        w_in = A["w_in"].rearrange("l (k p) c -> p (l k) c", p=P)
        tok_out = tok_scr.rearrange("(i p) c -> p i c", p=P)
        block = ctx.enter_context(nc.Block())

        @block.sync
        def _(sp):
            with nc.allow_non_contiguous_dma(reason="one conv weight per channel"):
                for tap in range(TAPS):
                    sp.dma_start(taps[:, tap, 0:SSD_BLOCKS], A["ssd_conv_w"][0, tap].rearrange("(b p) -> p b", p=P)).then_inc(consts_loaded, 16)
                    sp.dma_start(taps[:, tap, SSD_BLOCKS:], A["gdn_conv_w"][0, tap].rearrange("(b p) -> p b", p=P)).then_inc(consts_loaded, 16)
                sp.dma_start(bias[:, 0:SSD_BLOCKS], A["ssd_conv_b"].rearrange("l (b p) -> p (l b)", p=P)).then_inc(consts_loaded, 16)
            sp.dma_start(ident[:], A["c_ident"]).then_inc(consts_loaded, 16)
            for first, last, col in ((0, SSD_BLOCKS, COL_XBC), (SSD_BLOCKS, BLOCKS, COL_QKV - SSD_BLOCKS * P)):
                with sp.Fori(first // 2, last // 2) as i:
                    for j in range(2):
                        sp.wait_ge(proj_done, 2 * i)
                        sp.dma_start(w_blk[:, j], w_in[:, :, bass.ds((2 * i + j) * P + col, P)]).then_inc(w_loaded[j], 16)

        @block.gpsimd
        def _(pool):
            with pool.Fori(0, BLOCKS // 2) as i:
                for j in range(2):
                    pool.wait_ge(silu_done, 2 * i + j + 1)
                    pool.dma_start(ch_scr[bass.ds(2 * i + j, 1)].rearrange("o p t -> (o p) t"), post[:, j]).then_inc(ch_stored[j], 16)
                    pool.wait_ge(frames_done, 2 * i + j + 1)
                    pool.dma_start(tok_out[:, :, bass.ds((2 * i + j) * P, P)], frames[:, j]).then_inc(tok_stored[j], 16)
            for s in (*ch_stored, *tok_stored):
                pool.wait_ge(s, 16 * (BLOCKS // 2))

        @block.tensor
        def _(pe):
            def project(i, j):
                pe.wait_ge(w_loaded[j], 16 * (i + 1))
                pe.wait_ge(pre_done, 2 * i)
                for half in range(SEQ // BANK):
                    cols = slice(half * BANK, (half + 1) * BANK)
                    for k in range(KD):
                        last = nc.tensor.matmul(proj[j][:, cols], w_blk[:, j, k, :], hn_T[:, k, cols],
                                                start=(k == 0), stop=(k == KD - 1))
                last.then_inc(proj_done, 1)

            def turn(i, j):
                pe.wait_ge(silu_done, 2 * i + j + 1)
                pe.wait_ge(frames_done, 2 * i)
                for t in range(TILES):
                    last = nc.tensor.transpose(turned[j][:, t, :], post[:, j, t * P:(t + 1) * P], ident[:])
                last.then_inc(turn_done, 1)

            pe.wait_ge(consts_loaded, 16 * (2 * TAPS + 2))
            project(0, 0)
            with pe.Fori(0, BLOCKS // 2 - 1) as i:
                project(i, 1)
                turn(i, 0)
                project(i + 1, 0)
                turn(i, 1)
            end = BLOCKS // 2 - 1
            project(end, 1)
            turn(end, 0)
            turn(end, 1)

        @block.scalar
        def _(act):
            act.wait_ge(consts_loaded, 16 * (2 * TAPS + 2))
            act.wait_ge(halo_zero, 2)
            with act.Fori(0, BLOCKS // 2) as i:
                for j in range(2):
                    b = 2 * i + j
                    act.wait_ge(proj_done, b + 1)
                    act.wait_ge(tap_done, TAPS * 2 * i)
                    nc.scalar.copy(pre[:, j, HALO:], proj[j][:]).then_inc(pre_done, 1)
                    act.wait_ge(tap_done, TAPS * (b + 1))
                    act.wait_ge(turn_done, 2 * i)
                    act.wait_ge(ch_stored[j], 16 * i)
                    nc.scalar.activation(post[:, j], mixed[:, j], ACT.Silu, bias=bias[:, bass.ds(b, 1)]).then_inc(silu_done, 1)
                    act.wait_ge(turn_done, b + 1)
                    act.wait_ge(tok_stored[j], 16 * i)
                    nc.scalar.copy(frames[:, j], turned[j][:]).then_inc(frames_done, 1)

        @block.vector
        def _(dve):
            nc.vector.memset(pre[:, :, 0:HALO], 0.0).then_inc(halo_zero, 1)
            nc.vector.memset(bias[:, SSD_BLOCKS:], 0.0).then_inc(halo_zero, 1)
            dve.wait_ge(halo_zero, 2)
            dve.wait_ge(consts_loaded, 16 * (2 * TAPS + 2))
            with dve.Fori(0, BLOCKS // 2) as i:
                for j in range(2):
                    b = 2 * i + j
                    dve.wait_ge(pre_done, b + 1)
                    dve.wait_ge(silu_done, 2 * i)
                    nc.vector.tensor_scalar(mixed[:, j], pre[:, j, 0:SEQ], taps[:, 0, bass.ds(b, 1)], None,
                                            ALU.mult).then_inc(tap_done, 1)
                    for tap in range(1, TAPS):
                        dve.wait_ge(tap_done, TAPS * b + tap)
                        nc.vector.scalar_tensor_tensor(out=mixed[:, j], in0=pre[:, j, tap:tap + SEQ],
                                                       scalar=taps[:, tap, bass.ds(b, 1)], in1=mixed[:, j],
                                                       op0=ALU.mult, op1=ALU.add).then_inc(tap_done, 1)


def gate_stage(nc, A, hn_T, zgs_scr):
    ctx, sb, ps, sem = scope(nc)
    with ctx:
        w_zgs = sb("w_zgs", [P, KD, ZGS])
        h_tile = sb("h_tile", [P, 2, KD, P])
        zgs = sb("zgs", [P, 2, ZGS])
        z_ps = [ps(f"z_ps{j}", [P, ZG]) for j in range(2)]
        small_ps = [ps(f"small_ps{j}", [P, SMALL]) for j in range(2)]
        w_loaded, tile_copied, proj_done = sem("w_zgs_loaded"), sem("tile_copied"), sem("zgs_proj_done")
        silu_done, small_done = sem("zg_silu_done"), sem("small_done")
        stored = [sem("zgs_stored_even"), sem("zgs_stored_odd")]
        w_in = A["w_in"].rearrange("l (k p) c -> p (l k) c", p=P)
        parts = ((0, 0, SSD_W), (SSD_W, COL_GATE, GDN_W), (ZG, COL_DT, SSD_H),
                 (ZG + SSD_H, COL_ALPHA, GDN_H), (ZG + HEADS, COL_BETA, GDN_H))
        out_rows = zgs_scr.rearrange("(i p) c -> i p c", p=P)
        block = ctx.enter_context(nc.Block())

        @block.sync
        def _(sp):
            with nc.allow_non_contiguous_dma(reason="the per-head columns are narrow"):
                for at, col, n in parts:
                    sp.dma_start(w_zgs[:, :, at:at + n], w_in[:, :, col:col + n]).then_inc(w_loaded, 16)
            with sp.Fori(0, TILES // 2) as i:
                for j in range(2):
                    sp.wait_ge(silu_done, 2 * i + j + 1)
                    sp.wait_ge(small_done, 2 * i + j + 1)
                    sp.dma_start(out_rows[bass.ds(2 * i + j, 1)].rearrange("o p c -> (o p) c"), zgs[:, j]).then_inc(stored[j], 16)
            for s in stored:
                sp.wait_ge(s, 16 * (TILES // 2))

        @block.vector
        def _(dve):
            with dve.Fori(0, TILES // 2) as i:
                for j in range(2):
                    dve.wait_ge(proj_done, 2 * i)
                    nc.vector.tensor_copy(h_tile[:, j], hn_T[:, :, bass.ds((2 * i + j) * P, P)]).then_inc(tile_copied, 1)
                for j in range(2):
                    dve.wait_ge(proj_done, 2 * i + j + 1)
                    dve.wait_ge(stored[j], 16 * i)
                    nc.vector.tensor_copy(zgs[:, j, ZG:], small_ps[j][:]).then_inc(small_done, 1)

        @block.scalar
        def _(act):
            with act.Fori(0, TILES // 2) as i:
                for j in range(2):
                    act.wait_ge(proj_done, 2 * i + j + 1)
                    act.wait_ge(stored[j], 16 * i)
                    nc.scalar.activation(zgs[:, j, 0:ZG], z_ps[j][:], ACT.Silu).then_inc(silu_done, 1)

        @block.tensor
        def _(pe):
            pe.wait_ge(w_loaded, 16 * len(parts))
            with pe.Fori(0, TILES // 2) as i:
                for j in range(2):
                    pe.wait_ge(tile_copied, 2 * i + j + 1)
                    pe.wait_ge(silu_done, 2 * i)
                    pe.wait_ge(small_done, 2 * i)
                    for out, at, n in ((z_ps[j][:, 0:BANK], 0, BANK), (z_ps[j][:, BANK:], BANK, BANK),
                                       (small_ps[j][:], ZG, SMALL)):
                        for k in range(KD):
                            last = nc.tensor.matmul(out, h_tile[:, j, k, :], w_zgs[:, k, at:at + n],
                                                    start=(k == 0), stop=(k == KD - 1))
                    last.then_inc(proj_done, 1)


def over_free(ap, n):
    return ap[:, :, None].broadcast_to([ap.shape[0], ap.shape[1], n])


def over_heads(ap, n):
    return ap[:, None, :].broadcast_to([ap.shape[0], n, ap.shape[1]])


def view(flat, *shape):
    names = "abc"[:len(shape)]
    return flat.rearrange(f"p ({' '.join(names)}) -> p {' '.join(names)}", **dict(zip(names[1:], shape[1:])))


ARENA = 11024


def tile_stage(nc, A, ch_scr, tok_scr, zgs_scr, out):
    ctx, sb, ps, sem = scope(nc)
    NL = len(LEVELS)
    with ctx:
        ident = sb("ident_m", [P, P])
        upper = sb("upper", [P, P])
        ones = sb("ones", [P, P])
        floor = sb("floor", [P, P])
        level = sb("level", [P, NL, P])
        rank = sb("rank", [P, CANDS])
        w_out = sb("w_out", [P, KD, D])
        w_q = sb("w_q", [P, KD, LISTS * P])
        keys_T = sb("keys_T", [P, 2, N_KEYS])
        w_rows = sb("w_rows", [2 * KD, P])
        w_mix = sb("w_mix", [P, KD])
        head_bias = sb("head_bias", [P, SMALL])
        neg_a = sb("neg_a", [P, HEADS])
        d_head = sb("d_head", [P, SSD_H])
        eps = sb("eps_m", [P, 1])
        S_gdn = sb("S_gdn", [P, GDN_H, P])
        S_ssd = sb("S_ssd", [P, SSD_H, SSD_P])
        x2 = sb("x2", [P, D])
        picks = sb("picks", [P, PICKS], U32)
        gates = sb("gates", [P, PEER_H, TOPK])
        gates_e = sb("gates_e", [P, PICKS])
        h2_e = sb("h2_e", [P, D])
        y = sb("y", [P, D])
        at_row = sb("at_row", [P, PICKS], U32)
        at_tail = sb("at_tail", [P, LAG], U32)
        ring = sb("ring", [P, SLOTS, D])
        dots = sb("dots", [P, PICKS])
        coef = sb("coef", [P, PICKS])
        diag = sb("diag", [P, 2, P])
        stat_e = sb("stat_e", [P, 3])
        small = sb("small", [P, SMALL])
        small_abs = sb("small_abs", [P, SMALL])
        small_exp = sb("small_exp", [P, SMALL])
        soft = sb("soft", [P, HEADS])
        rate = sb("rate", [P, HEADS])
        beta_den = sb("beta_den", [P, GDN_H])
        beta_num = sb("beta_num", [P, GDN_H])
        beta = sb("beta", [P, GDN_H])
        logs = sb("logs", [P, 3, HEADS])
        exps = sb("exps", [P, 3, HEADS])
        qk_ms = sb("qk_ms", [P, 2 * GDN_H])
        qk_log = sb("qk_log", [P, 2 * GDN_H])
        qk_r = sb("qk_r", [P, 2 * GDN_H])
        stat = sb("stat", [P, 8])
        r_gdn = sb("r_gdn", [P, 3, GDN_H])
        total = sb("total", [P, PEER_H])

        TOK = CONV_CH - SSD_G * P
        arena = sb("arena", [P, ARENA])
        place = [0]

        def take(*shape):
            n = 1
            for d in shape:
                n *= d
            at, place[0] = place[0], place[0] + n
            flat = arena[:, at:at + n]
            return flat if len(shape) == 1 else view(flat, *shape)

        tok = take(TOK)
        ch = take(CH_N, P)
        zgs = take(ZGS)
        decay = take(HEADS, P)
        decay_flat = arena[:, place[0] - HEADS * P:place[0]]
        G = take(SSD_H, P)
        G_flat = arena[:, place[0] - SSD_H * P:place[0]]
        k_beta, k_out, kT, kbT, A_T, qk = (take(GDN_H, P) for _ in range(6))
        Y = decay[:, SSD_H:]
        x_dt, x_end = take(SSD_H, SSD_P), take(SSD_H, SSD_P)
        qkv = tok[:, SSD_W + SSD_G * P:].rearrange("p (m h w) -> p m h w", m=3, h=GDN_H)
        k_in, k_hat, v_beta = qkv[:, 0], qkv[:, 1], qkv[:, 2]
        qk_sq = decay_flat[:, 0:2 * GDN_W]
        M_T = view(decay_flat[:, 0:2 * GDN_W], 2, GDN_H, P)
        mixT = view(decay_flat[:, 0:D], KD, P)
        mix = G_flat
        v_new, X, MX, wT, o_gdn = k_hat, k_beta, kT, kbT, A_T
        y_ssd, y_skip = x_dt, x_end
        place[0] = 0
        h_T = take(KD, P)
        h2 = arena[:, place[0]:place[0] + D]
        q, q_T = take(2, 4, P), take(2, 4, P)
        score, rest = take(LISTS, N_KEYS), take(LISTS, N_KEYS)
        best = take(LISTS, TOPK)
        best_at = take(LISTS, TOPK).bitcast(U32)
        best_key = take(LISTS, TOPK)
        cand, cand_rest, cand_id = (take(PEER_H, CANDS) for _ in range(3))
        top = take(PEER_H, TOPK)
        top_at = take(PEER_H, TOPK).bitcast(U32)
        top_rank, top_id, shifted, weight = (take(PEER_H, TOPK) for _ in range(4))
        HALF_H = PEER_H // 2
        assert place[0] <= ARENA
        place[0] = 0
        chosen = take(HALF_H, TOPK, CANDS)

        bank = ps("tile_psum", [P, 6, BANK])
        y_ps = ps("y_psum", [P, 2, BANK])

        def heads(b, n=GDN_H, w=P, at=0):
            return bank[:, b, at:at + n * w].rearrange("p (h w) -> p h w", h=n)

        square = lambda b, n=1: bank[:, b:b + n].rearrange("p b (k w) -> p (b k) w", w=P)

        s = {n: sem(n) for n in (
            "consts", "neg_a_exp", "eps_set_m", "setup_done", "keys_turned", "keys_copied",
            "mix_loaded", "x2_in", "small_in", "small_abs_done", "small_exp_done",
            "soft_log", "rate_ready", "beta_parts", "beta_ready", "soft_sum", "cums_ready", "logs_ready", "logs_copied", "exps_ready",
            "decay_log", "decay_ready", "qk_sq_ready", "qk_sum", "qk_logged", "qk_r_ready", "k_hat_ready", "k_beta_ready",
            "k_in_ready", "k_turned", "kT_copied", "pairs_ready", "A_ready", "qk_ready",
            "M_ready", "Y_ready", "X_turned", "X_ready", "MX_ready", "MX_copied", "steps_ready",
            "w_ready", "w_copied", "v_new_ready", "v_new_copied", "gdn_out", "o_part", "S_gdn_part", "S_gdn_ready",
            "o_sq_ready", "o_sum", "o_logged", "o_r_ready", "o_scaled", "mix_gdn",
            "G_ready", "x_dt_ready", "x_end_ready", "ssd_out", "y_part", "y_gated", "S_ssd_part", "S_ssd_ready",
            "y_mean", "y_logged", "y_r_ready", "mix_ssd", "mix_turned", "mixT_copied", "out_proj", "x2_ready",
            "x2_mean", "x2_logged", "x2_r_ready", "ffn_row_ready", "h2_ready",
            "h_turned", "hT_copied", "q_ready", "q_copied", "q_turned", "qT_copied", "score_ready", "score_copied",
            "best_hi", "best_hi_at", "rest_ready", "best_lo", "best_lo_at",
            "key_ready", "cand_ready", "id_ready", "top_hi", "top_hi_at", "cand_rest_ready", "top_lo", "top_lo_at",
            "top_rank_ready", "chosen_ready", "chosen_id", "top_id_ready", "picks_ready", "shifted_ready", "weight_ready",
            "total_ready", "total_inv", "gates_ready", "gates_copied", "held", "held_dve", "h2_copied",
            "at_ready", "tail_ready", "x2_copied", "gelu_ready", "coef_ready", "diag_ready", "y_ready", "res_mean", "res_logged", "res_r_ready",
            "final_row_ready", "out_ready", "out_stored")}
        filled = [sem(f"slot_filled{j}") for j in range(SLOTS)]
        used = [sem(f"slot_used{j}") for j in range(SLOTS)]

        rows = lambda t, i: t.rearrange("(i p) c -> i p c", p=P)[bass.ds(i, 1)].rearrange("o p c -> (o p) c")
        x_rows = A["x"].rearrange("b s d -> (b s) d")
        out_rows = out.rearrange("b s d -> (b s) d")
        ch_cols = ch_scr[CH_FIRST:CH_FIRST + CH_N].rearrange("b p t -> p b t")
        tables = {"U": A["peer_u"].rearrange("l e d -> (l e) d"), "V": A["peer_v"].rearrange("l e d -> (l e) d")}
        xs = tok[:, 0:SSD_W].rearrange("p (h w) -> p h w", h=SSD_H)
        B_T, C_T, q_ch = ch[:, 0:SSD_G], ch[:, SSD_G:2 * SSD_G], ch[:, 2 * SSD_G:]
        e_in, e_all, e_out = exps[:, 0], exps[:, 1], exps[:, 2]
        N_CONST = 18
        LOADS = 4

        def mode_of(e):
            return FULL if not isinstance(e, int) or 0 < e < TILES else LAST if e else FIRST

        def uses_before(j, e):
            return USES[j] * e - FEWER if mode_of(e) != FIRST else 0

        def slot_of(item, e):
            return ORDER[mode_of(e)][item] % SLOTS

        def turn_of(item, e):
            return uses_before(slot_of(item, e), e) + ORDER[mode_of(e)][item] // SLOTS + 1

        def after_use(eng, item, e):
            if item in ORDER[mode_of(e)]:
                j, turn = slot_of(item, e), turn_of(item, e)
            else:
                item = (item[0], item[1], 0)
                n, less = ORDER[FULL][item], len(ORDER[FULL]) - len(ORDER[FIRST])
                assert ORDER[FIRST][item] == n - less
                j = n % SLOTS
                turn = uses_before(j, e) - USES[j] + n // SLOTS + 1
            eng.wait_ge(used[j], turn + 1)

        def after_fill(eng, item, e):
            eng.wait_ge(filled[slot_of(item, e)], 16 * turn_of(item, e))

        def expert_share(e, do):
            done = [0, 0]

            def share(last=False):
                done[0] += 1
                assert done[0] <= SEGMENTS or last
                to = len(SEQUENCE) if last else SHARE_ENDS[done[0] - 1]
                if e is not None:
                    for item in SEQUENCE[done[1]:to]:
                        if item[2] in BACKS[mode_of(e)]:
                            do(item, e)
                done[1] = to

            return share

        def tile_loop(eng, body):
            body(0, None)
            body(1, 0)
            with eng.Fori(2, TILES) as i:
                body(i, i - 1)
            body(None, TILES - 1)
            body(None, TILES)

        block = ctx.enter_context(nc.Block())

        @block.sync
        def _(sp):
            head_row = lambda name, n: A[name][0:1, 0:n].broadcast_to([P, n])
            with nc.allow_non_contiguous_dma(reason="norm weights by channel"):
                for dst, src in ((ident[:], A["c_ident"]), (upper[:], A["c_upper"]), (ones[:], A["c_ones"]),
                                 (floor[:], A["c_floor"]), (level[:], A["c_level"]), (rank[:], A["c_rank"]),
                                 (w_rows[0:KD], A["norm_ffn_w"].rearrange("l (k p) -> (l k) p", p=P)),
                                 (w_rows[KD:], A["norm_final_w"].rearrange("(k p) -> k p", p=P)),
                                 (w_mix[:, 0:4], A["ssd_norm_w"].rearrange("l (k p) -> p (l k)", p=P)),
                                 (w_mix[:, 4:5], A["gdn_norm_w"].rearrange("l p -> p l")),
                                 (head_bias[:, 0:SSD_H], head_row("ssd_dt_bias", SSD_H)),
                                 (head_bias[:, SSD_H:HEADS], head_row("gdn_dt_bias", GDN_H)),
                                 (neg_a[:, 0:SSD_H], head_row("ssd_a_log", SSD_H)),
                                 (neg_a[:, SSD_H:], head_row("gdn_a_log", GDN_H)),
                                 (d_head[:], head_row("ssd_d", SSD_H)),
                                 (w_out[:], A["w_out"].rearrange("l (k p) d -> p (l k) d", p=P)),
                                 (view(arena[:, 0:2 * P], 2, P), A["peer_sub_keys"].rearrange("l two k d -> k (l two) d")),
                                 (w_q[:], A["peer_w_q"].rearrange("l (k p) c -> p (l k) c", p=P))):
                    sp.dma_start(dst, src).then_inc(s["consts"], 16)

            def body(m, e):
                if m is not None:
                    if e is None:
                        sp.wait_ge(s["keys_turned"], 1)
                    else:
                        sp.wait_ge(s["picks_ready"], m)
                        sp.wait_ge(s["gates_ready"], m)
                    sp.dma_start(tok[:, 0:TOK_B + SSD_G * P], rows(tok_scr, m)[:, 0:TOK_B + SSD_G * P]).then_inc(s["mix_loaded"], 16)
                    sp.dma_start(tok[:, TOK_B + SSD_G * P:], rows(tok_scr, m)[:, TOK_Q:]).then_inc(s["mix_loaded"], 16)
                    sp.dma_start(ch, ch_cols[:, :, bass.ds(m * P, P)]).then_inc(s["mix_loaded"], 16)
                    sp.dma_start(zgs, rows(zgs_scr, m)).then_inc(s["mix_loaded"], 16)
                    if e is not None:
                        sp.wait_ge(s["x2_copied"], e + 1)
                    sp.dma_start(x2[:], rows(x_rows, m)).then_inc(s["x2_in"], 16)

            tile_loop(sp, body)

        @block.gpsimd
        def _(pool):
            def body(m, e):
                if e is None:
                    return
                mode = mode_of(e)
                if mode != FIRST:
                    nc.gpsimd.tensor_copy(at_tail[:], at_row[:, TAIL:]).then_inc(s["tail_ready"], 1)
                    pool.wait_ge(s["tail_ready"], e)
                if mode != LAST:
                    pool.wait_ge(s["picks_ready"], e + 1)
                    pool.sem_inc(s["held"])
                    nc.gpsimd.tensor_copy(at_row[:], picks[:]).then_inc(s["at_ready"], 1)
                    pool.wait_ge(s["at_ready"], e + 1)
                for item in gathers(mode):
                    kind, n, back = item
                    j = slot_of(item, e)
                    at = at_tail[:, n - TAIL:n - TAIL + 1] if back else at_row[:, n:n + 1]
                    pool.wait_ge(used[j], turn_of(item, e))
                    pool.sem_inc(s["held"])
                    pool.indirect_dma_start(ring[:, j], None, tables[kind],
                                            bass.IndirectOffsetOnAxis(ap=at, axis=0)).then_inc(filled[j], 16)
                for j in range(SLOTS):
                    turns = len(range(j, len(gathers(mode)), SLOTS))
                    pool.wait_ge(filled[j], 16 * (uses_before(j, e) + turns))

            tile_loop(pool, body)

        @block.tensor
        def _(pe):
            def do(item, e):
                kind, n, back = item
                if kind == "F":
                    pe.wait_ge(s["res_mean"], e)
                    row_of(1, (y_ps[:, 0], y_ps[:, 1])).then_inc(s["final_row_ready"], 1)
                if kind != "V" or n not in PE_PICKS:
                    return
                k = PE_PICKS.index(n)
                if k == 0 and mode_of(e) != FIRST:
                    pe.wait_ge(s["out_ready"], e - back)
                pe.wait_ge(s["diag_ready"], len(PE_PICKS) * (e - back) + k + 1)
                after_fill(pe, item, e)
                for half in range(2):
                    last = nc.tensor.matmul(y_ps[:, half], diag[:, k % 2], ring[:, slot_of(item, e), half * BANK:(half + 1) * BANK],
                                            start=(k == 0), stop=(n == PE_PICKS[-1]))
                last.then_inc(used[slot_of(item, e)], 1)

            def row_of(r, out):
                for k in range(KD):
                    row = KD * r + k
                    last = nc.tensor.matmul(out[k // 4][:, k % 4 * P:(k % 4 + 1) * P],
                                            ident[0:2 * KD, row:row + 1].broadcast_to([2 * KD, P]),
                                            w_rows[:], start=True, stop=True)
                return last

            def steps(m, share):
                pe.wait_ge(s["mix_loaded"], 16 * LOADS * (m + 1))
                if not isinstance(m, int) or m:
                    pe.wait_ge(s["h2_copied"], m)
                for g in range(SSD_G):
                    nc.tensor.matmul(heads(0, 2, P, 256)[:, g], B_T[:, g], C_T[:, g], start=True, stop=True)
                share()
                pe.wait_ge(s["rate_ready"], m + 1)
                nc.tensor.matmul(bank[:, 0, 0:HEADS], upper[:], rate[:], start=True, stop=True)
                nc.tensor.matmul(bank[:, 0, HEADS:2 * HEADS], ones[:], rate[:], start=True, stop=True)
                for h in range(HEADS):
                    last = nc.tensor.matmul(heads(1 + h // 4)[:, h % 4], rate[:, h:h + 1].broadcast_to([P, P]), upper[:],
                                            start=True, stop=True)
                last.then_inc(s["cums_ready"], 1)
                share()
                share()
                pe.wait_ge(s["k_hat_ready"], m + 1)
                pe.wait_ge(s["k_beta_ready"], m + 1)
                for h in range(GDN_H):
                    nc.tensor.transpose(heads(4)[:, h], k_hat[:, h], ident[:])
                    last = nc.tensor.transpose(heads(5)[:, h], k_beta[:, h], ident[:])
                last.then_inc(s["k_turned"], 1)
                share()
                pe.wait_ge(s["kT_copied"], 2 * (m + 1))
                pe.wait_ge(s["decay_log"], m + 1)
                for h in range(GDN_H):
                    nc.tensor.matmul(heads(1)[:, h], kT[:, h], kbT[:, h], start=True, stop=True)
                    last = nc.tensor.matmul(heads(2)[:, h], kT[:, h], q_ch[:, h], start=True, stop=True)
                last.then_inc(s["pairs_ready"], 1)
                for _ in range(3):
                    share()
                pe.wait_ge(s["G_ready"], m + 1)
                pe.wait_ge(s["x_end_ready"], m + 1)
                pe.wait_ge(s["A_ready"], m + 1)
                for h in range(SSD_H):
                    nc.tensor.matmul(heads(4, SSD_H, SSD_P)[:, h], G[:, h], x_dt[:, h], start=True, stop=True)
                for g in range(SSD_G):
                    half = slice(g * SSD_R * SSD_P, (g + 1) * SSD_R * SSD_P)
                    group = slice(g * SSD_R, (g + 1) * SSD_R)
                    nc.tensor.matmul(bank[:, 5, half], C_T[:, g], S_ssd[:, group].rearrange("p h w -> p (h w)"),
                                     start=True, stop=True)
                    last = nc.tensor.matmul(bank[:, 1, half], tok[:, TOK_B + g * P:TOK_B + (g + 1) * P],
                                            x_end[:, group].rearrange("p h w -> p (h w)"), start=True, stop=True)
                last.then_inc(s["ssd_out"], 1)
                share()
                pe.wait_ge(s["Y_ready"], NL * m + 1)
                for h in range(GDN_H):
                    last = nc.tensor.transpose(heads(3)[:, h], Y[:, h], ident[:])
                last.then_inc(s["X_turned"], 1)
                share()
                pe.wait_ge(s["qk_ready"], m + 1)
                for n in range(1, NL):
                    pe.wait_ge(s["M_ready"], NL * m + n + 1)
                    pe.wait_ge(s["X_ready"], (NL - 1) * m + n)
                    for h in range(GDN_H):
                        last = nc.tensor.matmul(heads(0)[:, h], M_T[:, n % 2, h], X[:, h], start=True, stop=True)
                    last.then_inc(s["MX_ready"], 1)
                    pe.wait_ge(s["MX_copied"], (NL - 1) * m + n)
                    pe.wait_ge(s["Y_ready"], NL * m + n)
                    for h in range(GDN_H):
                        if n < NL - 1:
                            nc.tensor.matmul(heads(2)[:, h], Y[:, h], MX[:, h], start=True, stop=True)
                        last = nc.tensor.matmul(heads(3)[:, h], MX[:, h], Y[:, h], start=True, stop=True)
                    last.then_inc(s["steps_ready"], 1)
                    share()
                pe.wait_ge(s["Y_ready"], NL * (m + 1))
                for h in range(GDN_H):
                    last = nc.tensor.matmul(heads(0)[:, h], k_in[:, h], Y[:, h], start=True, stop=True)
                last.then_inc(s["w_ready"], 1)
                pe.wait_ge(s["w_copied"], m + 1)
                for h in range(GDN_H):
                    nc.tensor.matmul(heads(2)[:, h], Y[:, h], v_beta[:, h], start=True, stop=False)
                    last = nc.tensor.matmul(heads(2)[:, h], wT[:, h], S_gdn[:, h], start=False, stop=True)
                last.then_inc(s["v_new_ready"], 1)
                share()
                pe.wait_ge(s["y_part"], 2 * (m + 1))
                pe.wait_ge(s["v_new_copied"], m + 1)
                for h in range(GDN_H):
                    nc.tensor.matmul(heads(3)[:, h], q_ch[:, h], S_gdn[:, h], start=True, stop=True)
                    nc.tensor.matmul(heads(4)[:, h], qk[:, h], v_new[:, h], start=True, stop=True)
                    last = nc.tensor.matmul(heads(5)[:, h], k_out[:, h], v_new[:, h], start=True, stop=True)
                last.then_inc(s["gdn_out"], 1)
                for _ in range(4):
                    share()
                pe.wait_ge(s["mix_ssd"], m + 1)
                pe.wait_ge(s["mix_gdn"], m + 1)
                pe.wait_ge(s["S_ssd_ready"], m + 1)
                for k in range(KD):
                    last = nc.tensor.transpose(heads(k // 4)[:, k % 4], mix[:, k * P:(k + 1) * P], ident[:])
                last.then_inc(s["mix_turned"], 1)
                share()
                pe.wait_ge(s["mixT_copied"], m + 1)
                for half in range(D // BANK):
                    for k in range(KD):
                        last = nc.tensor.matmul(bank[:, 2 + half], mixT[:, k], w_out[:, k, half * BANK:(half + 1) * BANK],
                                                start=(k == 0), stop=(k == KD - 1))
                        if k % 4 == 3:
                            if half and k == KD - 1:
                                last.then_inc(s["out_proj"], 1)
                            share()
                row_of(0, (bank[:, 0], bank[:, 1])).then_inc(s["ffn_row_ready"], 1)
                share()
                share()
                pe.wait_ge(s["h2_ready"], m + 1)
                pe.wait_ge(s["S_gdn_ready"], m + 1)
                for k in range(KD):
                    last = nc.tensor.transpose(square(4, 2)[:, k], h2[:, k * P:(k + 1) * P], ident[:])
                last.then_inc(s["h_turned"], 1)
                share()
                pe.wait_ge(s["hT_copied"], m + 1)
                for b in range(4):
                    for k in range(KD):
                        last = nc.tensor.matmul(bank[:, b], h_T[:, k], w_q[:, k, b * BANK:(b + 1) * BANK],
                                                start=(k == 0), stop=(k == KD - 1))
                        if k == KD - 1:
                            last.then_inc(s["q_ready"], 1)
                        if k % 4 == 3:
                            share()
                for b in range(4):
                    pe.wait_ge(s["q_copied"], 4 * m + b + 1)
                    if b >= 2:
                        pe.wait_ge(s["qT_copied"], 4 * m + b - 1)
                    for n in range(4):
                        last = nc.tensor.transpose(square(4 + b % 2)[:, n], q[:, b % 2, n], ident[:])
                    last.then_inc(s["q_turned"], 1)
                    pe.wait_ge(s["qT_copied"], 4 * m + b + 1)
                    for n in range(4):
                        last = nc.tensor.matmul(square(b)[:, n], q_T[:, b % 2, n], keys_T[:, n % 2], start=True, stop=True)
                    last.then_inc(s["score_ready"], 1)
                    if b == 3:
                        pe.wait_ge(s["score_copied"], m + 1)
                        row_of(0, (bank[:, 0], bank[:, 1])).then_inc(s["ffn_row_ready"], 1)
                    share()

            pe.wait_ge(s["consts"], 16 * N_CONST)
            for half in range(2):
                last = nc.tensor.transpose(bank[:, 0, half * P:(half + 1) * P], arena[:, half * P:(half + 1) * P], ident[:])
            last.then_inc(s["keys_turned"], 1)
            pe.wait_ge(s["keys_copied"], 1)

            def body(m, e):
                share = expert_share(e, do)
                if m is not None:
                    steps(m, share)
                share(last=True)

            tile_loop(pe, body)

        @block.scalar
        def _(act):
            def do(item, e):
                kind, n, back = item
                if kind == "G":
                    after_use(act, ("U", (n + 1) * GROUP - 1, 0), e)
                    group = slice(n * GROUP, (n + 1) * GROUP)
                    nc.scalar.activation(coef[:, group], dots[:, group], ACT.Gelu).then_inc(s["gelu_ready"], 1)
                    nc.scalar.preload_act_table_set(LOG_EXP_SET)
                if kind == "V" and n in PE_PICKS:
                    k = PE_PICKS.index(n)
                    act.wait_ge(s["coef_ready"], PICKS // GROUP * (e - back) + n // GROUP + 1)
                    if k >= 2:
                        after_use(act, ("V", PE_PICKS[k - 2], back), e)
                    nc.scalar.activation(diag[:, k % 2], ident[:], ACT.Copy, scale=coef[:, n:n + 1]).then_inc(s["diag_ready"], 1)
                if kind == "F":
                    act.wait_ge(s["y_ready"], e)
                    nc.scalar.activation(y_ps[:].rearrange("p b w -> p (b w)"), y[:], ACT.Square, scale=D ** -0.5,
                                         accum_out=stat_e[:, 0:1]).then_inc(s["res_mean"], 1)
                    act.wait_ge(s["res_mean"], e)
                    nc.scalar.activation(stat_e[:, 1:2], stat_e[:, 0:1], ACT.Ln, bias=eps[:]).then_inc(s["res_logged"], 1)
                    act.wait_ge(s["res_logged"], e)
                    nc.scalar.activation(stat_e[:, 2:3], stat_e[:, 1:2], ACT.Exp, scale=-0.5).then_inc(s["res_r_ready"], 1)
                if kind == "O":
                    act.wait_ge(s["out_ready"], e)
                    act.dma_start(rows(out_rows, e - 1), y[:]).then_inc(s["out_stored"], 16)

            def steps(m, share):
                act.wait_ge(s["small_in"], m + 1)
                nc.scalar.activation(small_abs[:], small[:], ACT.Abs).then_inc(s["small_abs_done"], 1)
                act.wait_ge(s["small_abs_done"], m + 1)
                nc.scalar.activation(small_exp[:], small_abs[:], ACT.Exp, scale=-1.0).then_inc(s["small_exp_done"], 1)
                act.wait_ge(s["small_exp_done"], m + 1)
                nc.scalar.activation(soft[:], small_exp[:, 0:HEADS], ACT.Ln, bias=1.0).then_inc(s["soft_log"], 1)
                nc.scalar.activation(qk_sq, tok[:, SSD_W + SSD_G * P:TOK - GDN_W], ACT.Square).then_inc(s["qk_sq_ready"], 1)
                share()
                act.wait_ge(s["qk_sum"], m + 1)
                nc.scalar.activation(qk_log[:], qk_ms[:], ACT.Ln, bias=eps[:]).then_inc(s["qk_logged"], 1)
                act.wait_ge(s["qk_logged"], m + 1)
                nc.scalar.activation(qk_r[:], qk_log[:], ACT.Exp, scale=-0.5).then_inc(s["qk_r_ready"], 1)
                share()
                act.wait_ge(s["logs_ready"], 2 * (m + 1))
                nc.scalar.activation(exps[:], logs[:], ACT.Exp).then_inc(s["exps_ready"], 1)
                act.wait_ge(s["decay_log"], m + 1)
                nc.scalar.activation(decay, decay, ACT.Exp).then_inc(s["decay_ready"], 1)
                share()
                act.wait_ge(s["k_turned"], m + 1)
                nc.scalar.copy(kT, heads(4)).then_inc(s["kT_copied"], 1)
                nc.scalar.copy(kbT, heads(5)).then_inc(s["kT_copied"], 1)
                for _ in range(5):
                    share()
                act.wait_ge(s["X_turned"], m + 1)
                act.wait_ge(s["k_in_ready"], m + 1)
                nc.scalar.copy(X, heads(3)).then_inc(s["X_ready"], 1)
                share()
                for n in range(1, NL):
                    act.wait_ge(s["MX_ready"], (NL - 1) * m + n)
                    nc.scalar.copy(MX, heads(0)).then_inc(s["MX_copied"], 1)
                    share()
                act.wait_ge(s["w_ready"], m + 1)
                nc.scalar.mul(wT, heads(0), -1.0).then_inc(s["w_copied"], 1)
                act.wait_ge(s["v_new_ready"], m + 1)
                nc.scalar.copy(v_new, heads(2)).then_inc(s["v_new_copied"], 1)
                share()
                share()
                act.wait_ge(s["y_gated"], m + 1)
                nc.scalar.activation(y_skip, y_ssd, ACT.Square, scale=SSD_W ** -0.5, accum_out=stat[:, 0:1]).then_inc(s["y_mean"], 1)
                act.wait_ge(s["y_mean"], m + 1)
                nc.scalar.activation(stat[:, 1:2], stat[:, 0:1], ACT.Ln, bias=eps[:]).then_inc(s["y_logged"], 1)
                act.wait_ge(s["y_logged"], m + 1)
                nc.scalar.activation(stat[:, 2:3], stat[:, 1:2], ACT.Exp, scale=-0.5).then_inc(s["y_r_ready"], 1)
                share()
                act.wait_ge(s["o_part"], 3 * (m + 1))
                nc.scalar.activation(view(qk_sq[:, 0:GDN_W], GDN_H, P), o_gdn, ACT.Square, scale=P ** -0.5).then_inc(s["o_sq_ready"], 1)
                share()
                act.wait_ge(s["o_sum"], m + 1)
                nc.scalar.activation(r_gdn[:, 1], r_gdn[:, 0], ACT.Ln, bias=eps[:]).then_inc(s["o_logged"], 1)
                act.wait_ge(s["o_logged"], m + 1)
                nc.scalar.activation(r_gdn[:, 2], r_gdn[:, 1], ACT.Exp, scale=-0.5).then_inc(s["o_r_ready"], 1)
                share()
                act.wait_ge(s["mix_turned"], m + 1)
                nc.scalar.copy(mixT, square(0, 2)).then_inc(s["mixT_copied"], 1)
                for _ in range(6):
                    share()
                act.wait_ge(s["x2_ready"], m + 1)
                nc.scalar.activation(mix, x2[:], ACT.Square, scale=D ** -0.5, accum_out=stat[:, 3:4]).then_inc(s["x2_mean"], 1)
                act.wait_ge(s["x2_mean"], m + 1)
                nc.scalar.activation(stat[:, 4:5], stat[:, 3:4], ACT.Ln, bias=eps[:]).then_inc(s["x2_logged"], 1)
                act.wait_ge(s["x2_logged"], m + 1)
                nc.scalar.activation(stat[:, 5:6], stat[:, 4:5], ACT.Exp, scale=-0.5).then_inc(s["x2_r_ready"], 1)
                share()
                act.wait_ge(s["h_turned"], m + 1)
                nc.scalar.copy(h_T, square(4, 2)).then_inc(s["hT_copied"], 1)
                share()
                for b in range(4):
                    share()
                    act.wait_ge(s["q_ready"], 4 * m + b + 1)
                    if b < 2:
                        nc.scalar.copy(q[:, b], square(b)).then_inc(s["q_copied"], 1)
                    share()
                for b in range(4):
                    act.wait_ge(s["q_turned"], 4 * m + b + 1)
                    nc.scalar.copy(q_T[:, b % 2], square(4 + b % 2)).then_inc(s["qT_copied"], 1)
                    if b < 2:
                        nc.scalar.copy(q[:, b], square(2 + b)).then_inc(s["q_copied"], 1)
                    if b < 3:
                        share()
                act.wait_ge(s["score_ready"], 4 * (m + 1))
                nc.scalar.copy(score, square(0, 4)).then_inc(s["score_copied"], 1)
                share()
                for _ in range(16):
                    share()
                act.wait_ge(s["shifted_ready"], m + 1)
                nc.scalar.activation(weight, shifted, ACT.Exp).then_inc(s["weight_ready"], 1)

            nc.scalar.preload_act_table_set(LOG_EXP_SET)
            act.wait_ge(s["consts"], 16 * N_CONST)
            act.wait_ge(s["eps_set_m"], 1)
            nc.scalar.activation(neg_a[:], neg_a[:], ACT.Exp).then_inc(s["neg_a_exp"], 1)
            act.wait_ge(s["keys_turned"], 1)
            nc.scalar.copy(keys_T[:], bank[:, 0, 0:2 * P].rearrange("p (n k) -> p n k", n=2)).then_inc(s["keys_copied"], 1)

            def body(m, e):
                share = expert_share(e, do)
                if m is not None:
                    steps(m, share)
                share(last=True)

            tile_loop(act, body)
            act.wait_ge(s["out_stored"], 16 * TILES + 1)

        @block.vector
        def _(dve):
            tt, ts, stt = nc.vector.tensor_tensor, nc.vector.tensor_scalar, nc.vector.scalar_tensor_tensor

            def do(item, e):
                kind, n, back = item
                if kind == "U":
                    if n == 0:
                        dve.wait_ge(s["h2_copied"], e + 1)
                    after_fill(dve, item, e)
                    j = slot_of(item, e)
                    nc.vector.tensor_tensor_reduce(out=ring[:, j], in0=ring[:, j], in1=h2_e[:], scale=1.0, scalar=0.0,
                                                   op0=ALU.mult, op1=ALU.add, accum_out=dots[:, n:n + 1]).then_inc(used[j], 1)
                if kind == "K":
                    dve.wait_ge(s["gates_ready"], e + 1)
                    nc.vector.tensor_copy(gates_e[:], gates[:].rearrange("p h k -> p (h k)")).then_inc(s["gates_copied"], 1)
                if kind == "C":
                    group = slice(n * GROUP, (n + 1) * GROUP)
                    dve.wait_ge(s["gates_copied"], e - back + 1)
                    dve.wait_ge(s["gelu_ready"], PICKS // GROUP * (e - back) + n + 1)
                    tt(coef[:, group], coef[:, group], gates_e[:, group], ALU.mult).then_inc(s["coef_ready"], 1)
                if kind == "X":
                    dve.wait_ge(s["out_stored"], 16 * e + 1)
                    nc.vector.tensor_copy(y[:], x2[:]).then_inc(s["x2_copied"], 1)
                if kind == "V" and n in DVE_PICKS:
                    k = DVE_PICKS.index(n)
                    dve.wait_ge(s["coef_ready"], PICKS // GROUP * (e - back) + n // GROUP + 1)
                    if k == 0:
                        dve.wait_ge(s["x2_copied"], e - back + 1)
                    else:
                        after_use(dve, ("V", DVE_PICKS[k - 1], back), e)
                    after_fill(dve, item, e)
                    j = slot_of(item, e)
                    stt(out=y[:], in0=ring[:, j], scalar=coef[:, n:n + 1], in1=y[:],
                        op0=ALU.mult, op1=ALU.add).then_inc(used[j], 1)
                if kind == "F":
                    after_use(dve, ("V", PE_PICKS[-1], 1), e)
                    after_use(dve, ("V", DVE_PICKS[-1], 1), e)
                    tt(y[:], y[:], y_ps[:].rearrange("p b w -> p (b w)"), ALU.add).then_inc(s["y_ready"], 1)
                if kind == "O":
                    dve.wait_ge(s["res_r_ready"], e)
                    dve.wait_ge(s["final_row_ready"], e)
                    stt(out=y[:], in0=y[:], scalar=stat_e[:, 2:3], in1=y_ps[:].rearrange("p b w -> p (b w)"),
                        op0=ALU.mult, op1=ALU.mult).then_inc(s["out_ready"], 1)

            def top16(m, n, src, low, value, where, hi, hi_at, low_ready, lo, lo_at, share):
                def lists(op, last_sem):
                    for t in range(n):
                        last = op(t)
                        if t % 8 == 7:
                            if t == n - 1:
                                last.then_inc(s[last_sem], 1)
                            share()

                lists(lambda t: nc.vector.max(value[:, t, 0:8], src[:, t]), hi)
                dve.wait_ge(s[hi], m + 1)
                dve.sem_inc(s["held_dve"])
                lists(lambda t: nc.vector.match_replace(low[:, t], value[:, t, 0:8], src[:, t], -3e38), low_ready)
                lists(lambda t: nc.vector.max_index(where[:, t, 0:8], value[:, t, 0:8], src[:, t]), hi_at)
                dve.wait_ge(s[low_ready], m + 1)
                dve.sem_inc(s["held_dve"])
                lists(lambda t: nc.vector.max(value[:, t, 8:16], low[:, t]), lo)
                dve.wait_ge(s[lo], m + 1)
                dve.sem_inc(s["held_dve"])
                lists(lambda t: nc.vector.max_index(where[:, t, 8:16], value[:, t, 8:16], low[:, t]), lo_at)
                dve.wait_ge(s[hi_at], m + 1)
                dve.wait_ge(s[lo_at], m + 1)

            def steps(m, share):
                dve.wait_ge(s["mix_loaded"], 16 * LOADS * (m + 1))
                tt(small[:], zgs[:, ZG:], head_bias[:], ALU.add).then_inc(s["small_in"], 1)
                share()
                dve.wait_ge(s["soft_log"], m + 1)
                stt(out=soft[:], in0=small[:, 0:HEADS], scalar=0.0, in1=soft[:], op0=ALU.max, op1=ALU.add).then_inc(s["soft_sum"], 1)
                dve.wait_ge(s["soft_sum"], m + 1)
                tt(rate[:], soft[:], neg_a[:], ALU.mult).then_inc(s["rate_ready"], 1)
                b_exp = small_exp[:, HEADS:]
                ts(beta_den[:], b_exp, 1.0, None, ALU.add).then_inc(s["beta_parts"], 1)
                stt(out=beta_num[:], in0=small[:, HEADS:], scalar=0.0, in1=b_exp, op0=ALU.is_ge, op1=ALU.max).then_inc(s["beta_parts"], 1)
                dve.wait_ge(s["beta_parts"], 3 * m + 2)
                nc.vector.reciprocal(beta_den[:], beta_den[:]).then_inc(s["beta_parts"], 1)
                dve.wait_ge(s["beta_parts"], 3 * (m + 1))
                tt(beta[:], beta_num[:], beta_den[:], ALU.mult).then_inc(s["beta_ready"], 1)
                dve.wait_ge(s["qk_sq_ready"], m + 1)
                nc.vector.tensor_reduce(qk_ms[:], view(qk_sq, 2 * GDN_H, P), AX_X, ALU.add).then_inc(s["qk_sum"], 1)
                share()
                dve.wait_ge(s["cums_ready"], m + 1)
                nc.vector.tensor_copy(logs[:, 0:2], heads(0, 2, HEADS)).then_inc(s["logs_copied"], 1)
                dve.wait_ge(s["logs_copied"], m + 1)
                tt(logs[:, 2], logs[:, 1], logs[:, 0], ALU.subtract).then_inc(s["logs_ready"], 2)
                dve.wait_ge(s["qk_sum"], m + 1)
                for h in range(HEADS):
                    last = stt(out=decay[:, h], in0=heads(1 + h // 4)[:, h % 4], scalar=logs[:, 0, h:h + 1], in1=floor[:],
                               op0=ALU.subtract, op1=ALU.min)
                last.then_inc(s["decay_log"], 1)
                share()
                dve.wait_ge(s["qk_r_ready"], m + 1)
                tt(k_hat, qkv[:, 1], over_free(qk_r[:, GDN_H:], P), ALU.mult).then_inc(s["k_hat_ready"], 1)
                dve.wait_ge(s["k_hat_ready"], m + 1)
                dve.wait_ge(s["beta_ready"], m + 1)
                tt(k_beta, k_hat, over_free(beta[:], P), ALU.mult).then_inc(s["k_beta_ready"], 1)
                share()
                tt(v_beta, qkv[:, 2], over_free(beta[:], P), ALU.mult)
                dve.wait_ge(s["exps_ready"], m + 1)
                tt(k_out, k_hat, over_free(e_out[:, SSD_H:], P), ALU.mult)
                dve.wait_ge(s["k_beta_ready"], m + 1)
                tt(k_in, k_beta, over_free(e_in[:, SSD_H:], P), ALU.mult).then_inc(s["k_in_ready"], 1)
                share()
                tt(x_dt, xs, over_free(soft[:, 0:SSD_H], SSD_P), ALU.mult).then_inc(s["x_dt_ready"], 1)
                dve.wait_ge(s["x_dt_ready"], m + 1)
                tt(x_end, x_dt, over_free(e_out[:, 0:SSD_H], SSD_P), ALU.mult).then_inc(s["x_end_ready"], 1)
                share()
                dve.wait_ge(s["decay_ready"], m + 1)
                for g in range(SSD_G):
                    group = slice(g * SSD_R, (g + 1) * SSD_R)
                    last = tt(G[:, group], over_heads(heads(0, 2, P, 256)[:, g], SSD_R), decay[:, group], ALU.mult)
                last.then_inc(s["G_ready"], 1)
                share()
                dve.wait_ge(s["pairs_ready"], m + 1)
                tt(A_T, heads(1), decay[:, SSD_H:], ALU.mult).then_inc(s["A_ready"], 1)
                tt(qk, heads(2), decay[:, SSD_H:], ALU.mult).then_inc(s["qk_ready"], 1)
                share()
                dve.wait_ge(s["A_ready"], m + 1)
                dve.wait_ge(s["G_ready"], m + 1)
                tt(M_T[:, 0], A_T, over_heads(level[:, 0], GDN_H), ALU.mult).then_inc(s["M_ready"], 1)
                dve.wait_ge(s["M_ready"], NL * m + 1)
                dve.wait_ge(s["qk_ready"], m + 1)
                tt(Y, over_heads(ident[:], GDN_H), M_T[:, 0], ALU.subtract).then_inc(s["Y_ready"], 1)
                tt(M_T[:, 1], A_T, over_heads(level[:, 1], GDN_H), ALU.mult).then_inc(s["M_ready"], 1)
                share()
                for n in range(1, NL):
                    if n > 1:
                        dve.wait_ge(s["steps_ready"], (NL - 1) * m + n - 1)
                        tt(X, X, heads(2), ALU.subtract).then_inc(s["X_ready"], 1)
                        tt(Y, Y, heads(3), ALU.subtract).then_inc(s["Y_ready"], 1)
                    if n + 1 < NL:
                        dve.wait_ge(s["Y_ready"], NL * m + n)
                        tt(M_T[:, (n + 1) % 2], A_T, over_heads(level[:, n + 1], GDN_H), ALU.mult).then_inc(s["M_ready"], 1)
                    share()
                dve.wait_ge(s["steps_ready"], (NL - 1) * (m + 1))
                tt(Y, Y, heads(3), ALU.subtract).then_inc(s["Y_ready"], 1)
                dve.wait_ge(s["ssd_out"], m + 1)
                tt(y_ssd, heads(5, SSD_H, SSD_P), over_free(e_in[:, 0:SSD_H], SSD_P), ALU.mult).then_inc(s["y_part"], 1)
                tt(y_skip, xs, over_free(d_head[:], SSD_P), ALU.mult)
                dve.wait_ge(s["y_part"], 2 * m + 1)
                tt(y_ssd, y_ssd, heads(4, SSD_H, SSD_P), ALU.add).then_inc(s["y_part"], 1)
                dve.wait_ge(s["y_part"], 2 * (m + 1))
                tt(y_ssd, y_ssd, y_skip, ALU.add).then_inc(s["S_ssd_part"], 1)
                share()
                dve.wait_ge(s["S_ssd_part"], 2 * m + 1)
                tt(y_ssd, y_ssd, view(zgs[:, 0:SSD_W], SSD_H, SSD_P), ALU.mult).then_inc(s["y_gated"], 1)
                tt(S_ssd[:], S_ssd[:], over_free(e_all[:, 0:SSD_H], SSD_P), ALU.mult).then_inc(s["S_ssd_part"], 1)
                dve.wait_ge(s["S_ssd_part"], 2 * (m + 1))
                tt(S_ssd[:], S_ssd[:], heads(1, SSD_H, SSD_P), ALU.add).then_inc(s["S_ssd_ready"], 1)
                share()
                dve.wait_ge(s["gdn_out"], m + 1)
                tt(o_gdn, heads(3), over_free(e_in[:, SSD_H:], P), ALU.mult).then_inc(s["o_part"], 1)
                dve.wait_ge(s["o_part"], 3 * m + 1)
                tt(o_gdn, o_gdn, heads(4), ALU.add).then_inc(s["o_part"], 1)
                tt(S_gdn[:], S_gdn[:], over_free(e_all[:, SSD_H:], P), ALU.mult).then_inc(s["S_gdn_part"], 1)
                share()
                dve.wait_ge(s["o_part"], 3 * m + 2)
                stt(out=o_gdn, in0=o_gdn, scalar=P ** -0.5, in1=over_free(qk_r[:, 0:GDN_H], P),
                    op0=ALU.mult, op1=ALU.mult).then_inc(s["o_part"], 1)
                dve.wait_ge(s["S_gdn_part"], m + 1)
                tt(S_gdn[:], S_gdn[:], heads(5), ALU.add).then_inc(s["S_gdn_ready"], 1)
                share()
                dve.wait_ge(s["y_r_ready"], m + 1)
                ts(mix[:, 0:SSD_W], y_ssd.rearrange("p h w -> p (h w)"), stat[:, 2:3], None, ALU.mult).then_inc(s["mix_ssd"], 1)
                dve.wait_ge(s["o_sq_ready"], m + 1)
                nc.vector.tensor_reduce(r_gdn[:, 0], view(qk_sq[:, 0:GDN_W], GDN_H, P), AX_X, ALU.add).then_inc(s["o_sum"], 1)
                share()
                dve.wait_ge(s["o_r_ready"], m + 1)
                tt(o_gdn, o_gdn, over_free(r_gdn[:, 2], P), ALU.mult).then_inc(s["o_scaled"], 1)
                dve.wait_ge(s["o_scaled"], m + 1)
                tt(view(mix[:, SSD_W:], GDN_H, P), o_gdn, view(zgs[:, SSD_W:ZG], GDN_H, P), ALU.mult).then_inc(s["mix_gdn"], 1)
                share()
                for _ in range(5):
                    share()
                dve.wait_ge(s["out_proj"], m + 1)
                dve.wait_ge(s["x2_in"], 16 * (m + 1))
                tt(x2[:], x2[:], bank[:, 2:4].rearrange("p b w -> p (b w)"), ALU.add).then_inc(s["x2_ready"], 1)
                share()
                dve.wait_ge(s["x2_r_ready"], m + 1)
                dve.wait_ge(s["ffn_row_ready"], 2 * m + 1)
                stt(out=h2, in0=x2[:], scalar=stat[:, 5:6], in1=bank[:, 0:2].rearrange("p b w -> p (b w)"),
                    op0=ALU.mult, op1=ALU.mult).then_inc(s["h2_ready"], 1)
                for _ in range(13):
                    share()
                dve.wait_ge(s["score_copied"], m + 1)
                dve.sem_inc(s["held_dve"])
                top16(m, LISTS, score, rest, best, best_at, "best_hi", "best_hi_at", "rest_ready", "best_lo", "best_lo_at", share)
                nc.vector.tensor_copy(best_key, best_at).then_inc(s["key_ready"], 1)
                b, k = (t.rearrange("p (h two) k -> p h two k", two=2) for t in (best, best_key))
                n8, at = TOPK // 2, 0
                dve.wait_ge(s["key_ready"], m + 1)
                for a, n in RUNS:
                    tt(cand[:, :, at:at + n], b[:, :, 0, a:a + 1].broadcast_to([P, PEER_H, n]), b[:, :, 1, 0:n], ALU.add)
                    stt(out=cand_id[:, :, at:at + n], in0=k[:, :, 0, a:a + 1].broadcast_to([P, PEER_H, n]), scalar=float(N_KEYS),
                        in1=k[:, :, 1, 0:n], op0=ALU.mult, op1=ALU.add)
                    at += n
                stt(out=cand_id[:, :, at:], in0=k[:, :, 0, n8:], scalar=float(N_KEYS),
                    in1=k[:, :, 1, 0:1].broadcast_to([P, PEER_H, n8]), op0=ALU.mult, op1=ALU.add).then_inc(s["id_ready"], 1)
                tt(cand[:, :, at:], b[:, :, 0, n8:], b[:, :, 1, 0:1].broadcast_to([P, PEER_H, n8]),
                   ALU.add).then_inc(s["cand_ready"], 1)
                share()
                dve.wait_ge(s["cand_ready"], m + 1)
                dve.sem_inc(s["held_dve"])
                top16(m, PEER_H, cand, cand_rest, top, top_at, "top_hi", "top_hi_at", "cand_rest_ready", "top_lo", "top_lo_at", share)
                nc.vector.tensor_copy(top_rank, top_at).then_inc(s["top_rank_ready"], 1)
                tt(shifted, top, top[:, :, 0:1].broadcast_to([P, PEER_H, TOPK]), ALU.subtract).then_inc(s["shifted_ready"], 1)
                dve.wait_ge(s["top_rank_ready"], m + 1)
                full = [P, HALF_H, TOPK, CANDS]
                for half in range(2):
                    hs = slice(half * HALF_H, (half + 1) * HALF_H)
                    if half:
                        dve.wait_ge(s["top_id_ready"], 2 * m + 1)
                    tt(chosen, rank[:, None, None, :].broadcast_to(full), top_rank[:, hs, :, None].broadcast_to(full),
                       ALU.is_equal).then_inc(s["chosen_ready"], 1)
                    share()
                    dve.wait_ge(s["chosen_ready"], 2 * m + half + 1)
                    tt(chosen, chosen, cand_id[:, hs, None, :].broadcast_to(full), ALU.mult).then_inc(s["chosen_id"], 1)
                    share()
                    dve.wait_ge(s["chosen_id"], 2 * m + half + 1)
                    nc.vector.tensor_reduce(top_id[:, hs], chosen, AX_X, ALU.add).then_inc(s["top_id_ready"], 1)
                    share()
                dve.wait_ge(s["weight_ready"], m + 1)
                nc.vector.tensor_reduce(total[:], weight, AX_X, ALU.add).then_inc(s["total_ready"], 1)
                dve.wait_ge(s["total_ready"], m + 1)
                nc.vector.reciprocal(total[:], total[:]).then_inc(s["total_inv"], 1)
                dve.wait_ge(s["total_inv"], m + 1)
                tt(gates[:], weight, over_free(total[:], TOPK), ALU.mult).then_inc(s["gates_ready"], 1)
                dve.wait_ge(s["top_id_ready"], 2 * (m + 1))
                nc.vector.tensor_copy(picks[:].rearrange("p (h k) -> p h k", h=PEER_H), top_id).then_inc(s["picks_ready"], 1)

            nc.vector.memset(eps[:], EPS).then_inc(s["eps_set_m"], 1)
            nc.vector.memset(S_gdn[:], 0.0).then_inc(s["setup_done"], 1)
            nc.vector.memset(S_ssd[:], 0.0).then_inc(s["setup_done"], 1)
            dve.wait_ge(s["consts"], 16 * N_CONST)
            nc.vector.memset(head_bias[:, HEADS:], 0.0).then_inc(s["setup_done"], 1)
            for k in range(KD):
                nc.vector.tensor_scalar(w_out[:, k], w_out[:, k], w_mix[:, min(k, 4):min(k, 4) + 1], None,
                                        ALU.mult).then_inc(s["setup_done"], 1)
            dve.wait_ge(s["neg_a_exp"], 1)
            ts(neg_a[:], neg_a[:], -1.0, None, ALU.mult).then_inc(s["setup_done"], 1)
            dve.wait_ge(s["setup_done"], 4 + KD)
            for j in range(SLOTS):
                dve.sem_inc(used[j])
            dve.sem_inc(s["out_stored"])

            def body(m, e):
                share = expert_share(e, do)
                if m is not None:
                    steps(m, share)
                share(last=True)
                if m is not None:
                    dve.wait_ge(s["h2_ready"], m + 1)
                    if e is not None:
                        after_use(dve, ("U", PICKS - 1, 0), e)
                    dve.wait_ge(s["ffn_row_ready"], 2 * (m + 1))
                    stt(out=h2_e[:], in0=x2[:], scalar=stat[:, 5:6], in1=bank[:, 0:2].rearrange("p b w -> p (b w)"),
                        op0=ALU.mult, op1=ALU.mult).then_inc(s["h2_copied"], 1)

            tile_loop(dve, body)


def program(nc, A, out):
    ch_scr = nc.dram_tensor("ch_scr", [BLOCKS, P, SEQ], F32).ap()
    tok_scr = nc.dram_tensor("tok_scr", [SEQ, CONV_CH], F32).ap()
    zgs_scr = nc.dram_tensor("zgs_scr", [SEQ, ZGS], F32).ap()
    with nc.sbuf_tensor("hn_T", [P, KD, SEQ], F32) as hn_T:
        norm_stage(nc, A, hn_T)
        conv_stage(nc, A, hn_T, ch_scr, tok_scr)
        gate_stage(nc, A, hn_T, zgs_scr)
    tile_stage(nc, A, ch_scr, tok_scr, zgs_scr, out)


_OUT = ((1, SEQ, D), "float32")


def constants():
    import numpy as np

    s, l = np.arange(P)[:, None], np.arange(P)[None, :]
    level = [((s // b % 2 == 0) & (l // b == s // b + 1)).astype(np.float32) for b in LEVELS]
    return {
        "c_ident": np.eye(P, dtype=np.float32),
        "c_upper": (s <= l).astype(np.float32),
        "c_ones": np.ones((P, P), np.float32),
        "c_floor": np.where(s <= l, 0.0, NEG).astype(np.float32),
        "c_level": np.stack(level, axis=1),
        "c_rank": np.broadcast_to(np.arange(CANDS, dtype=np.float32), (P, CANDS)).copy(),
    }


def kernel(**inputs):
    import numpy as _np
    import concourse.bacc as _bacc
    from concourse import mybir as _mybir
    from concourse.bass_utils import run_bass_kernel_spmd as _run

    nc = _bacc.Bacc("TRN2", target_bir_lowering=False, num_devices=1)
    arrays, args = {}, {}
    for name, value in {**inputs, **constants()}.items():
        a = _np.ascontiguousarray(value)
        arrays[f"in_{name}_dram"] = a
        args[name] = nc.dram_tensor(f"in_{name}_dram", a.shape, _mybir.dt.from_np(a.dtype), kind="ExternalInput").ap()
    out = nc.dram_tensor("out_0_dram", _OUT[0], _mybir.dt.from_np(_np.dtype(_OUT[1])), kind="ExternalOutput").ap()
    program(nc, args, out)
    r = _run(nc, [arrays], core_ids=[0])
    return r.results[0]["out_0_dram"]
```

```python
from contextlib import ExitStack

import concourse.bass as bass
from concourse import mybir

ALU = mybir.AluOpType
ACT = mybir.ActivationFunctionType
F32 = mybir.dt.float32
U32 = mybir.dt.uint32
LOG_EXP_SET = "natural_log_exp_and_others"
AX_X = mybir.AxisListType.X

P = 128
D = 1024
SEQ = 1024
KD = D // P
TILES = SEQ // P
BANK = 512
EPS = 1e-6
TAPS = 4
HALO = TAPS - 1

SSD_H, SSD_P, SSD_G = 8, 64, 2
SSD_R = SSD_H // SSD_G
SSD_W = SSD_H * SSD_P
GDN_H = 4
GDN_W = GDN_H * P
HEADS = SSD_H + GDN_H
SSD_BLOCKS = (SSD_W + 2 * SSD_G * P) // P
GDN_BLOCKS = 3 * GDN_W // P
BLOCKS = SSD_BLOCKS + GDN_BLOCKS
CONV_CH = BLOCKS * P

COL_XBC = SSD_W
COL_DT = COL_XBC + SSD_BLOCKS * P
COL_QKV = COL_DT + SSD_H
COL_GATE = COL_QKV + GDN_BLOCKS * P
COL_BETA = COL_GATE + GDN_W
COL_ALPHA = COL_BETA + GDN_H
SMALL = HEADS + GDN_H
ZG = SSD_W + GDN_W
ZGS = ZG + SMALL
ZGS_PARTS = ((0, 0, SSD_W), (SSD_W, COL_GATE, GDN_W), (ZG, COL_DT, SSD_H),
             (ZG + SSD_H, COL_ALPHA, GDN_H), (ZG + HEADS, COL_BETA, GDN_H))

TOK_B = SSD_W
TOK_Q = SSD_BLOCKS * P
TOK_K = TOK_Q + GDN_W
TOK_V = TOK_K + GDN_W
CH_FIRST = SSD_W // P
CH_N = 2 * SSD_G + GDN_H

LEVELS = [1 << n for n in range(7)]
NEG = -1e4

PEER_H = 8
TOPK = 16
LISTS = 2 * PEER_H
N_KEYS = 128
PICKS = PEER_H * TOPK
RUNS = [(a, TOPK // (a + 1)) for a in range(TOPK // 2)]
CANDS = sum(n for _, n in RUNS) + TOPK // 2

SLOTS = 10
GROUP = 32
LAG = 40
TAIL = PICKS - LAG
HEAD = SLOTS
assert LAG % SLOTS == 0


def expert_sequence():
    seq, v = [], 0
    for n in range(PICKS):
        seq.append(("U", n, 0))
        while v < min(LAG, (n + 1) * 4 // 3 + 1):
            seq.append(("V", TAIL + v, 1))
            v += 1
        if n >= LAG:
            seq.append(("V", n - LAG, 0))
        if n % GROUP == GROUP - 1:
            seq.append(("G", n // GROUP, 0))
        if n == 3:
            seq.append(("C", PICKS // GROUP - 1, 1))
        if n % GROUP == 5 and n > GROUP:
            seq.append(("C", n // GROUP - 1, 0))
        for at, item in ((8, ("K", 0, 0)), (30, ("F", 0, 1)), (33, ("O", 0, 1)), (LAG - 1, ("X", 0, 0))):
            if n == at:
                seq.append(item)
    return seq


SEQUENCE = expert_sequence()
FIRST, FULL, LAST = "first", "full", "last"
BACKS = {FIRST: (0,), FULL: (0, 1), LAST: (1,)}


def gathers(mode):
    return [item for item in SEQUENCE if item[0] in "UV" and item[2] in BACKS[mode]]


ORDER = {mode: {item: n for n, item in enumerate(gathers(mode))} for mode in BACKS}
PACE = ([(4, .5)] * 3
        + [(4, .5)] * 6
        + [(8, .5)] * 6
        + [(6, .5)] * 4 + [(4, .5)] * 2
        + [(5, .1)] * 5 + [(4, .1)]
        + [(5, .1)] * 13
        + [(3, .9)] * 10 + [(5, .9)] + [(3, .9)] * 5
        + [(6, .9)] * 6
        + [(15, .5)])
SEGMENTS = len(PACE) - 1


def share_ends():
    return [round(len(SEQUENCE) * sum(work for work, _ in PACE[:n + 1]) / sum(work for work, _ in PACE))
            for n in range(len(PACE))]


SHARE_ENDS = share_ends()


def split_v():
    split, owed, at = ([], []), 0.0, 0
    for end, (_, on_pe) in zip(SHARE_ENDS, PACE):
        for kind, n, _ in SEQUENCE[at:end]:
            if kind == "V":
                owed += on_pe
                split[owed < 1].append(n)
                owed -= owed >= 1
        at = end
    return [sorted(s) for s in split]


PE_PICKS, DVE_PICKS = split_v()
USES = [len(range(j, len(ORDER[FULL]), SLOTS)) for j in range(SLOTS)]
FEWER = LAG // SLOTS


def scope(nc):
    ctx, taken = ExitStack(), []

    def clear():
        nc.clear_and_free_semaphores(taken)
        nc.all_engine_barrier()

    ctx.callback(clear)
    sb = lambda name, shape, dt=F32: ctx.enter_context(nc.sbuf_tensor(name, shape, dt))
    ps = lambda name, shape, dt=F32: ctx.enter_context(nc.psum_tensor(name, shape, dt))

    def sem(name):
        taken.append(nc.alloc_semaphore(name))
        return taken[-1]

    return ctx, sb, ps, sem


def front_stage(nc, A, ch_scr, tok_scr, zgs_scr, w_out, w_q, w_late_loaded):
    ctx, sb, ps, sem = scope(nc)
    with ctx:
        hn_T = sb("hn_T", [P, KD, SEQ])
        w_zgs = sb("w_zgs", [P, KD, ZGS])
        ident = sb("ident_f", [P, P])
        eps = sb("eps", [P, 1])
        mean_sq = sb("mean_sq", [P, 2])
        log_ms = sb("log_ms", [P, 1])
        rstd = sb("rstd", [P, 2])
        w_col = sb("w_col", [P, KD])
        w_blk = sb("w_blk", [P, 2, KD, P])
        pre = sb("pre", [P, 2, max(HALO + SEQ, ZGS)])
        mixed = sb("conv_sum", [P, 2, SEQ])
        post = sb("post", [P, 2, SEQ])
        frames = sb("frames", [P, 2, TILES, P])
        taps = sb("taps", [P, TAPS, BLOCKS])
        bias = sb("conv_bias", [P, BLOCKS])
        x_in = w_blk.rearrange("p j k c -> p j (k c)")
        x_n, x_sq = pre[:, :, 0:D], mixed[:, 0]
        h_tile, zgs = w_blk, pre[:, :, 0:ZGS]
        proj = [ps(f"proj{j}", [P, SEQ]) for j in range(2)]
        turned = [ps(f"turned{j}", [P, TILES, P]) for j in range(2)]
        small_ps = [turned[j][:, 0, 0:SMALL] for j in range(2)]
        x_loaded = [sem("x_loaded_even"), sem("x_loaded_odd")]
        norm_consts_loaded, conv_consts_loaded = sem("norm_consts_loaded"), sem("conv_consts_loaded")
        mean_done, rstd_done, xn_done = sem("mean_done"), sem("rstd_done"), sem("xn_done")
        eps_set, log_done = sem("eps_set"), sem("log_done")
        norm_turned, hnT_done, halo_zero = sem("norm_turned"), sem("hnT_done"), sem("halo_zero")
        w_loaded = [sem("w_loaded_even"), sem("w_loaded_odd")]
        proj_done, pre_done, tap_done = sem("proj_done"), sem("pre_done"), sem("tap_done")
        silu_done, turn_done, frames_done = sem("silu_done"), sem("post_turn_done"), sem("frames_done")
        ch_stored = [sem("ch_stored_even"), sem("ch_stored_odd")]
        tok_stored = [sem("tok_stored_even"), sem("tok_stored_odd")]
        w_zgs_loaded, tile_copied, zg_done = sem("w_zgs_loaded"), sem("tile_copied"), sem("zg_done")
        zg_silu_done, small_done = sem("zg_silu_done"), sem("small_done")
        zgs_stored = [sem("zgs_stored_even"), sem("zgs_stored_odd")]
        x_rows = A["x"].rearrange("b (i p) d -> (b i) p d", p=P)
        w_in = A["w_in"].rearrange("l (k p) c -> p (l k) c", p=P)
        tok_out = tok_scr.rearrange("(i p) c -> p i c", p=P)
        zgs_out = zgs_scr.rearrange("(i p) c -> i p c", p=P)
        w_out_src = A["w_out"].rearrange("l (k p) d -> p (l k) d", p=P)
        w_q_src = A["peer_w_q"].rearrange("l (k p) c -> p (l k) c", p=P)
        CONV_CONSTS = 2 * TAPS + 1
        PAIRS = TILES // 2
        LAST = BLOCKS // 2 - 1
        block = ctx.enter_context(nc.Block())

        @block.sync
        def _(sp):
            with nc.allow_non_contiguous_dma(reason="one column of weights per channel block"):
                sp.dma_start(w_col[:], A["norm_mix_w"].rearrange("l (k p) -> p (l k)", p=P)).then_inc(norm_consts_loaded, 16)
            sp.dma_start(ident[:], A["c_ident"]).then_inc(norm_consts_loaded, 16)

            def load_x(i, j):
                sp.dma_start(x_in[:, j, :], x_rows[bass.ds(2 * i + j, 1)].rearrange("o p d -> (o p) d")).then_inc(x_loaded[j], 16)

            load_x(0, 0)
            load_x(0, 1)
            with sp.Fori(1, PAIRS) as i:
                for j in range(2):
                    sp.wait_ge(xn_done, 2 * (i - 1) + j + 1)
                    load_x(i, j)
            for first, last, col in ((0, SSD_BLOCKS, COL_XBC), (SSD_BLOCKS, BLOCKS, COL_QKV - SSD_BLOCKS * P)):
                def load_w(i, j):
                    sp.dma_start(w_blk[:, j], w_in[:, :, bass.ds((2 * i + j) * P + col, P)]).then_inc(w_loaded[j], 16)

                if first == 0:
                    for j in range(2):
                        sp.wait_ge(xn_done, 2 * (PAIRS - 1) + j + 1)
                        load_w(0, j)
                with sp.Fori(max(first // 2, 1), last // 2) as i:
                    for j in range(2):
                        sp.wait_ge(proj_done, 2 * (i - 1) + j + 1)
                        load_w(i, j)
            with nc.allow_non_contiguous_dma(reason="the per-head columns are narrow"):
                for at, col, n in ZGS_PARTS:
                    sp.dma_start(w_zgs[:, :, at:at + n], w_in[:, :, col:col + n]).then_inc(w_zgs_loaded, 16)
            with sp.Fori(0, PAIRS) as i:
                for j in range(2):
                    sp.wait_ge(zg_silu_done, 2 * i + j + 1)
                    sp.wait_ge(small_done, 2 * i + j + 1)
                    sp.dma_start(zgs_out[bass.ds(2 * i + j, 1)].rearrange("o p c -> (o p) c"), zgs[:, j]).then_inc(zgs_stored[j], 16)
                    some = bass.ds(2 * i + j, 1)
                    sp.dma_start(w_out[:, some], w_out_src[:, some]).then_inc(w_late_loaded, 16)
                    sp.dma_start(w_q[:, some], w_q_src[:, some]).then_inc(w_late_loaded, 16)
            for s in zgs_stored:
                sp.wait_ge(s, 16 * PAIRS)

        @block.gpsimd
        def _(pool):
            with nc.allow_non_contiguous_dma(reason="one conv weight per channel"):
                for tap in range(TAPS):
                    pool.dma_start(taps[:, tap, 0:SSD_BLOCKS], A["ssd_conv_w"][0, tap].rearrange("(b p) -> p b", p=P)).then_inc(conv_consts_loaded, 16)
                    pool.dma_start(taps[:, tap, SSD_BLOCKS:], A["gdn_conv_w"][0, tap].rearrange("(b p) -> p b", p=P)).then_inc(conv_consts_loaded, 16)
                pool.dma_start(bias[:, 0:SSD_BLOCKS], A["ssd_conv_b"].rearrange("l (b p) -> p (l b)", p=P)).then_inc(conv_consts_loaded, 16)
            with pool.Fori(0, BLOCKS // 2) as i:
                for j in range(2):
                    pool.wait_ge(silu_done, 2 * i + j + 1)
                    pool.dma_start(ch_scr[bass.ds(2 * i + j, 1)].rearrange("o p t -> (o p) t"), post[:, j]).then_inc(ch_stored[j], 16)
                    pool.wait_ge(frames_done, 2 * i + j + 1)
                    pool.dma_start(tok_out[:, :, bass.ds((2 * i + j) * P, P)], frames[:, j]).then_inc(tok_stored[j], 16)
            for s in (*ch_stored, *tok_stored):
                pool.wait_ge(s, 16 * (BLOCKS // 2))

        @block.tensor
        def _(pe):
            def turn_x(i, j):
                pe.wait_ge(xn_done, 2 * i + j + 1)
                for k in range(KD):
                    last = nc.tensor.transpose(turned[j][:, k, :], x_n[:, j, k * P:(k + 1) * P], ident[:])
                last.then_inc(norm_turned, 1)

            def project(i, j):
                pe.wait_ge(w_loaded[j], 16 * (i + 1))
                for half in range(SEQ // BANK):
                    cols = slice(half * BANK, (half + 1) * BANK)
                    for k in range(KD):
                        last = nc.tensor.matmul(proj[j][:, cols], w_blk[:, j, k, :], hn_T[:, k, cols],
                                                start=(k == 0), stop=(k == KD - 1))
                last.then_inc(proj_done, 1)

            def turn(i, j):
                pe.wait_ge(silu_done, 2 * i + j + 1)
                for t in range(TILES):
                    last = nc.tensor.transpose(turned[j][:, t, :], post[:, j, t * P:(t + 1) * P], ident[:])
                last.then_inc(turn_done, 1)

            def gate(i, j):
                pe.wait_ge(tile_copied, 2 * i + j + 1)
                for out, at, n in ((proj[j][:, 0:BANK], 0, BANK), (proj[j][:, BANK:], BANK, BANK), (small_ps[j], ZG, SMALL)):
                    for k in range(KD):
                        last = nc.tensor.matmul(out, h_tile[:, j, k, :], w_zgs[:, k, at:at + n],
                                                start=(k == 0), stop=(k == KD - 1))
                last.then_inc(zg_done, 1)

            pe.wait_ge(norm_consts_loaded, 32)
            turn_x(0, 0)
            turn_x(0, 1)
            with pe.Fori(1, PAIRS) as i:
                for j in range(2):
                    pe.wait_ge(hnT_done, 2 * (i - 1) + j + 1)
                    turn_x(i, j)
            pe.wait_ge(hnT_done, TILES)
            project(0, 0)
            project(0, 1)
            turn(0, 0)
            with pe.Fori(1, BLOCKS // 2) as i:
                pe.wait_ge(pre_done, 2 * i - 1)
                project(i, 0)
                pe.wait_ge(frames_done, 2 * i - 1)
                turn(i - 1, 1)
                pe.wait_ge(pre_done, 2 * i)
                project(i, 1)
                pe.wait_ge(frames_done, 2 * i)
                turn(i, 0)
            pe.wait_ge(w_zgs_loaded, 16 * len(ZGS_PARTS))
            pe.wait_ge(pre_done, BLOCKS)
            pe.wait_ge(frames_done, BLOCKS - 1)
            gate(0, 0)
            turn(LAST, 1)
            pe.wait_ge(frames_done, BLOCKS)
            gate(0, 1)
            with pe.Fori(1, PAIRS) as i:
                for j in range(2):
                    pe.wait_ge(zg_silu_done, 2 * (i - 1) + j + 1)
                    pe.wait_ge(small_done, 2 * (i - 1) + j + 1)
                    gate(i, j)

        @block.scalar
        def _(act):
            nc.scalar.preload_act_table_set(LOG_EXP_SET)
            act.wait_ge(eps_set, 1)

            def rms(i, j):
                act.wait_ge(x_loaded[j], 16 * (i + 1))
                nc.scalar.activation(x_sq, x_in[:, j, :], ACT.Square, scale=D ** -0.5,
                                     accum_out=mean_sq[:, j:j + 1]).then_inc(mean_done, 1)
                act.wait_ge(mean_done, 2 * i + j + 1)
                nc.scalar.activation(log_ms[:], mean_sq[:, j:j + 1], ACT.Ln, bias=eps[:]).then_inc(log_done, 1)
                act.wait_ge(log_done, 2 * i + j + 1)
                nc.scalar.activation(rstd[:, j:j + 1], log_ms[:], ACT.Exp, scale=-0.5).then_inc(rstd_done, 1)

            rms(0, 0)
            act.wait_ge(rstd_done, 1)
            rms(0, 1)
            with act.Fori(1, PAIRS) as i:
                for j in range(2):
                    act.wait_ge(rstd_done, 2 * i + j)
                    act.wait_ge(xn_done, 2 * (i - 1) + j + 1)
                    rms(i, j)
            act.wait_ge(conv_consts_loaded, 16 * CONV_CONSTS)
            act.wait_ge(halo_zero, 2)

            def shape(i, j):
                b = 2 * i + j
                peeled = isinstance(i, int)
                act.wait_ge(proj_done, b + 1)
                if not peeled:
                    act.wait_ge(tap_done, TAPS * (b - 1))
                nc.scalar.copy(pre[:, j, HALO:HALO + SEQ], proj[j][:]).then_inc(pre_done, 1)
                act.wait_ge(tap_done, TAPS * (b + 1))
                if not peeled:
                    act.wait_ge(turn_done, b - 1)
                    act.wait_ge(ch_stored[j], 16 * i)
                nc.scalar.activation(post[:, j], mixed[:, j], ACT.Silu, bias=bias[:, bass.ds(b, 1)]).then_inc(silu_done, 1)
                act.wait_ge(turn_done, b + 1)
                if not peeled:
                    act.wait_ge(tok_stored[j], 16 * i)
                nc.scalar.copy(frames[:, j], turned[j][:]).then_inc(frames_done, 1)

            shape(0, 0)
            shape(0, 1)
            with act.Fori(1, BLOCKS // 2) as i:
                shape(i, 0)
                shape(i, 1)
            def zg(i, j):
                act.wait_ge(zg_done, 2 * i + j + 1)
                nc.scalar.activation(zgs[:, j, 0:ZG], proj[j][:], ACT.Silu).then_inc(zg_silu_done, 1)

            zg(0, 0)
            zg(0, 1)
            with act.Fori(1, PAIRS) as i:
                for j in range(2):
                    act.wait_ge(zgs_stored[j], 16 * i)
                    zg(i, j)

        @block.vector
        def _(dve):
            nc.vector.memset(eps[:], EPS).then_inc(eps_set, 1)
            nc.vector.memset(bias[:, SSD_BLOCKS:], 0.0).then_inc(halo_zero, 1)
            dve.wait_ge(norm_consts_loaded, 32)

            def scale_x(i, j):
                dve.wait_ge(rstd_done, 2 * i + j + 1)
                nc.vector.tensor_scalar(x_n[:, j, :], x_in[:, j, :], rstd[:, j:j + 1], None, ALU.mult).then_inc(xn_done, 1)

            def weigh(i, j):
                dve.wait_ge(norm_turned, 2 * i + j + 1)
                nc.vector.tensor_tensor(hn_T[:, :, bass.ds((2 * i + j) * P, P)], turned[j][:],
                                        w_col[:, :, None].broadcast_to([P, KD, P]), ALU.mult).then_inc(hnT_done, 1)

            scale_x(0, 0)
            scale_x(0, 1)
            with dve.Fori(1, PAIRS) as i:
                for j in range(2):
                    weigh(i - 1, j)
                    scale_x(i, j)
            weigh(PAIRS - 1, 0)
            weigh(PAIRS - 1, 1)
            dve.wait_ge(hnT_done, TILES)

            def copy_tile(i, j):
                nc.vector.tensor_copy(h_tile[:, j], hn_T[:, :, bass.ds((2 * i + j) * P, P)]).then_inc(tile_copied, 1)

            nc.vector.memset(pre[:, :, 0:HALO], 0.0).then_inc(halo_zero, 1)
            dve.wait_ge(halo_zero, 2)
            dve.wait_ge(conv_consts_loaded, 16 * CONV_CONSTS)

            def conv(i, j):
                b = 2 * i + j
                dve.wait_ge(pre_done, b + 1)
                nc.vector.tensor_scalar(mixed[:, j], pre[:, j, 0:SEQ], taps[:, 0, bass.ds(b, 1)], None,
                                        ALU.mult).then_inc(tap_done, 1)
                for tap in range(1, TAPS):
                    dve.wait_ge(tap_done, TAPS * b + tap)
                    nc.vector.scalar_tensor_tensor(out=mixed[:, j], in0=pre[:, j, tap:tap + SEQ],
                                                   scalar=taps[:, tap, bass.ds(b, 1)], in1=mixed[:, j],
                                                   op0=ALU.mult, op1=ALU.add).then_inc(tap_done, 1)

            conv(0, 0)
            conv(0, 1)
            with dve.Fori(1, LAST) as i:
                for j in range(2):
                    dve.wait_ge(silu_done, 2 * (i - 1) + j + 1)
                    conv(i, j)
            for j in range(2):
                dve.wait_ge(silu_done, 2 * (LAST - 1) + j + 1)
                conv(LAST, j)
                copy_tile(0, j)
            def small(i, j):
                dve.wait_ge(zg_done, 2 * i + j + 1)
                nc.vector.tensor_copy(zgs[:, j, ZG:], small_ps[j]).then_inc(small_done, 1)

            small(0, 0)
            copy_tile(1, 0)
            small(0, 1)
            copy_tile(1, 1)
            with dve.Fori(1, PAIRS - 1) as i:
                for j in range(2):
                    dve.wait_ge(zgs_stored[j], 16 * i)
                    small(i, j)
                    copy_tile(i + 1, j)
            for j in range(2):
                dve.wait_ge(zgs_stored[j], 16 * (PAIRS - 1))
                small(PAIRS - 1, j)


def over_free(ap, n):
    return ap[:, :, None].broadcast_to([ap.shape[0], ap.shape[1], n])


def over_heads(ap, n):
    return ap[:, None, :].broadcast_to([ap.shape[0], n, ap.shape[1]])


def view(flat, *shape):
    names = "abc"[:len(shape)]
    return flat.rearrange(f"p ({' '.join(names)}) -> p {' '.join(names)}", **dict(zip(names[1:], shape[1:])))


ARENA = 11024


def tile_stage(nc, A, ch_scr, tok_scr, zgs_scr, out, w_out, w_q, w_late_loaded):
    ctx, sb, ps, sem = scope(nc)
    NL = len(LEVELS)
    with ctx:
        ident = sb("ident_m", [P, P])
        upper = sb("upper", [P, P])
        ones = sb("ones", [P, P])
        floor = sb("floor", [P, P])
        level = sb("level", [P, NL, P])
        rank = sb("rank", [P, CANDS])
        keys_T = sb("keys_T", [P, 2, N_KEYS])
        w_rows = sb("w_rows", [2 * KD, P])
        w_mix = sb("w_mix", [P, KD])
        head_bias = sb("head_bias", [P, SMALL])
        neg_a = sb("neg_a", [P, HEADS])
        d_head = sb("d_head", [P, SSD_H])
        eps = sb("eps_m", [P, 1])
        S_gdn = sb("S_gdn", [P, GDN_H, P])
        S_ssd = sb("S_ssd", [P, SSD_H, SSD_P])
        x2 = sb("x2", [P, D])
        picks = sb("picks", [P, PICKS], U32)
        gates = sb("gates", [P, PEER_H, TOPK])
        gates_e = sb("gates_e", [P, PICKS])
        h2_e = sb("h2_e", [P, D])
        y = sb("y", [P, D])
        at_row = sb("at_row", [P, PICKS], U32)
        at_tail = sb("at_tail", [P, LAG], U32)
        at_head = sb("at_head", [P, HEAD], U32)
        ring = sb("ring", [P, SLOTS, D])
        dots = sb("dots", [P, PICKS])
        coef = sb("coef", [P, PICKS])
        diag = sb("diag", [P, 2, P])
        stat_e = sb("stat_e", [P, 3])
        small = sb("small", [P, SMALL])
        small_abs = sb("small_abs", [P, SMALL])
        small_exp = sb("small_exp", [P, SMALL])
        soft = sb("soft", [P, HEADS])
        rate = sb("rate", [P, HEADS])
        beta_den = sb("beta_den", [P, GDN_H])
        beta_num = sb("beta_num", [P, GDN_H])
        beta = sb("beta", [P, GDN_H])
        logs = sb("logs", [P, 3, HEADS])
        exps = sb("exps", [P, 3, HEADS])
        qk_ms = sb("qk_ms", [P, 2 * GDN_H])
        qk_log = sb("qk_log", [P, 2 * GDN_H])
        qk_r = sb("qk_r", [P, 2 * GDN_H])
        stat = sb("stat", [P, 8])
        r_gdn = sb("r_gdn", [P, 3, GDN_H])
        total = sb("total", [P, PEER_H])

        TOK = CONV_CH - SSD_G * P
        arena = sb("arena", [P, ARENA])
        place = [0]

        def take(*shape):
            n = 1
            for d in shape:
                n *= d
            at, place[0] = place[0], place[0] + n
            flat = arena[:, at:at + n]
            return flat if len(shape) == 1 else view(flat, *shape)

        tok = take(TOK)
        ch = take(CH_N, P)
        zgs = take(ZGS)
        decay = take(HEADS, P)
        decay_flat = arena[:, place[0] - HEADS * P:place[0]]
        G = take(SSD_H, P)
        G_flat = arena[:, place[0] - SSD_H * P:place[0]]
        k_beta, k_out, kT, kbT, A_T, qk = (take(GDN_H, P) for _ in range(6))
        Y = decay[:, SSD_H:]
        x_dt, x_end = take(SSD_H, SSD_P), take(SSD_H, SSD_P)
        qkv = tok[:, SSD_W + SSD_G * P:].rearrange("p (m h w) -> p m h w", m=3, h=GDN_H)
        k_in, k_hat, v_beta = qkv[:, 0], qkv[:, 1], qkv[:, 2]
        qk_sq = decay_flat[:, 0:2 * GDN_W]
        M_T = view(decay_flat[:, 0:2 * GDN_W], 2, GDN_H, P)
        mixT = view(decay_flat[:, 0:D], KD, P)
        mix = G_flat
        v_new, X, MX, wT, o_gdn = k_hat, k_beta, kT, kbT, A_T
        y_ssd, y_skip = x_dt, x_end
        place[0] = 0
        h_T = take(KD, P)
        h2 = arena[:, place[0]:place[0] + D]
        q, q_T = take(2, 4, P), take(2, 4, P)
        score, rest = take(LISTS, N_KEYS), take(LISTS, N_KEYS)
        best = take(LISTS, TOPK)
        best_at = take(LISTS, TOPK).bitcast(U32)
        best_key = take(LISTS, TOPK)
        cand, cand_rest, cand_id = (take(PEER_H, CANDS) for _ in range(3))
        top = take(PEER_H, TOPK)
        top_at = take(PEER_H, TOPK).bitcast(U32)
        top_rank, top_id, shifted, weight = (take(PEER_H, TOPK) for _ in range(4))
        HALF_H = PEER_H // 2
        assert place[0] <= ARENA
        place[0] = 0
        chosen = take(HALF_H, TOPK, CANDS)

        bank = ps("tile_psum", [P, 6, BANK])
        y_ps = ps("y_psum", [P, 2, BANK])

        def heads(b, n=GDN_H, w=P, at=0):
            return bank[:, b, at:at + n * w].rearrange("p (h w) -> p h w", h=n)

        square = lambda b, n=1: bank[:, b:b + n].rearrange("p b (k w) -> p (b k) w", w=P)

        s = {n: sem(n) for n in (
            "consts", "neg_a_exp", "eps_set_m", "setup_done", "w_out_ready", "keys_turned", "keys_copied",
            "mix_loaded", "x2_in", "small_in", "small_abs_done", "small_exp_done",
            "soft_log", "rate_ready", "beta_parts", "beta_ready", "soft_sum", "cums_ready", "logs_ready", "logs_copied", "exps_ready",
            "decay_log", "decay_ready", "qk_sq_ready", "qk_sum", "qk_logged", "qk_r_ready", "k_hat_ready", "k_beta_ready",
            "k_in_ready", "k_turned", "kT_copied", "pairs_ready", "A_ready", "qk_ready",
            "M_ready", "Y_ready", "X_turned", "X_ready", "MX_ready", "MX_copied", "steps_ready",
            "w_ready", "w_copied", "v_new_ready", "v_new_copied", "gdn_out", "o_part", "S_gdn_part", "S_gdn_ready",
            "o_sq_ready", "o_sum", "o_logged", "o_r_ready", "o_scaled", "mix_gdn",
            "G_ready", "x_dt_ready", "x_end_ready", "ssd_out", "y_part", "y_gated", "S_ssd_part", "S_ssd_ready",
            "y_mean", "y_logged", "y_r_ready", "mix_ssd", "mix_turned", "mixT_copied", "out_proj", "x2_ready",
            "x2_mean", "x2_logged", "x2_r_ready", "ffn_row_ready", "h2_ready",
            "h_turned", "hT_copied", "q_ready", "q_copied", "q_turned", "qT_copied", "score_ready", "score_copied",
            "best_hi", "best_hi_at", "rest_ready", "best_lo", "best_lo_at",
            "key_ready", "cand_ready", "id_ready", "top_hi", "top_hi_at", "cand_rest_ready", "top_lo", "top_lo_at",
            "top_rank_ready", "chosen_ready", "chosen_id", "top_id_ready", "picks_ready", "shifted_ready", "weight_ready",
            "total_ready", "total_inv", "gates_ready", "gates_copied", "held", "held_dve", "h2_copied",
            "at_ready", "head_ready", "tail_ready", "x2_copied", "gelu_ready", "coef_ready", "diag_ready", "y_ready", "res_mean", "res_logged", "res_r_ready",
            "final_row_ready", "out_ready", "out_stored")}
        filled = [sem(f"slot_filled{j}") for j in range(SLOTS)]
        used = [sem(f"slot_used{j}") for j in range(SLOTS)]

        rows = lambda t, i: t.rearrange("(i p) c -> i p c", p=P)[bass.ds(i, 1)].rearrange("o p c -> (o p) c")
        x_rows = A["x"].rearrange("b s d -> (b s) d")
        out_rows = out.rearrange("b s d -> (b s) d")
        ch_cols = ch_scr[CH_FIRST:CH_FIRST + CH_N].rearrange("b p t -> p b t")
        tables = {"U": A["peer_u"].rearrange("l e d -> (l e) d"), "V": A["peer_v"].rearrange("l e d -> (l e) d")}
        xs = tok[:, 0:SSD_W].rearrange("p (h w) -> p h w", h=SSD_H)
        B_T, C_T, q_ch = ch[:, 0:SSD_G], ch[:, SSD_G:2 * SSD_G], ch[:, 2 * SSD_G:]
        e_in, e_all, e_out = exps[:, 0], exps[:, 1], exps[:, 2]
        N_CONST = 16
        LOADS = 4

        def mode_of(e):
            return FULL if not isinstance(e, int) or 0 < e < TILES else LAST if e else FIRST

        def uses_before(j, e):
            return USES[j] * e - FEWER if mode_of(e) != FIRST else 0

        def slot_of(item, e):
            return ORDER[mode_of(e)][item] % SLOTS

        def turn_of(item, e):
            return uses_before(slot_of(item, e), e) + ORDER[mode_of(e)][item] // SLOTS + 1

        def after_use(eng, item, e):
            if item in ORDER[mode_of(e)]:
                j, turn = slot_of(item, e), turn_of(item, e)
            else:
                item = (item[0], item[1], 0)
                n, less = ORDER[FULL][item], len(ORDER[FULL]) - len(ORDER[FIRST])
                assert ORDER[FIRST][item] == n - less
                j = n % SLOTS
                turn = uses_before(j, e) - USES[j] + n // SLOTS + 1
            eng.wait_ge(used[j], turn + 1)

        def after_fill(eng, item, e):
            eng.wait_ge(filled[slot_of(item, e)], 16 * turn_of(item, e))

        def expert_share(e, do):
            done = [0, 0]

            def share(last=False):
                done[0] += 1
                assert done[0] <= SEGMENTS or last
                to = len(SEQUENCE) if last else SHARE_ENDS[done[0] - 1]
                if e is not None:
                    for item in SEQUENCE[done[1]:to]:
                        if item[2] in BACKS[mode_of(e)]:
                            do(item, e)
                done[1] = to

            return share

        def tile_loop(eng, body):
            body(0, None)
            body(1, 0)
            with eng.Fori(2, TILES) as i:
                body(i, i - 1)
            body(None, TILES - 1)
            body(None, TILES)

        block = ctx.enter_context(nc.Block())

        @block.sync
        def _(sp):
            with nc.allow_non_contiguous_dma(reason="norm weights by channel"):
                for dst, src in ((ident[:], A["c_ident"]), (upper[:], A["c_upper"]), (ones[:], A["c_ones"]),
                                 (floor[:], A["c_floor"]), (level[:], A["c_level"]), (rank[:], A["c_rank"]),
                                 (w_mix[:, 0:4], A["ssd_norm_w"].rearrange("l (k p) -> p (l k)", p=P)),
                                 (w_mix[:, 4:5], A["gdn_norm_w"].rearrange("l p -> p l"))):
                    sp.dma_start(dst, src).then_inc(s["consts"], 16)

            def body(m, e):
                if m is not None:
                    if e is not None:
                        sp.wait_ge(s["picks_ready"], m)
                        sp.wait_ge(s["gates_ready"], m)
                    sp.dma_start(tok[:, 0:TOK_B + SSD_G * P], rows(tok_scr, m)[:, 0:TOK_B + SSD_G * P]).then_inc(s["mix_loaded"], 16)
                    sp.dma_start(tok[:, TOK_B + SSD_G * P:], rows(tok_scr, m)[:, TOK_Q:]).then_inc(s["mix_loaded"], 16)
                    sp.dma_start(ch, ch_cols[:, :, bass.ds(m * P, P)]).then_inc(s["mix_loaded"], 16)
                    sp.dma_start(zgs, rows(zgs_scr, m)).then_inc(s["mix_loaded"], 16)
                    if e is not None:
                        sp.wait_ge(s["x2_copied"], e + 1)
                    sp.dma_start(x2[:], rows(x_rows, m)).then_inc(s["x2_in"], 16)

            tile_loop(sp, body)

        @block.gpsimd
        def _(pool):
            def body(m, e):
                if e is None:
                    return
                mode = mode_of(e)
                if mode != FIRST:
                    nc.gpsimd.tensor_copy(at_tail[:], at_row[:, TAIL:]).then_inc(s["tail_ready"], 1)
                    pool.wait_ge(s["tail_ready"], e)
                if mode != LAST:
                    pool.wait_ge(s["picks_ready"], e + 1)
                    pool.sem_inc(s["held"])
                    nc.gpsimd.tensor_copy(at_head[:], picks[:, 0:HEAD]).then_inc(s["head_ready"], 1)
                    pool.wait_ge(s["head_ready"], e + 1)
                for turn, item in enumerate(gathers(mode)):
                    kind, n, back = item
                    j = slot_of(item, e)
                    if turn == SLOTS and mode != LAST:
                        nc.gpsimd.tensor_copy(at_row[:], picks[:]).then_inc(s["at_ready"], 1)
                        pool.wait_ge(s["at_ready"], e + 1)
                    if back:
                        at = at_tail[:, n - TAIL:n - TAIL + 1]
                    else:
                        assert turn >= SLOTS or n < HEAD
                        at = (at_row if turn >= SLOTS else at_head)[:, n:n + 1]
                    pool.wait_ge(used[j], turn_of(item, e))
                    pool.sem_inc(s["held"])
                    pool.indirect_dma_start(ring[:, j], None, tables[kind],
                                            bass.IndirectOffsetOnAxis(ap=at, axis=0)).then_inc(filled[j], 16)

            tile_loop(pool, body)

        @block.tensor
        def _(pe):
            def do(item, e):
                kind, n, back = item
                if kind == "F":
                    pe.wait_ge(s["res_mean"], e)
                    row_of(1, (y_ps[:, 0], y_ps[:, 1])).then_inc(s["final_row_ready"], 1)
                if kind != "V" or n not in PE_PICKS:
                    return
                k = PE_PICKS.index(n)
                if k == 0 and mode_of(e) != FIRST:
                    pe.wait_ge(s["out_ready"], e - back)
                pe.wait_ge(s["diag_ready"], len(PE_PICKS) * (e - back) + k + 1)
                after_fill(pe, item, e)
                for half in range(2):
                    last = nc.tensor.matmul(y_ps[:, half], diag[:, k % 2], ring[:, slot_of(item, e), half * BANK:(half + 1) * BANK],
                                            start=(k == 0), stop=(n == PE_PICKS[-1]))
                last.then_inc(used[slot_of(item, e)], 1)

            def row_of(r, out):
                for k in range(KD):
                    row = KD * r + k
                    last = nc.tensor.matmul(out[k // 4][:, k % 4 * P:(k % 4 + 1) * P],
                                            ident[0:2 * KD, row:row + 1].broadcast_to([2 * KD, P]),
                                            w_rows[:], start=True, stop=True)
                return last

            def steps(m, share):
                pe.wait_ge(s["mix_loaded"], 16 * LOADS * (m + 1))
                if not isinstance(m, int) or m:
                    pe.wait_ge(s["h2_copied"], m)
                for g in range(SSD_G):
                    nc.tensor.matmul(heads(0, 2, P, 256)[:, g], B_T[:, g], C_T[:, g], start=True, stop=True)
                share()
                pe.wait_ge(s["rate_ready"], m + 1)
                nc.tensor.matmul(bank[:, 0, 0:HEADS], upper[:], rate[:], start=True, stop=True)
                nc.tensor.matmul(bank[:, 0, HEADS:2 * HEADS], ones[:], rate[:], start=True, stop=True)
                for h in range(HEADS):
                    last = nc.tensor.matmul(heads(1 + h // 4)[:, h % 4], rate[:, h:h + 1].broadcast_to([P, P]), upper[:],
                                            start=True, stop=True)
                last.then_inc(s["cums_ready"], 1)
                share()
                share()
                pe.wait_ge(s["k_hat_ready"], m + 1)
                pe.wait_ge(s["k_beta_ready"], m + 1)
                for h in range(GDN_H):
                    nc.tensor.transpose(heads(4)[:, h], k_hat[:, h], ident[:])
                    last = nc.tensor.transpose(heads(5)[:, h], k_beta[:, h], ident[:])
                last.then_inc(s["k_turned"], 1)
                share()
                pe.wait_ge(s["kT_copied"], 2 * (m + 1))
                pe.wait_ge(s["decay_log"], m + 1)
                for h in range(GDN_H):
                    nc.tensor.matmul(heads(1)[:, h], kT[:, h], kbT[:, h], start=True, stop=True)
                    last = nc.tensor.matmul(heads(2)[:, h], kT[:, h], q_ch[:, h], start=True, stop=True)
                last.then_inc(s["pairs_ready"], 1)
                for _ in range(3):
                    share()
                pe.wait_ge(s["G_ready"], m + 1)
                pe.wait_ge(s["x_end_ready"], m + 1)
                pe.wait_ge(s["A_ready"], m + 1)
                for h in range(SSD_H):
                    nc.tensor.matmul(heads(4, SSD_H, SSD_P)[:, h], G[:, h], x_dt[:, h], start=True, stop=True)
                for g in range(SSD_G):
                    half = slice(g * SSD_R * SSD_P, (g + 1) * SSD_R * SSD_P)
                    group = slice(g * SSD_R, (g + 1) * SSD_R)
                    nc.tensor.matmul(bank[:, 5, half], C_T[:, g], S_ssd[:, group].rearrange("p h w -> p (h w)"),
                                     start=True, stop=True)
                    last = nc.tensor.matmul(bank[:, 1, half], tok[:, TOK_B + g * P:TOK_B + (g + 1) * P],
                                            x_end[:, group].rearrange("p h w -> p (h w)"), start=True, stop=True)
                last.then_inc(s["ssd_out"], 1)
                share()
                pe.wait_ge(s["Y_ready"], NL * m + 1)
                for h in range(GDN_H):
                    last = nc.tensor.transpose(heads(3)[:, h], Y[:, h], ident[:])
                last.then_inc(s["X_turned"], 1)
                share()
                pe.wait_ge(s["qk_ready"], m + 1)
                for n in range(1, NL):
                    pe.wait_ge(s["M_ready"], NL * m + n + 1)
                    pe.wait_ge(s["X_ready"], (NL - 1) * m + n)
                    for h in range(GDN_H):
                        last = nc.tensor.matmul(heads(0)[:, h], M_T[:, n % 2, h], X[:, h], start=True, stop=True)
                    last.then_inc(s["MX_ready"], 1)
                    pe.wait_ge(s["MX_copied"], (NL - 1) * m + n)
                    pe.wait_ge(s["Y_ready"], NL * m + n)
                    for h in range(GDN_H):
                        if n < NL - 1:
                            nc.tensor.matmul(heads(2)[:, h], Y[:, h], MX[:, h], start=True, stop=True)
                        last = nc.tensor.matmul(heads(3)[:, h], MX[:, h], Y[:, h], start=True, stop=True)
                    last.then_inc(s["steps_ready"], 1)
                    share()
                pe.wait_ge(s["Y_ready"], NL * (m + 1))
                for h in range(GDN_H):
                    last = nc.tensor.matmul(heads(0)[:, h], k_in[:, h], Y[:, h], start=True, stop=True)
                last.then_inc(s["w_ready"], 1)
                pe.wait_ge(s["w_copied"], m + 1)
                for h in range(GDN_H):
                    nc.tensor.matmul(heads(2)[:, h], Y[:, h], v_beta[:, h], start=True, stop=False)
                    last = nc.tensor.matmul(heads(2)[:, h], wT[:, h], S_gdn[:, h], start=False, stop=True)
                last.then_inc(s["v_new_ready"], 1)
                share()
                pe.wait_ge(s["y_part"], 2 * (m + 1))
                pe.wait_ge(s["v_new_copied"], m + 1)
                for h in range(GDN_H):
                    nc.tensor.matmul(heads(3)[:, h], q_ch[:, h], S_gdn[:, h], start=True, stop=True)
                    nc.tensor.matmul(heads(4)[:, h], qk[:, h], v_new[:, h], start=True, stop=True)
                    last = nc.tensor.matmul(heads(5)[:, h], k_out[:, h], v_new[:, h], start=True, stop=True)
                last.then_inc(s["gdn_out"], 1)
                for _ in range(4):
                    share()
                pe.wait_ge(s["mix_ssd"], m + 1)
                pe.wait_ge(s["mix_gdn"], m + 1)
                pe.wait_ge(s["S_ssd_ready"], m + 1)
                for k in range(KD):
                    last = nc.tensor.transpose(heads(k // 4)[:, k % 4], mix[:, k * P:(k + 1) * P], ident[:])
                last.then_inc(s["mix_turned"], 1)
                share()
                pe.wait_ge(s["mixT_copied"], m + 1)
                pe.wait_ge(s["w_out_ready"], KD)
                for half in range(D // BANK):
                    for k in range(KD):
                        last = nc.tensor.matmul(bank[:, 2 + half], mixT[:, k], w_out[:, k, half * BANK:(half + 1) * BANK],
                                                start=(k == 0), stop=(k == KD - 1))
                        if k % 4 == 3:
                            if half and k == KD - 1:
                                last.then_inc(s["out_proj"], 1)
                            share()
                row_of(0, (bank[:, 0], bank[:, 1])).then_inc(s["ffn_row_ready"], 1)
                share()
                share()
                pe.wait_ge(s["h2_ready"], m + 1)
                pe.wait_ge(s["S_gdn_ready"], m + 1)
                for k in range(KD):
                    last = nc.tensor.transpose(square(4, 2)[:, k], h2[:, k * P:(k + 1) * P], ident[:])
                last.then_inc(s["h_turned"], 1)
                share()
                pe.wait_ge(s["hT_copied"], m + 1)
                for b in range(4):
                    for k in range(KD):
                        last = nc.tensor.matmul(bank[:, b], h_T[:, k], w_q[:, k, b * BANK:(b + 1) * BANK],
                                                start=(k == 0), stop=(k == KD - 1))
                        if k == KD - 1:
                            last.then_inc(s["q_ready"], 1)
                        if k % 4 == 3:
                            share()
                for b in range(4):
                    pe.wait_ge(s["q_copied"], 4 * m + b + 1)
                    if b >= 2:
                        pe.wait_ge(s["qT_copied"], 4 * m + b - 1)
                    for n in range(4):
                        last = nc.tensor.transpose(square(4 + b % 2)[:, n], q[:, b % 2, n], ident[:])
                    last.then_inc(s["q_turned"], 1)
                    pe.wait_ge(s["qT_copied"], 4 * m + b + 1)
                    for n in range(4):
                        last = nc.tensor.matmul(square(b)[:, n], q_T[:, b % 2, n], keys_T[:, n % 2], start=True, stop=True)
                    last.then_inc(s["score_ready"], 1)
                    if b == 3:
                        pe.wait_ge(s["score_copied"], m + 1)
                        row_of(0, (bank[:, 0], bank[:, 1])).then_inc(s["ffn_row_ready"], 1)
                    share()

            pe.wait_ge(s["consts"], 16 * N_CONST)
            pe.wait_ge(w_late_loaded, 16 * 2 * KD)
            for half in range(2):
                last = nc.tensor.transpose(bank[:, 0, half * P:(half + 1) * P], ring[:, 0, half * P:(half + 1) * P], ident[:])
            last.then_inc(s["keys_turned"], 1)
            pe.wait_ge(s["keys_copied"], 1)

            def body(m, e):
                share = expert_share(e, do)
                if m is not None:
                    steps(m, share)
                share(last=True)

            tile_loop(pe, body)

        @block.scalar
        def _(act):
            def do(item, e):
                kind, n, back = item
                if kind == "G":
                    after_use(act, ("U", (n + 1) * GROUP - 1, 0), e)
                    group = slice(n * GROUP, (n + 1) * GROUP)
                    nc.scalar.activation(coef[:, group], dots[:, group], ACT.Gelu).then_inc(s["gelu_ready"], 1)
                    nc.scalar.preload_act_table_set(LOG_EXP_SET)
                if kind == "V" and n in PE_PICKS:
                    k = PE_PICKS.index(n)
                    act.wait_ge(s["coef_ready"], PICKS // GROUP * (e - back) + n // GROUP + 1)
                    if k >= 2:
                        after_use(act, ("V", PE_PICKS[k - 2], back), e)
                    nc.scalar.activation(diag[:, k % 2], ident[:], ACT.Copy, scale=coef[:, n:n + 1]).then_inc(s["diag_ready"], 1)
                if kind == "F":
                    act.wait_ge(s["y_ready"], e)
                    nc.scalar.activation(y_ps[:].rearrange("p b w -> p (b w)"), y[:], ACT.Square, scale=D ** -0.5,
                                         accum_out=stat_e[:, 0:1]).then_inc(s["res_mean"], 1)
                    act.wait_ge(s["res_mean"], e)
                    nc.scalar.activation(stat_e[:, 1:2], stat_e[:, 0:1], ACT.Ln, bias=eps[:]).then_inc(s["res_logged"], 1)
                    act.wait_ge(s["res_logged"], e)
                    nc.scalar.activation(stat_e[:, 2:3], stat_e[:, 1:2], ACT.Exp, scale=-0.5).then_inc(s["res_r_ready"], 1)
                if kind == "O":
                    act.wait_ge(s["out_ready"], e)
                    act.dma_start(rows(out_rows, e - 1), y[:]).then_inc(s["out_stored"], 16)

            def steps(m, share):
                act.wait_ge(s["small_in"], m + 1)
                nc.scalar.activation(small_abs[:], small[:], ACT.Abs).then_inc(s["small_abs_done"], 1)
                act.wait_ge(s["small_abs_done"], m + 1)
                nc.scalar.activation(small_exp[:], small_abs[:], ACT.Exp, scale=-1.0).then_inc(s["small_exp_done"], 1)
                act.wait_ge(s["small_exp_done"], m + 1)
                nc.scalar.activation(soft[:], small_exp[:, 0:HEADS], ACT.Ln, bias=1.0).then_inc(s["soft_log"], 1)
                nc.scalar.activation(qk_sq, tok[:, SSD_W + SSD_G * P:TOK - GDN_W], ACT.Square).then_inc(s["qk_sq_ready"], 1)
                share()
                act.wait_ge(s["qk_sum"], m + 1)
                nc.scalar.activation(qk_log[:], qk_ms[:], ACT.Ln, bias=eps[:]).then_inc(s["qk_logged"], 1)
                act.wait_ge(s["qk_logged"], m + 1)
                nc.scalar.activation(qk_r[:], qk_log[:], ACT.Exp, scale=-0.5).then_inc(s["qk_r_ready"], 1)
                share()
                act.wait_ge(s["logs_ready"], 2 * (m + 1))
                nc.scalar.activation(exps[:], logs[:], ACT.Exp).then_inc(s["exps_ready"], 1)
                act.wait_ge(s["decay_log"], m + 1)
                nc.scalar.activation(decay, decay, ACT.Exp).then_inc(s["decay_ready"], 1)
                share()
                act.wait_ge(s["k_turned"], m + 1)
                nc.scalar.copy(kT, heads(4)).then_inc(s["kT_copied"], 1)
                nc.scalar.copy(kbT, heads(5)).then_inc(s["kT_copied"], 1)
                for _ in range(5):
                    share()
                act.wait_ge(s["X_turned"], m + 1)
                act.wait_ge(s["k_in_ready"], m + 1)
                nc.scalar.copy(X, heads(3)).then_inc(s["X_ready"], 1)
                share()
                for n in range(1, NL):
                    act.wait_ge(s["MX_ready"], (NL - 1) * m + n)
                    nc.scalar.copy(MX, heads(0)).then_inc(s["MX_copied"], 1)
                    share()
                act.wait_ge(s["w_ready"], m + 1)
                nc.scalar.mul(wT, heads(0), -1.0).then_inc(s["w_copied"], 1)
                act.wait_ge(s["v_new_ready"], m + 1)
                nc.scalar.copy(v_new, heads(2)).then_inc(s["v_new_copied"], 1)
                share()
                share()
                act.wait_ge(s["y_gated"], m + 1)
                nc.scalar.activation(y_skip, y_ssd, ACT.Square, scale=SSD_W ** -0.5, accum_out=stat[:, 0:1]).then_inc(s["y_mean"], 1)
                act.wait_ge(s["y_mean"], m + 1)
                nc.scalar.activation(stat[:, 1:2], stat[:, 0:1], ACT.Ln, bias=eps[:]).then_inc(s["y_logged"], 1)
                act.wait_ge(s["y_logged"], m + 1)
                nc.scalar.activation(stat[:, 2:3], stat[:, 1:2], ACT.Exp, scale=-0.5).then_inc(s["y_r_ready"], 1)
                share()
                act.wait_ge(s["o_part"], 3 * (m + 1))
                nc.scalar.activation(view(qk_sq[:, 0:GDN_W], GDN_H, P), o_gdn, ACT.Square, scale=P ** -0.5).then_inc(s["o_sq_ready"], 1)
                share()
                act.wait_ge(s["o_sum"], m + 1)
                nc.scalar.activation(r_gdn[:, 1], r_gdn[:, 0], ACT.Ln, bias=eps[:]).then_inc(s["o_logged"], 1)
                act.wait_ge(s["o_logged"], m + 1)
                nc.scalar.activation(r_gdn[:, 2], r_gdn[:, 1], ACT.Exp, scale=-0.5).then_inc(s["o_r_ready"], 1)
                share()
                act.wait_ge(s["mix_turned"], m + 1)
                nc.scalar.copy(mixT, square(0, 2)).then_inc(s["mixT_copied"], 1)
                for _ in range(6):
                    share()
                act.wait_ge(s["x2_ready"], m + 1)
                nc.scalar.activation(mix, x2[:], ACT.Square, scale=D ** -0.5, accum_out=stat[:, 3:4]).then_inc(s["x2_mean"], 1)
                act.wait_ge(s["x2_mean"], m + 1)
                nc.scalar.activation(stat[:, 4:5], stat[:, 3:4], ACT.Ln, bias=eps[:]).then_inc(s["x2_logged"], 1)
                act.wait_ge(s["x2_logged"], m + 1)
                nc.scalar.activation(stat[:, 5:6], stat[:, 4:5], ACT.Exp, scale=-0.5).then_inc(s["x2_r_ready"], 1)
                share()
                act.wait_ge(s["h_turned"], m + 1)
                nc.scalar.copy(h_T, square(4, 2)).then_inc(s["hT_copied"], 1)
                share()
                for b in range(4):
                    share()
                    act.wait_ge(s["q_ready"], 4 * m + b + 1)
                    if b < 2:
                        nc.scalar.copy(q[:, b], square(b)).then_inc(s["q_copied"], 1)
                    share()
                for b in range(4):
                    act.wait_ge(s["q_turned"], 4 * m + b + 1)
                    nc.scalar.copy(q_T[:, b % 2], square(4 + b % 2)).then_inc(s["qT_copied"], 1)
                    if b < 2:
                        nc.scalar.copy(q[:, b], square(2 + b)).then_inc(s["q_copied"], 1)
                    if b < 3:
                        share()
                act.wait_ge(s["score_ready"], 4 * (m + 1))
                nc.scalar.copy(score, square(0, 4)).then_inc(s["score_copied"], 1)
                share()
                for _ in range(16):
                    share()
                act.wait_ge(s["shifted_ready"], m + 1)
                nc.scalar.activation(weight, shifted, ACT.Exp).then_inc(s["weight_ready"], 1)

            head_row = lambda name, n: A[name][0:1, 0:n].broadcast_to([P, n])
            for dst, src in ((neg_a[:, 0:SSD_H], head_row("ssd_a_log", SSD_H)),
                             (neg_a[:, SSD_H:], head_row("gdn_a_log", GDN_H)),
                             (head_bias[:, 0:SSD_H], head_row("ssd_dt_bias", SSD_H)),
                             (head_bias[:, SSD_H:HEADS], head_row("gdn_dt_bias", GDN_H)),
                             (d_head[:], head_row("ssd_d", SSD_H)),
                             (view(ring[:, 0, 0:2 * P], 2, P), A["peer_sub_keys"].rearrange("l two k d -> k (l two) d")),
                             (w_rows[0:KD], A["norm_ffn_w"].rearrange("l (k p) -> (l k) p", p=P)),
                             (w_rows[KD:], A["norm_final_w"].rearrange("(k p) -> k p", p=P))):
                act.dma_start(dst, src).then_inc(s["consts"], 16)
            nc.scalar.preload_act_table_set(LOG_EXP_SET)
            act.wait_ge(s["consts"], 16 * N_CONST)
            act.wait_ge(s["eps_set_m"], 1)
            nc.scalar.activation(neg_a[:], neg_a[:], ACT.Exp).then_inc(s["neg_a_exp"], 1)
            act.wait_ge(s["keys_turned"], 1)
            nc.scalar.copy(keys_T[:], bank[:, 0, 0:2 * P].rearrange("p (n k) -> p n k", n=2)).then_inc(s["keys_copied"], 1)

            def body(m, e):
                share = expert_share(e, do)
                if m is not None:
                    steps(m, share)
                share(last=True)

            tile_loop(act, body)
            act.wait_ge(s["out_stored"], 16 * TILES + 1)

        @block.vector
        def _(dve):
            tt, ts, stt = nc.vector.tensor_tensor, nc.vector.tensor_scalar, nc.vector.scalar_tensor_tensor

            def do(item, e):
                kind, n, back = item
                if kind == "U":
                    if n == 0:
                        dve.wait_ge(s["h2_copied"], e + 1)
                    after_fill(dve, item, e)
                    j = slot_of(item, e)
                    nc.vector.tensor_tensor_reduce(out=ring[:, j], in0=ring[:, j], in1=h2_e[:], scale=1.0, scalar=0.0,
                                                   op0=ALU.mult, op1=ALU.add, accum_out=dots[:, n:n + 1]).then_inc(used[j], 1)
                if kind == "K":
                    dve.wait_ge(s["gates_ready"], e + 1)
                    nc.vector.tensor_copy(gates_e[:], gates[:].rearrange("p h k -> p (h k)")).then_inc(s["gates_copied"], 1)
                if kind == "C":
                    group = slice(n * GROUP, (n + 1) * GROUP)
                    dve.wait_ge(s["gates_copied"], e - back + 1)
                    dve.wait_ge(s["gelu_ready"], PICKS // GROUP * (e - back) + n + 1)
                    tt(coef[:, group], coef[:, group], gates_e[:, group], ALU.mult).then_inc(s["coef_ready"], 1)
                if kind == "X":
                    dve.wait_ge(s["out_stored"], 16 * e + 1)
                    nc.vector.tensor_copy(y[:], x2[:]).then_inc(s["x2_copied"], 1)
                if kind == "V" and n in DVE_PICKS:
                    k = DVE_PICKS.index(n)
                    dve.wait_ge(s["coef_ready"], PICKS // GROUP * (e - back) + n // GROUP + 1)
                    if k == 0:
                        dve.wait_ge(s["x2_copied"], e - back + 1)
                    else:
                        after_use(dve, ("V", DVE_PICKS[k - 1], back), e)
                    after_fill(dve, item, e)
                    j = slot_of(item, e)
                    stt(out=y[:], in0=ring[:, j], scalar=coef[:, n:n + 1], in1=y[:],
                        op0=ALU.mult, op1=ALU.add).then_inc(used[j], 1)
                if kind == "F":
                    after_use(dve, ("V", PE_PICKS[-1], 1), e)
                    after_use(dve, ("V", DVE_PICKS[-1], 1), e)
                    tt(y[:], y[:], y_ps[:].rearrange("p b w -> p (b w)"), ALU.add).then_inc(s["y_ready"], 1)
                if kind == "O":
                    dve.wait_ge(s["res_r_ready"], e)
                    dve.wait_ge(s["final_row_ready"], e)
                    stt(out=y[:], in0=y[:], scalar=stat_e[:, 2:3], in1=y_ps[:].rearrange("p b w -> p (b w)"),
                        op0=ALU.mult, op1=ALU.mult).then_inc(s["out_ready"], 1)

            def top16(m, n, src, low, value, where, hi, hi_at, low_ready, lo, lo_at, share):
                def lists(op, last_sem):
                    for t in range(n):
                        last = op(t)
                        if t % 8 == 7:
                            if t == n - 1:
                                last.then_inc(s[last_sem], 1)
                            share()

                lists(lambda t: nc.vector.max(value[:, t, 0:8], src[:, t]), hi)
                dve.wait_ge(s[hi], m + 1)
                dve.sem_inc(s["held_dve"])
                lists(lambda t: nc.vector.match_replace(low[:, t], value[:, t, 0:8], src[:, t], -3e38), low_ready)
                lists(lambda t: nc.vector.max_index(where[:, t, 0:8], value[:, t, 0:8], src[:, t]), hi_at)
                dve.wait_ge(s[low_ready], m + 1)
                dve.sem_inc(s["held_dve"])
                lists(lambda t: nc.vector.max(value[:, t, 8:16], low[:, t]), lo)
                dve.wait_ge(s[lo], m + 1)
                dve.sem_inc(s["held_dve"])
                lists(lambda t: nc.vector.max_index(where[:, t, 8:16], value[:, t, 8:16], low[:, t]), lo_at)
                dve.wait_ge(s[hi_at], m + 1)
                dve.wait_ge(s[lo_at], m + 1)

            def steps(m, share):
                dve.wait_ge(s["mix_loaded"], 16 * LOADS * (m + 1))
                tt(small[:], zgs[:, ZG:], head_bias[:], ALU.add).then_inc(s["small_in"], 1)
                share()
                dve.wait_ge(s["soft_log"], m + 1)
                stt(out=soft[:], in0=small[:, 0:HEADS], scalar=0.0, in1=soft[:], op0=ALU.max, op1=ALU.add).then_inc(s["soft_sum"], 1)
                dve.wait_ge(s["soft_sum"], m + 1)
                tt(rate[:], soft[:], neg_a[:], ALU.mult).then_inc(s["rate_ready"], 1)
                b_exp = small_exp[:, HEADS:]
                ts(beta_den[:], b_exp, 1.0, None, ALU.add).then_inc(s["beta_parts"], 1)
                stt(out=beta_num[:], in0=small[:, HEADS:], scalar=0.0, in1=b_exp, op0=ALU.is_ge, op1=ALU.max).then_inc(s["beta_parts"], 1)
                dve.wait_ge(s["beta_parts"], 3 * m + 2)
                nc.vector.reciprocal(beta_den[:], beta_den[:]).then_inc(s["beta_parts"], 1)
                dve.wait_ge(s["beta_parts"], 3 * (m + 1))
                tt(beta[:], beta_num[:], beta_den[:], ALU.mult).then_inc(s["beta_ready"], 1)
                dve.wait_ge(s["qk_sq_ready"], m + 1)
                nc.vector.tensor_reduce(qk_ms[:], view(qk_sq, 2 * GDN_H, P), AX_X, ALU.add).then_inc(s["qk_sum"], 1)
                share()
                dve.wait_ge(s["cums_ready"], m + 1)
                nc.vector.tensor_copy(logs[:, 0:2], heads(0, 2, HEADS)).then_inc(s["logs_copied"], 1)
                dve.wait_ge(s["logs_copied"], m + 1)
                tt(logs[:, 2], logs[:, 1], logs[:, 0], ALU.subtract).then_inc(s["logs_ready"], 2)
                dve.wait_ge(s["qk_sum"], m + 1)
                for h in range(HEADS):
                    last = stt(out=decay[:, h], in0=heads(1 + h // 4)[:, h % 4], scalar=logs[:, 0, h:h + 1], in1=floor[:],
                               op0=ALU.subtract, op1=ALU.min)
                last.then_inc(s["decay_log"], 1)
                share()
                dve.wait_ge(s["qk_r_ready"], m + 1)
                tt(k_hat, qkv[:, 1], over_free(qk_r[:, GDN_H:], P), ALU.mult).then_inc(s["k_hat_ready"], 1)
                dve.wait_ge(s["k_hat_ready"], m + 1)
                dve.wait_ge(s["beta_ready"], m + 1)
                tt(k_beta, k_hat, over_free(beta[:], P), ALU.mult).then_inc(s["k_beta_ready"], 1)
                share()
                tt(v_beta, qkv[:, 2], over_free(beta[:], P), ALU.mult)
                dve.wait_ge(s["exps_ready"], m + 1)
                tt(k_out, k_hat, over_free(e_out[:, SSD_H:], P), ALU.mult)
                dve.wait_ge(s["k_beta_ready"], m + 1)
                tt(k_in, k_beta, over_free(e_in[:, SSD_H:], P), ALU.mult).then_inc(s["k_in_ready"], 1)
                share()
                tt(x_dt, xs, over_free(soft[:, 0:SSD_H], SSD_P), ALU.mult).then_inc(s["x_dt_ready"], 1)
                dve.wait_ge(s["x_dt_ready"], m + 1)
                tt(x_end, x_dt, over_free(e_out[:, 0:SSD_H], SSD_P), ALU.mult).then_inc(s["x_end_ready"], 1)
                share()
                dve.wait_ge(s["decay_ready"], m + 1)
                for g in range(SSD_G):
                    group = slice(g * SSD_R, (g + 1) * SSD_R)
                    last = tt(G[:, group], over_heads(heads(0, 2, P, 256)[:, g], SSD_R), decay[:, group], ALU.mult)
                last.then_inc(s["G_ready"], 1)
                share()
                dve.wait_ge(s["pairs_ready"], m + 1)
                tt(A_T, heads(1), decay[:, SSD_H:], ALU.mult).then_inc(s["A_ready"], 1)
                tt(qk, heads(2), decay[:, SSD_H:], ALU.mult).then_inc(s["qk_ready"], 1)
                share()
                dve.wait_ge(s["A_ready"], m + 1)
                dve.wait_ge(s["G_ready"], m + 1)
                tt(M_T[:, 0], A_T, over_heads(level[:, 0], GDN_H), ALU.mult).then_inc(s["M_ready"], 1)
                dve.wait_ge(s["M_ready"], NL * m + 1)
                dve.wait_ge(s["qk_ready"], m + 1)
                tt(Y, over_heads(ident[:], GDN_H), M_T[:, 0], ALU.subtract).then_inc(s["Y_ready"], 1)
                tt(M_T[:, 1], A_T, over_heads(level[:, 1], GDN_H), ALU.mult).then_inc(s["M_ready"], 1)
                share()
                for n in range(1, NL):
                    if n > 1:
                        dve.wait_ge(s["steps_ready"], (NL - 1) * m + n - 1)
                        tt(X, X, heads(2), ALU.subtract).then_inc(s["X_ready"], 1)
                        tt(Y, Y, heads(3), ALU.subtract).then_inc(s["Y_ready"], 1)
                    if n + 1 < NL:
                        dve.wait_ge(s["Y_ready"], NL * m + n)
                        tt(M_T[:, (n + 1) % 2], A_T, over_heads(level[:, n + 1], GDN_H), ALU.mult).then_inc(s["M_ready"], 1)
                    if isinstance(m, int) and m == 0 and n < 5:
                        dve.wait_ge(w_late_loaded, 16 * 2 * KD)
                        for k in (2 * n - 2, 2 * n - 1):
                            nc.vector.tensor_scalar(w_out[:, k], w_out[:, k], w_mix[:, min(k, 4):min(k, 4) + 1], None,
                                                    ALU.mult).then_inc(s["w_out_ready"], 1)
                    share()
                dve.wait_ge(s["steps_ready"], (NL - 1) * (m + 1))
                tt(Y, Y, heads(3), ALU.subtract).then_inc(s["Y_ready"], 1)
                dve.wait_ge(s["ssd_out"], m + 1)
                tt(y_ssd, heads(5, SSD_H, SSD_P), over_free(e_in[:, 0:SSD_H], SSD_P), ALU.mult).then_inc(s["y_part"], 1)
                tt(y_skip, xs, over_free(d_head[:], SSD_P), ALU.mult)
                dve.wait_ge(s["y_part"], 2 * m + 1)
                tt(y_ssd, y_ssd, heads(4, SSD_H, SSD_P), ALU.add).then_inc(s["y_part"], 1)
                dve.wait_ge(s["y_part"], 2 * (m + 1))
                tt(y_ssd, y_ssd, y_skip, ALU.add).then_inc(s["S_ssd_part"], 1)
                share()
                dve.wait_ge(s["S_ssd_part"], 2 * m + 1)
                tt(y_ssd, y_ssd, view(zgs[:, 0:SSD_W], SSD_H, SSD_P), ALU.mult).then_inc(s["y_gated"], 1)
                tt(S_ssd[:], S_ssd[:], over_free(e_all[:, 0:SSD_H], SSD_P), ALU.mult).then_inc(s["S_ssd_part"], 1)
                dve.wait_ge(s["S_ssd_part"], 2 * (m + 1))
                tt(S_ssd[:], S_ssd[:], heads(1, SSD_H, SSD_P), ALU.add).then_inc(s["S_ssd_ready"], 1)
                share()
                dve.wait_ge(s["gdn_out"], m + 1)
                tt(o_gdn, heads(3), over_free(e_in[:, SSD_H:], P), ALU.mult).then_inc(s["o_part"], 1)
                dve.wait_ge(s["o_part"], 3 * m + 1)
                tt(o_gdn, o_gdn, heads(4), ALU.add).then_inc(s["o_part"], 1)
                tt(S_gdn[:], S_gdn[:], over_free(e_all[:, SSD_H:], P), ALU.mult).then_inc(s["S_gdn_part"], 1)
                share()
                dve.wait_ge(s["o_part"], 3 * m + 2)
                stt(out=o_gdn, in0=o_gdn, scalar=P ** -0.5, in1=over_free(qk_r[:, 0:GDN_H], P),
                    op0=ALU.mult, op1=ALU.mult).then_inc(s["o_part"], 1)
                dve.wait_ge(s["S_gdn_part"], m + 1)
                tt(S_gdn[:], S_gdn[:], heads(5), ALU.add).then_inc(s["S_gdn_ready"], 1)
                share()
                dve.wait_ge(s["y_r_ready"], m + 1)
                ts(mix[:, 0:SSD_W], y_ssd.rearrange("p h w -> p (h w)"), stat[:, 2:3], None, ALU.mult).then_inc(s["mix_ssd"], 1)
                dve.wait_ge(s["o_sq_ready"], m + 1)
                nc.vector.tensor_reduce(r_gdn[:, 0], view(qk_sq[:, 0:GDN_W], GDN_H, P), AX_X, ALU.add).then_inc(s["o_sum"], 1)
                share()
                dve.wait_ge(s["o_r_ready"], m + 1)
                tt(o_gdn, o_gdn, over_free(r_gdn[:, 2], P), ALU.mult).then_inc(s["o_scaled"], 1)
                dve.wait_ge(s["o_scaled"], m + 1)
                tt(view(mix[:, SSD_W:], GDN_H, P), o_gdn, view(zgs[:, SSD_W:ZG], GDN_H, P), ALU.mult).then_inc(s["mix_gdn"], 1)
                share()
                for _ in range(5):
                    share()
                dve.wait_ge(s["out_proj"], m + 1)
                dve.wait_ge(s["x2_in"], 16 * (m + 1))
                tt(x2[:], x2[:], bank[:, 2:4].rearrange("p b w -> p (b w)"), ALU.add).then_inc(s["x2_ready"], 1)
                share()
                dve.wait_ge(s["x2_r_ready"], m + 1)
                dve.wait_ge(s["ffn_row_ready"], 2 * m + 1)
                stt(out=h2, in0=x2[:], scalar=stat[:, 5:6], in1=bank[:, 0:2].rearrange("p b w -> p (b w)"),
                    op0=ALU.mult, op1=ALU.mult).then_inc(s["h2_ready"], 1)
                for _ in range(13):
                    share()
                dve.wait_ge(s["score_copied"], m + 1)
                dve.sem_inc(s["held_dve"])
                top16(m, LISTS, score, rest, best, best_at, "best_hi", "best_hi_at", "rest_ready", "best_lo", "best_lo_at", share)
                nc.vector.tensor_copy(best_key, best_at).then_inc(s["key_ready"], 1)
                b, k = (t.rearrange("p (h two) k -> p h two k", two=2) for t in (best, best_key))
                n8, at = TOPK // 2, 0
                dve.wait_ge(s["key_ready"], m + 1)
                for a, n in RUNS:
                    tt(cand[:, :, at:at + n], b[:, :, 0, a:a + 1].broadcast_to([P, PEER_H, n]), b[:, :, 1, 0:n], ALU.add)
                    stt(out=cand_id[:, :, at:at + n], in0=k[:, :, 0, a:a + 1].broadcast_to([P, PEER_H, n]), scalar=float(N_KEYS),
                        in1=k[:, :, 1, 0:n], op0=ALU.mult, op1=ALU.add)
                    at += n
                stt(out=cand_id[:, :, at:], in0=k[:, :, 0, n8:], scalar=float(N_KEYS),
                    in1=k[:, :, 1, 0:1].broadcast_to([P, PEER_H, n8]), op0=ALU.mult, op1=ALU.add).then_inc(s["id_ready"], 1)
                tt(cand[:, :, at:], b[:, :, 0, n8:], b[:, :, 1, 0:1].broadcast_to([P, PEER_H, n8]),
                   ALU.add).then_inc(s["cand_ready"], 1)
                share()
                dve.wait_ge(s["cand_ready"], m + 1)
                dve.sem_inc(s["held_dve"])
                top16(m, PEER_H, cand, cand_rest, top, top_at, "top_hi", "top_hi_at", "cand_rest_ready", "top_lo", "top_lo_at", share)
                nc.vector.tensor_copy(top_rank, top_at).then_inc(s["top_rank_ready"], 1)
                tt(shifted, top, top[:, :, 0:1].broadcast_to([P, PEER_H, TOPK]), ALU.subtract).then_inc(s["shifted_ready"], 1)
                dve.wait_ge(s["top_rank_ready"], m + 1)
                full = [P, HALF_H, TOPK, CANDS]
                for half in range(2):
                    hs = slice(half * HALF_H, (half + 1) * HALF_H)
                    if half:
                        dve.wait_ge(s["top_id_ready"], 2 * m + 1)
                    tt(chosen, rank[:, None, None, :].broadcast_to(full), top_rank[:, hs, :, None].broadcast_to(full),
                       ALU.is_equal).then_inc(s["chosen_ready"], 1)
                    share()
                    dve.wait_ge(s["chosen_ready"], 2 * m + half + 1)
                    tt(chosen, chosen, cand_id[:, hs, None, :].broadcast_to(full), ALU.mult).then_inc(s["chosen_id"], 1)
                    share()
                    dve.wait_ge(s["chosen_id"], 2 * m + half + 1)
                    nc.vector.tensor_reduce(top_id[:, hs], chosen, AX_X, ALU.add).then_inc(s["top_id_ready"], 1)
                    share()
                dve.wait_ge(s["weight_ready"], m + 1)
                nc.vector.tensor_reduce(total[:], weight, AX_X, ALU.add).then_inc(s["total_ready"], 1)
                dve.wait_ge(s["total_ready"], m + 1)
                nc.vector.reciprocal(total[:], total[:]).then_inc(s["total_inv"], 1)
                dve.wait_ge(s["total_inv"], m + 1)
                tt(gates[:], weight, over_free(total[:], TOPK), ALU.mult).then_inc(s["gates_ready"], 1)
                dve.wait_ge(s["top_id_ready"], 2 * (m + 1))
                nc.vector.tensor_copy(picks[:].rearrange("p (h k) -> p h k", h=PEER_H), top_id).then_inc(s["picks_ready"], 1)

            nc.vector.memset(eps[:], EPS).then_inc(s["eps_set_m"], 1)
            nc.vector.memset(S_gdn[:], 0.0).then_inc(s["setup_done"], 1)
            nc.vector.memset(S_ssd[:], 0.0).then_inc(s["setup_done"], 1)
            dve.wait_ge(s["consts"], 16 * N_CONST)
            nc.vector.memset(head_bias[:, HEADS:], 0.0).then_inc(s["setup_done"], 1)
            dve.wait_ge(s["neg_a_exp"], 1)
            ts(neg_a[:], neg_a[:], -1.0, None, ALU.mult).then_inc(s["setup_done"], 1)
            dve.wait_ge(s["setup_done"], 4)
            for j in range(SLOTS):
                dve.sem_inc(used[j])
            dve.sem_inc(s["out_stored"])

            def body(m, e):
                share = expert_share(e, do)
                if m is not None:
                    steps(m, share)
                share(last=True)
                if m is not None:
                    dve.wait_ge(s["h2_ready"], m + 1)
                    if e is not None:
                        after_use(dve, ("U", PICKS - 1, 0), e)
                    dve.wait_ge(s["ffn_row_ready"], 2 * (m + 1))
                    stt(out=h2_e[:], in0=x2[:], scalar=stat[:, 5:6], in1=bank[:, 0:2].rearrange("p b w -> p (b w)"),
                        op0=ALU.mult, op1=ALU.mult).then_inc(s["h2_copied"], 1)

            tile_loop(dve, body)


def program(nc, A, out):
    ch_scr = nc.dram_tensor("ch_scr", [BLOCKS, P, SEQ], F32).ap()
    tok_scr = nc.dram_tensor("tok_scr", [SEQ, CONV_CH], F32).ap()
    zgs_scr = nc.dram_tensor("zgs_scr", [SEQ, ZGS], F32).ap()
    with (nc.sbuf_tensor("w_out", [P, KD, D], F32) as w_out, nc.sbuf_tensor("w_q", [P, KD, LISTS * P], F32) as w_q,
          nc.semaphore("w_late_loaded") as w_late_loaded):
        front_stage(nc, A, ch_scr, tok_scr, zgs_scr, w_out, w_q, w_late_loaded)
        tile_stage(nc, A, ch_scr, tok_scr, zgs_scr, out, w_out, w_q, w_late_loaded)


_OUT = ((1, SEQ, D), "float32")


def constants():
    import numpy as np

    s, l = np.arange(P)[:, None], np.arange(P)[None, :]
    level = [((s // b % 2 == 0) & (l // b == s // b + 1)).astype(np.float32) for b in LEVELS]
    return {
        "c_ident": np.eye(P, dtype=np.float32),
        "c_upper": (s <= l).astype(np.float32),
        "c_ones": np.ones((P, P), np.float32),
        "c_floor": np.where(s <= l, 0.0, NEG).astype(np.float32),
        "c_level": np.stack(level, axis=1),
        "c_rank": np.broadcast_to(np.arange(CANDS, dtype=np.float32), (P, CANDS)).copy(),
    }


def kernel(**inputs):
    import numpy as _np
    import concourse.bacc as _bacc
    from concourse import mybir as _mybir
    from concourse.bass_utils import run_bass_kernel_spmd as _run

    nc = _bacc.Bacc("TRN2", target_bir_lowering=False, num_devices=1)
    arrays, args = {}, {}
    for name, value in {**inputs, **constants()}.items():
        a = _np.ascontiguousarray(value)
        arrays[f"in_{name}_dram"] = a
        args[name] = nc.dram_tensor(f"in_{name}_dram", a.shape, _mybir.dt.from_np(a.dtype), kind="ExternalInput").ap()
    out = nc.dram_tensor("out_0_dram", _OUT[0], _mybir.dt.from_np(_np.dtype(_OUT[1])), kind="ExternalOutput").ap()
    program(nc, args, out)
    r = _run(nc, [arrays], core_ids=[0])
    return r.results[0]["out_0_dram"]
```
